# Optimizing a Trainium2 kernel written in Bass

```python
import functools
import jax, jax.numpy as jnp
from jax import lax
import numpy as np

'''Hybrid diffusion / flow-matching backbone: DEPTH interleaved layers. Layer i uses token mixer (i mod 4):
0 = grouped 2-D Fourier mixing (FNet), 1 = windowed GQA with per-head sink logits, 2 = Conformer convolution module,
3 = chunked gMLP spatial gating. Every mixer is followed by a squared-ReLU MLP. Every sub-layer is pre-RMSNorm plus
adaLN (shift, scale, gate from SiLU(c) through a per-layer linear map). The context is an un-noised prefix that uses the
same layer weights, modulated by c_ctx, and reads only context tokens. Latent tokens read latent and context tokens.
Inputs: x (BATCH, SEQ, D_MODEL), c (BATCH, D_MODEL), ctx (BATCH, CTX_LEN, D_MODEL), c_ctx (D_MODEL,), per-layer params.
Output: latent stream (BATCH, SEQ, D_MODEL).'''

D_MODEL = 1024
BATCH = 1
SEQ = 1024
DEPTH = 2

GRID_W = 64
CTX_LEN = 256
N_MIXERS = 4
NORM_EPS = 1e-6
FNET_GROUPS = 4
ATTN_HEAD_DIM = 64
ATTN_Q_HEADS = D_MODEL // ATTN_HEAD_DIM
ATTN_KV_HEADS = 2
ATTN_GROUP = ATTN_Q_HEADS // ATTN_KV_HEADS
WINDOW = 128
ATTN_BLOCK = 128
ROPE_THETA = 10000.0
ROPE_PAIRS = ATTN_HEAD_DIM // 4
CONV_WIDTH = 31
GMLP_CHUNK = 128
GMLP_GROUPS = 4
GMLP_HALF = D_MODEL
D_FF = 4 * D_MODEL

kernel_name = 'hybrid_fourier_swa_conv_gmlp_prefix_dit'

def _rms_norm(x, g):
    xf = x.astype(jnp.float32)
    y = xf * lax.rsqrt(jnp.mean(jnp.square(xf), axis=-1, keepdims=True) + NORM_EPS)
    return (y * g.astype(jnp.float32)).astype(x.dtype)

def _layer_norm(x, g, b):
    xf = x.astype(jnp.float32)
    mu = jnp.mean(xf, axis=-1, keepdims=True)
    var = jnp.mean(jnp.square(xf - mu), axis=-1, keepdims=True)
    y = (xf - mu) * lax.rsqrt(var + NORM_EPS)
    return (y * g.astype(jnp.float32) + b.astype(jnp.float32)).astype(x.dtype)

def _modulate(h, shift, scale):
    return h * (1.0 + scale) + shift

def _axial_rope_tables(rows):
    row = jnp.repeat(jnp.arange(rows, dtype=jnp.float32), GRID_W)
    col = jnp.tile(jnp.arange(GRID_W, dtype=jnp.float32), rows)
    inv = ROPE_THETA ** (-jnp.arange(ROPE_PAIRS, dtype=jnp.float32) / ROPE_PAIRS)
    ang_r = row[:, None] * inv[None, :]
    ang_c = col[:, None] * inv[None, :]
    return (jnp.cos(ang_r), jnp.sin(ang_r), jnp.cos(ang_c), jnp.sin(ang_c))

def _rotate(x, cos, sin):
    x1, x2 = x[..., :ROPE_PAIRS], x[..., ROPE_PAIRS:]
    cos = cos[None, :, None, :]
    sin = sin[None, :, None, :]
    return jnp.concatenate([x1 * cos - x2 * sin, x2 * cos + x1 * sin], axis=-1)

def _apply_axial_rope(x, tabs):
    cr, sr, cc, sc = tabs
    xf = x.astype(jnp.float32)
    half = ATTN_HEAD_DIM // 2
    out = jnp.concatenate([_rotate(xf[..., :half], cr, sr), _rotate(xf[..., half:], cc, sc)], axis=-1)
    return out.astype(x.dtype)

def _fourier_mixer(h, w_out, b_out):
    b, s, _ = h.shape
    hf = h.astype(jnp.float32).reshape(b, s, FNET_GROUPS, D_MODEL // FNET_GROUPS)
    mixed = jnp.fft.fft2(hf, axes=(1, 3), norm='ortho').real
    mixed = mixed.reshape(b, s, D_MODEL).astype(h.dtype)
    return mixed @ w_out + b_out

def _attn_qkv(h, w_qkv, q_g, k_g):
    b, s, _ = h.shape
    nq = ATTN_Q_HEADS * ATTN_HEAD_DIM
    nk = ATTN_KV_HEADS * ATTN_HEAD_DIM
    qkv = h @ w_qkv
    q = _rms_norm(qkv[..., :nq].reshape(b, s, ATTN_Q_HEADS, ATTN_HEAD_DIM), q_g)
    k = _rms_norm(qkv[..., nq:nq + nk].reshape(b, s, ATTN_KV_HEADS, ATTN_HEAD_DIM), k_g)
    v = qkv[..., nq + nk:].reshape(b, s, ATTN_KV_HEADS, ATTN_HEAD_DIM)
    return q, k, v

def _sink_softmax(scores, sink_kg):
    s_sink = jnp.broadcast_to(sink_kg[:, :, None, None], scores.shape[:-1] + (1,))
    p = jax.nn.softmax(jnp.concatenate([scores, s_sink], axis=-1), axis=-1)
    return p[..., :-1]

def _banded_attention(q, k, v, k_ctx, v_ctx, sink_kg):
    b, seq_len = q.shape[0], q.shape[1]
    nb = seq_len // ATTN_BLOCK
    scale = ATTN_HEAD_DIM ** -0.5
    n_band = 3 * ATTN_BLOCK
    qb = q.reshape(b, nb, ATTN_BLOCK, ATTN_KV_HEADS, ATTN_GROUP, ATTN_HEAD_DIM).transpose(1, 0, 2, 3, 4, 5)

    def band(t):
        tb = t.reshape(b, nb, ATTN_BLOCK, ATTN_KV_HEADS, ATTN_HEAD_DIM)
        tp = jnp.pad(tb, ((0, 0), (1, 1), (0, 0), (0, 0), (0, 0)))
        return jnp.concatenate([tp[:, :-2], tp[:, 1:-1], tp[:, 2:]], axis=2).transpose(1, 0, 2, 3, 4)

    kb, vb = band(k), band(v)

    def one_block(args):
        qj, kj, vj, j = args
        qpos = j * ATTN_BLOCK + jnp.arange(ATTN_BLOCK)
        kpos = (j - 1) * ATTN_BLOCK + jnp.arange(n_band)
        valid = (jnp.abs(qpos[:, None] - kpos[None, :]) <= WINDOW) & (kpos >= 0)[None, :] & (kpos < seq_len)[None, :]
        s_win = jnp.einsum('bqkgd,bskd->bkgqs', qj, kj).astype(jnp.float32) * scale
        s_win = jnp.where(valid, s_win, -jnp.inf)
        s_ctx = jnp.einsum('bqkgd,blkd->bkgql', qj, k_ctx).astype(jnp.float32) * scale
        p = _sink_softmax(jnp.concatenate([s_win, s_ctx], axis=-1), sink_kg)
        p_win = p[..., :n_band].astype(vj.dtype)
        p_ctx = p[..., n_band:].astype(v_ctx.dtype)
        return jnp.einsum('bkgqs,bskd->bqkgd', p_win, vj) + jnp.einsum('bkgql,blkd->bqkgd', p_ctx, v_ctx)

    out = lax.map(one_block, (qb, kb, vb, jnp.arange(nb)))
    return out.transpose(1, 0, 2, 3, 4, 5).reshape(b, seq_len, ATTN_Q_HEADS * ATTN_HEAD_DIM)

def _context_attention(qc, kc, vc, sink_kg):
    b, l = qc.shape[0], qc.shape[1]
    scale = ATTN_HEAD_DIM ** -0.5
    qg = qc.reshape(b, l, ATTN_KV_HEADS, ATTN_GROUP, ATTN_HEAD_DIM)
    sc = jnp.einsum('blkgd,bmkd->bkglm', qg, kc).astype(jnp.float32) * scale
    p = _sink_softmax(sc, sink_kg).astype(vc.dtype)
    return jnp.einsum('bkglm,bmkd->blkgd', p, vc).reshape(b, l, ATTN_Q_HEADS * ATTN_HEAD_DIM)

def _window_gqa_mixer(h_lat, h_ctx, rope, w_qkv, q_g, k_g, sink, w_o, with_ctx_out):
    q, k, v = _attn_qkv(h_lat, w_qkv, q_g, k_g)
    q = _apply_axial_rope(q, rope)
    k = _apply_axial_rope(k, rope)
    qc, kc, vc = _attn_qkv(h_ctx, w_qkv, q_g, k_g)
    sink_kg = sink.astype(jnp.float32).reshape(ATTN_KV_HEADS, ATTN_GROUP)
    y_lat = _banded_attention(q, k, v, kc, vc, sink_kg) @ w_o
    y_ctx = _context_attention(qc, kc, vc, sink_kg) @ w_o if with_ctx_out else None
    return y_lat, y_ctx

def _conv_module(h, w_in, b_in, dw, dw_b, ln_g, ln_b, w_out, b_out):
    a = h @ w_in + b_in
    u = a[..., :D_MODEL] * jax.nn.sigmoid(a[..., D_MODEL:])
    u = lax.conv_general_dilated(u, dw[:, None, :].astype(u.dtype), window_strides=(1,),
                                 padding=[(CONV_WIDTH // 2, CONV_WIDTH // 2)],
                                 dimension_numbers=('NWC', 'WIO', 'NWC'),
                                 feature_group_count=D_MODEL) + dw_b
    u = jax.nn.silu(_layer_norm(u, ln_g, ln_b))
    return u @ w_out + b_out

def _chunk_gmlp(h, w_in, b_in, ln_g, ln_b, w_s, b_s, w_out):
    b, s, _ = h.shape
    z = jax.nn.gelu(h @ w_in + b_in)
    u, v = z[..., :GMLP_HALF], z[..., GMLP_HALF:]
    v = _layer_norm(v, ln_g, ln_b)
    nc = s // GMLP_CHUNK
    vc = v.reshape(b, nc, GMLP_CHUNK, GMLP_GROUPS, GMLP_HALF // GMLP_GROUPS)
    sg = jnp.einsum('gpq,bnqgd->bnpgd', w_s, vc) + b_s.T[None, None, :, :, None]
    return (u * sg.reshape(b, s, GMLP_HALF)) @ w_out

def _sq_relu_mlp(h, w1, w2):
    return jnp.square(jax.nn.relu(h @ w1)) @ w2

def setup_inputs(seed: int = 0) -> dict:
    key = jax.random.key(seed)
    ks = iter(jax.random.split(key, 40))

    def nrm(shape, s):
        return jax.random.normal(next(ks), shape, jnp.float32) * s

    n_a, n_b, n_c, n_d = (len(range(m, DEPTH, N_MIXERS)) for m in range(N_MIXERS))
    D = D_MODEL
    qkv_w = (ATTN_Q_HEADS + 2 * ATTN_KV_HEADS) * ATTN_HEAD_DIM
    gd = GMLP_HALF // GMLP_GROUPS
    return {
        'x': nrm((BATCH, SEQ, D), 1.0),
        'c': nrm((BATCH, D), 1.0),
        'ctx': nrm((BATCH, CTX_LEN, D), 1.0),
        'c_ctx': nrm((D,), 1.0),
        'ada_w': nrm((DEPTH, D, 6 * D), 0.5 * D ** -0.5),
        'ada_b': nrm((DEPTH, 6 * D), 0.02),
        'norm1_g': 1.0 + nrm((DEPTH, D), 0.05),
        'norm2_g': 1.0 + nrm((DEPTH, D), 0.05),
        'mlp_w1': nrm((DEPTH, D, D_FF), D ** -0.5),
        'mlp_w2': nrm((DEPTH, D_FF, D), D_FF ** -0.5),
        'fnet_w': nrm((n_a, D, D), D ** -0.5),
        'fnet_b': nrm((n_a, D), 0.02),
        'attn_w_qkv': nrm((n_b, D, qkv_w), D ** -0.5),
        'attn_q_g': 1.0 + nrm((n_b, ATTN_HEAD_DIM), 0.05),
        'attn_k_g': 1.0 + nrm((n_b, ATTN_HEAD_DIM), 0.05),
        'attn_sink': nrm((n_b, ATTN_Q_HEADS), 0.5),
        'attn_w_o': nrm((n_b, D, D), D ** -0.5),
        'conv_w_in': nrm((n_c, D, 2 * D), D ** -0.5),
        'conv_b_in': nrm((n_c, 2 * D), 0.02),
        'conv_dw': nrm((n_c, CONV_WIDTH, D), CONV_WIDTH ** -0.5),
        'conv_dw_b': nrm((n_c, D), 0.02),
        'conv_ln_g': 1.0 + nrm((n_c, D), 0.05),
        'conv_ln_b': nrm((n_c, D), 0.02),
        'conv_w_out': nrm((n_c, D, D), D ** -0.5),
        'conv_b_out': nrm((n_c, D), 0.02),
        'gmlp_w_in': nrm((n_d, D, 2 * GMLP_HALF), D ** -0.5),
        'gmlp_b_in': nrm((n_d, 2 * GMLP_HALF), 0.02),
        'gmlp_ln_g': 1.0 + nrm((n_d, GMLP_HALF), 0.05),
        'gmlp_ln_b': nrm((n_d, GMLP_HALF), 0.02),
        'gmlp_w_s': nrm((n_d, GMLP_GROUPS, GMLP_CHUNK, GMLP_CHUNK), 0.5 * GMLP_CHUNK ** -0.5),
        'gmlp_b_s': 1.0 + nrm((n_d, GMLP_GROUPS, GMLP_CHUNK), 0.1),
        'gmlp_w_out': nrm((n_d, GMLP_HALF, D), GMLP_HALF ** -0.5),
    }

def reference(x, c, ctx, c_ctx, ada_w, ada_b, norm1_g, norm2_g, mlp_w1, mlp_w2,
              fnet_w, fnet_b, attn_w_qkv, attn_q_g, attn_k_g, attn_sink, attn_w_o,
              conv_w_in, conv_b_in, conv_dw, conv_dw_b, conv_ln_g, conv_ln_b, conv_w_out, conv_b_out,
              gmlp_w_in, gmlp_b_in, gmlp_ln_g, gmlp_ln_b, gmlp_w_s, gmlp_b_s, gmlp_w_out):
    ROWS = x.shape[1] // GRID_W
    rope = _axial_rope_tables(ROWS)
    silu_c = jax.nn.silu(c)
    silu_cc = jax.nn.silu(c_ctx)
    h_lat, h_ctx = x, ctx
    for i in range(DEPTH):
        last = i == DEPTH - 1
        kind, li = i % N_MIXERS, i // N_MIXERS
        sh1, sc1, g1, sh2, sc2, g2 = jnp.split((silu_c @ ada_w[i] + ada_b[i])[:, None, :], 6, axis=-1)
        csh1, csc1, cg1, csh2, csc2, cg2 = jnp.split(silu_cc @ ada_w[i] + ada_b[i], 6, axis=-1)
        need_ctx_in = (not last) or kind == 1
        n_lat = _modulate(_rms_norm(h_lat, norm1_g[i]), sh1, sc1)
        n_ctx = _modulate(_rms_norm(h_ctx, norm1_g[i]), csh1, csc1) if need_ctx_in else None
        if kind == 1:
            y_lat, y_ctx = _window_gqa_mixer(n_lat, n_ctx, rope, attn_w_qkv[li], attn_q_g[li], attn_k_g[li],
                                             attn_sink[li], attn_w_o[li], not last)
        else:
            if kind == 0:
                mix = functools.partial(_fourier_mixer, w_out=fnet_w[li], b_out=fnet_b[li])
            elif kind == 2:
                mix = functools.partial(_conv_module, w_in=conv_w_in[li], b_in=conv_b_in[li], dw=conv_dw[li],
                                        dw_b=conv_dw_b[li], ln_g=conv_ln_g[li], ln_b=conv_ln_b[li],
                                        w_out=conv_w_out[li], b_out=conv_b_out[li])
            else:
                mix = functools.partial(_chunk_gmlp, w_in=gmlp_w_in[li], b_in=gmlp_b_in[li], ln_g=gmlp_ln_g[li],
                                        ln_b=gmlp_ln_b[li], w_s=gmlp_w_s[li], b_s=gmlp_b_s[li],
                                        w_out=gmlp_w_out[li])
            y_lat = mix(n_lat)
            y_ctx = mix(n_ctx) if not last else None
        h_lat = h_lat + g1 * y_lat
        h_lat = h_lat + g2 * _sq_relu_mlp(_modulate(_rms_norm(h_lat, norm2_g[i]), sh2, sc2), mlp_w1[i], mlp_w2[i])
        if not last:
            h_ctx = h_ctx + cg1 * y_ctx
            h_ctx = h_ctx + cg2 * _sq_relu_mlp(_modulate(_rms_norm(h_ctx, norm2_g[i]), csh2, csc2),
                                               mlp_w1[i], mlp_w2[i])
    return h_lat


_drawn_inputs = setup_inputs


def setup_inputs(seed=0):
    import zlib

    import numpy as np

    out = dict(_drawn_inputs(seed))
    spreads = {}
    factors = {'ctx': 3.854,
     'norm1_g': 4.644,
     'fnet_b': 8.0,
     'attn_q_g': 8.0,
     'attn_k_g': 8.0,
     'attn_sink': 8.0}
    for name, (base, spread) in spreads.items():
        noise = np.random.default_rng([zlib.crc32(name.encode()), seed]).standard_normal(out[name].shape)
        drawn = base * np.exp(spread * noise) if base else spread * noise
        out[name] = __import__('jax').numpy.asarray(drawn.astype(out[name].dtype))
    for name, factor in factors.items():
        out[name] = (out[name] * factor).astype(out[name].dtype)
    return out
```

```python
import numpy as np
import concourse.bass as bass
from concourse import mybir
from contextlib import ExitStack

F32 = mybir.dt.float32
F32R = mybir.dt.float32r
ALU = mybir.AluOpType
ACT = mybir.ActivationFunctionType
AX = mybir.AxisListType

P = 128
D = 1024
KC = D // P
LAT, CTX = 1024, 256
T = LAT + CTX
NT = T // P
DEPTH = 2
DFF = 4 * D
EPS = 1e-6
HD = 64
HEADS, KVH = 16, 2
QB = LAT // P
KEYS = 3 * P + CTX
GW = 256
BIG = 1e30
PRE = 64
BLOCKS = [(0, 512), (512, 512), (1024, 256)]

V_N1, V_N2, V_ADAB, V_FB, V_C = 0, 16, 32, 128, 136
V_ALL = 152
PIECE = 512
SH1, SC1, G1, SH2, SC2, G2 = range(6)


def f32(ap):
    return ap.bitcast(F32)


def mm3(pe, out, lhs, rhs, first, last):
    (lh, ll), (rh, rl) = lhs, rhs
    pe.matmul(out, lh, rh, start=first, stop=False)
    pe.matmul(out, lh, rl, start=False, stop=False)
    return pe.matmul(out, ll, rh, start=False, stop=last)


def lo_part(eng, lo, full, hi):
    return eng.tensor_tensor(lo, full, f32(hi), ALU.subtract)


def hybrid_kernel(nc, x, ctxt, vecs, ada_w, w1, w2, fnet_w, wqkv, wo, qkg, sink, dft, rope, masks, eye, out, park, qd):
    ctx = ExitStack()
    with ctx:
        held = ExitStack()
        numbers = []

        def sem(name):
            s = held.enter_context(nc.semaphore(name))
            numbers.append(s.num)
            return s

        def recycle_semaphores():
            with nc.Block() as block:
                @block.gpsimd
                def _(pool):
                    pool.sem_clear(range(min(numbers), max(numbers) + 1))
            held.close()
            numbers.clear()

        def sb(name, shape, dt=F32, where=ctx):
            return where.enter_context(nc.sbuf_tensor(name, shape, dt))

        def banks(name, n, where):
            return [where.enter_context(nc.psum_tensor(f"{name}{i}", [P, 512], F32)) for i in range(n)]

        vec = sb("vec", [P, V_ALL])
        mod = sb("mod", [P, DEPTH, 6, KC, 2])
        g1b = sb("g1b", [P, KC, 2])
        svec = sb("svec", [P, KC, 2])
        ident = sb("ident", [P, P])
        meanw = sb("meanw", [P, P])
        eps = sb("eps", [P, 1])
        rstd_tm = sb("rstd_tm", [P, NT])

        def shift(l, n, k, v):
            return mod[:, l, (SH1, SH2)[n], k, v:v + 1]

        def scale(l, n, k, v):
            return mod[:, l, (SC1, SC2)[n], k, v:v + 1]

        RING = 4
        PIECES = DEPTH * 6 * D // PIECE
        with ExitStack() as ph:
            wbuf = [sb(f"ada_w{i}", [P, KC, PIECE], where=ph) for i in range(RING)]
            xt = [sb(f"xt{i}", [P, D], where=ph) for i in range(2)]
            xsq = sb("xsq", [P, D], where=ph)
            sig = sb("sig", [P, KC, 2], where=ph)
            ssq = sb("ssq", [P, NT], where=ph)
            ps = banks("ada_ps", 1, ph)[0]
            s_small, s_eps, s_e, s_d, s_silu = sem("a_small"), sem("a_eps"), sem("a_exp"), sem("a_d"), sem("a_silu")
            s_w = [sem(f"a_w{i}") for i in range(RING)]
            s_x = [sem(f"a_x{i}") for i in range(2)]
            s_ada, s_ssq, s_std = sem("a_done"), sem("a_ssq"), sem("a_std")
            with nc.Block() as block:
                @block.sync
                def _(sp):
                    sp.dma_start(vec[:], vecs).then_inc(s_small, 16)
                    sp.dma_start(ident[:], eye).then_inc(s_small, 16)
                    with sp.Fori(0, PIECES // RING) as r:
                        for i in range(RING):
                            sp.wait_ge(s_ada, r * RING + (PRE + i + 1 - RING))
                            sp.dma_start(wbuf[i][:], ada_w[bass.ds(r * RING + i, 1)]
                                         .rearrange("a p k n -> p (a k) n")).then_inc(s_w[i], 16)

                @block.gpsimd
                def _(pool):
                    pool.sem_inc(s_ada, PRE)
                    pool.memset(eps[:], EPS).then_inc(s_eps, 1)
                    pool.memset(meanw[:], 1.0 / D).then_inc(s_eps, 1)

                @block.scalar
                def _(act):
                    act.dma_start(xt[0][:], x[0:P, :]).then_inc(s_x[0], 16)
                    act.dma_start(xt[1][:], x[P:2 * P, :]).then_inc(s_x[1], 16)
                    act.wait_ge(s_small, 32)
                    act.activation(sig[:], vec[:, V_C:V_C + 2 * KC], ACT.Exp, scale=-1.0).then_inc(s_e, 1)
                    for t in range(NT):
                        act.wait_ge(s_x[t % 2], 16 * (t // 2 + 1))
                        if t:
                            act.wait_ge(s_ssq, t)
                        act.activation(xsq[:], xt[t % 2][:], ACT.Square, accum_out=ssq[:, t:t + 1]).then_inc(s_ssq, 1)
                        if t + 2 < NT:
                            act.wait_ge(s_ssq, t + 1)
                            src = x[(t + 2) * P:(t + 3) * P, :] if t + 2 < QB else ctxt[(t + 2 - QB) * P:(t + 3 - QB) * P, :]
                            act.dma_start(xt[t % 2][:], src).then_inc(s_x[t % 2], 16)
                    act.wait_ge(s_eps, 2)
                    act.wait_ge(s_ssq, NT)
                    act.activation(ssq[:], ssq[:], ACT.Sqrt, bias=eps[:], scale=1.0 / D).then_inc(s_std, 1)

                @block.vector
                def _(dve):
                    dve.wait_ge(s_e, 1)
                    dve.tensor_scalar_add(sig[:], sig[:], 1.0).then_inc(s_d, 1)
                    dve.wait_ge(s_d, 1)
                    dve.reciprocal(sig[:], sig[:]).then_inc(s_d, 1)
                    dve.wait_ge(s_d, 2)
                    dve.tensor_tensor(svec[:], sig[:], vec[:, V_C:V_C + 2 * KC].rearrange("p (k v) -> p k v", v=2),
                                      ALU.mult).then_inc(s_silu, 1)
                    dve.wait_ge(s_std, 1)
                    dve.reciprocal(rstd_tm[:], ssq[:]).then_inc(s_d, 1)
                    dve.wait_ge(s_ada, PRE + PIECES)
                    modv = mod[:].rearrange("p l s k v -> p (l s k) v")
                    bias = vec[:, V_ADAB:V_ADAB + DEPTH * 6 * KC].rearrange("p (m v) -> p m v", v=1)
                    dve.tensor_tensor(modv, ps[:, 0:2 * DEPTH * 6 * KC].rearrange("p (m v) -> p m v", v=2),
                                      bias.to_broadcast([P, DEPTH * 6 * KC, 2]), ALU.add).then_inc(s_d, 1)
                    n = 4
                    for l in range(DEPTH):
                        for which, col in ((SC1, V_N1), (SC2, V_N2)):
                            for v in range(2):
                                dve.wait_ge(s_d, n)
                                m = mod[:, l, which, :, v]
                                dve.scalar_tensor_tensor(out=m, in0=m, scalar=1.0, in1=vec[:, col + KC * l:col + KC * (l + 1)],
                                                         op0=ALU.add, op1=ALU.mult).then_inc(s_d, 1)
                                n += 1
                    for v in range(2):
                        dve.tensor_tensor(g1b[:, :, v], mod[:, 0, G1, :, v], vec[:, V_FB:V_FB + KC], ALU.mult).then_inc(s_d, 1)

                @block.tensor
                def _(pe):
                    pe.wait_ge(s_silu, 1)
                    M = PIECE // P
                    with pe.Fori(0, PIECES // RING) as r:
                        for i in range(RING):
                            pe.wait_ge(s_w[i], r * 16 + 16)
                            for m in range(M):
                                for k in range(KC):
                                    last = pe.matmul(ps[:, bass.ds(r * (RING * M * 2) + (i * M + m) * 2, 2)],
                                                     wbuf[i][:, k, m * P:(m + 1) * P], svec[:, k, :],
                                                     start=(k == 0), stop=(k == KC - 1))
                                    if m == M - 1 and k == KC - 1:
                                        last.then_inc(s_ada, 1)

        nh = sb("nh", [P, KC, T], F32R)
        nl = sb("nl", [P, KC, T], F32R)

        fnet_mix(nc, sem, sb, banks, x, ctxt, dft, rstd_tm, mod, nh, nl)
        with ExitStack() as layer0:
            ht = sb("ht0", [P, KC, T], where=layer0)
            fnet_out(nc, sem, sb, banks, x, ctxt, fnet_w, mod, g1b, ident, nh, nl, ht)
            mlp(nc, sem, sb, banks, 0, 3, w1, w2, mod, meanw, eps, nh, nl, ht)
            norm_out(nc, sem, sb, banks, 1, park, mod, meanw, eps, nh, nl, ht)
        recycle_semaphores()
        with ExitStack() as att:
            kh = sb("kh", [P, KVH, (QB + 4) * P], F32R, where=att)
            kl = sb("kl", [P, KVH, (QB + 4) * P], F32R, where=att)
            vs = sb("vs", [P, QB + 4, KVH, 2 * HD], F32R, where=att)
            qkv(nc, sem, sb, banks, wqkv, qkg, rope, ident, eps, nh, nl, qd, kh, kl, vs)
            attention(nc, sem, sb, banks, masks, sink, ident, qd, kh, kl, vs, nh, nl)
        ht = sb("ht1", [P, KC, LAT])
        attn_out(nc, sem, sb, banks, wo, park, mod, nh, nl, ht)
        mlp(nc, sem, sb, banks, 1, 2, w1, w2, mod, meanw, eps, nh, nl, ht)
        write_out(nc, sem, sb, banks, ident, ht, out)


def fnet_mix(nc, sem, sb, banks, x, ctxt, dft, rstd_tm, mod, nh, nl):
    GR = D // GW
    SETS = [([(0, 0)], 0, 0, 0), ([(1, 2)], 0, 256, 0), ([(2, 4), (3, 6)], 1, 0, 0), ([(0, 8)], 1, 256, 1)]
    FIXED = {0: 0, 3: 1}
    with ExitStack() as ph:
        tabf = sb("tabf", [P, 2, 512], where=ph)
        tabh = sb("tabh", [P, 4, 2, 512], F32R, where=ph)
        tabl = sb("tabl", [P, 4, 2, 512], F32R, where=ph)
        xg = [sb(f"xg{i}", [P, NT, P], where=ph) for i in range(2)]
        xr = sb("xr", [P, NT * P], where=ph)
        sd = sb("sd", [P, 512], where=ph)
        gh = [sb(f"gh{i}", [P, NT, P], F32R, where=ph) for i in range(2)]
        gl = [sb(f"gl{i}", [P, NT, P], F32R, where=ph) for i in range(2)]
        uvh = sb("uvh", [P, 2, 2, 2, 512], F32R, where=ph)
        uvl = sb("uvl", [P, 2, 2, 2, 512], F32R, where=ph)
        uvf = [sb(f"uvf{i}", [P, 2, 256], where=ph) for i in range(2)]
        sdc = sb("sdc", [P, KC, 2], where=ph)
        gain = sb("gain", [P, 2, 2], where=ph)
        yt = sb("yt", [P, 512], where=ph)
        bt = sb("bt", [P, 256], where=ph)
        seq_ps, y_ps = banks("seq_ps", 4, ph), banks("y_ps", 3, ph)
        s_tab, s_th, s_tl, s_c, s_gain = sem("m_tab"), sem("m_tabh"), sem("m_tabl"), sem("m_sdc"), sem("m_gain")
        s_x = [sem(f"m_x{i}") for i in range(2)]
        s_xr, s_bf, s_g, s_gh, s_gl = sem("m_xr"), sem("m_butterfly"), sem("m_g"), sem("m_gh"), sem("m_gl")
        s_seq, s_uvf, s_fix, s_uvh, s_uvl = sem("m_seq"), sem("m_uvf"), sem("m_fix"), sem("m_uvh"), sem("m_uvl")
        s_y, s_bt, s_yt, s_yh, s_yl = sem("m_y"), sem("m_bt"), sem("m_yt"), sem("m_yh"), sem("m_yl")
        xv = x.rearrange("(n p) d -> p n d", p=P)
        cv = ctxt.rearrange("(n p) d -> p n d", p=P)
        with nc.Block() as block:
            @block.gpsimd
            def _(pool):
                for s in (s_xr, s_gl, s_seq, s_uvf, s_uvl, s_y, s_yt, s_yl):
                    pool.sem_inc(s, PRE)

            @block.sync
            def _(sp):
                for i in range(4):
                    if i:
                        sp.wait_ge(s_tl, i)
                    sp.dma_start(tabf[:], dft[i]).then_inc(s_tab, 16)
                with sp.Fori(0, GR) as g:
                    for i in range(2):
                        sp.wait_ge(s_xr, g * 2 + (PRE + i - 1))
                        col = bass.ds(g * GW + i * P, P)
                        sp.dma_start(xg[i][:, 0:QB, :], xv[:, :, col]).then_inc(s_x[i], 16)
                        sp.dma_start(xg[i][:, QB:NT, :], cv[:, :, col]).then_inc(s_x[i], 16)

            @block.scalar
            def _(act):
                for i in range(4):
                    act.wait_ge(s_tab, 16 * (i + 1))
                    act.activation(tabh[:, i], tabf[:], ACT.Copy).then_inc(s_th, 1)
                for v, n in ((0, LAT), (1, CTX)):
                    act.activation(sdc[:, :, v], mod[:, 0, SH1, :, v], ACT.Copy, scale=float(n)).then_inc(s_c, 1)
                with act.Fori(0, GR) as g:
                    act.wait_ge(s_gain, g + 1)
                    for i in range(2):
                        act.wait_ge(s_g, g * 2 + (i + 1))
                        act.wait_ge(s_seq, g * 8 + (PRE + 4 * i - 4))
                        act.activation(gh[i][:].rearrange("p n c -> p (n c)"), xr[:], ACT.Copy).then_inc(s_gh, 1)
                        if i == 0:
                            act.wait_ge(s_y, g * 6 + PRE)
                        for j, (_, b, off, v) in enumerate(SETS):
                            u = i * 4 + j
                            act.wait_ge(s_seq, g * 8 + (PRE + u + 1))
                            act.wait_ge(s_uvl, g * 8 + (PRE + u - 1))
                            act.activation(uvf[u % 2][:].rearrange("p a s -> p (a s)"), seq_ps[j][:], ACT.Copy,
                                           scale=gain[:, i, v:v + 1]).then_inc(s_uvf, 1)
                            if j in FIXED:
                                act.wait_ge(s_fix, g * 4 + (i * 2 + v + 1))
                            else:
                                act.wait_ge(s_uvf, g * 8 + (PRE + u + 1))
                            act.activation(uvh[:, b, i, :, off:off + 256], uvf[u % 2][:], ACT.Copy).then_inc(s_uvh, 1)
                    for m in range(2):
                        chunk = nh[:, bass.ds(g * 2 + m, 1), :].rearrange("p a s -> p (a s)")
                        dst = chunk[:, 0:LAT].rearrange("p (s f) -> p f s", f=4)
                        act.wait_ge(s_y, g * 6 + (PRE + 3 * m + 1))
                        act.activation(dst[:, 0::2, :], y_ps[0][:].rearrange("p (a s) -> p a s", a=2), ACT.Copy,
                                       scale=2.0 ** -9).then_inc(s_yh, 1)
                        act.wait_ge(s_y, g * 6 + (PRE + 3 * m + 2))
                        act.wait_ge(s_yt, g * 2 + (PRE + m))
                        act.activation(bt[:], y_ps[1][:, 256:512], ACT.Copy).then_inc(s_bt, 1)
                        act.wait_ge(s_yt, g * 2 + (PRE + m + 1))
                        act.activation(dst[:, 1, :], yt[:, 0:256], ACT.Copy, scale=2.0 ** -9)
                        act.activation(dst[:, 3, :], yt[:, 256:512], ACT.Copy, scale=2.0 ** -9).then_inc(s_yh, 1)
                        act.wait_ge(s_y, g * 6 + (PRE + 3 * m + 3))
                        act.activation(chunk[:, LAT:T], y_ps[2][:, 0:256], ACT.Copy, scale=2.0 ** -8).then_inc(s_yh, 1)

            @block.vector
            def _(dve):
                for i in range(4):
                    dve.wait_ge(s_th, i + 1)
                    lo_part(dve, tabl[:, i], tabf[:], tabh[:, i]).then_inc(s_tl, 1)
                dve.wait_ge(s_c, 2)
                with dve.Fori(0, GR) as g:
                    dve.wait_ge(s_uvf, g * 8 + PRE)
                    dve.tensor_copy(gain[:], mod[:, 0, SC1, bass.ds(g * 2, 2), :]).then_inc(s_gain, 1)
                    for i in range(2):
                        dve.wait_ge(s_x[i], g * 32 + 32)
                        dve.wait_ge(s_gl, g * 2 + (PRE + i))
                        dve.tensor_tensor(xr[:].rearrange("p (n c) -> p n c", n=NT), xg[i][:],
                                          rstd_tm[:].rearrange("p (n c) -> p n c", c=1).to_broadcast([P, NT, P]),
                                          ALU.mult).then_inc(s_xr, 1)
                        dve.wait_ge(s_xr, g * 2 + (PRE + i + 1))
                        dve.tensor_tensor(sd[:], xr[:, 0:512], xr[:, 512:1024], ALU.add)
                        dve.tensor_tensor(xr[:, 512:1024], xr[:, 0:512], xr[:, 512:1024], ALU.subtract).then_inc(s_bf, 1)
                        dve.wait_ge(s_bf, g * 2 + (i + 1))
                        dve.tensor_tensor(xr[:, 0:256], sd[:, 0:256], sd[:, 256:512], ALU.add)
                        dve.tensor_tensor(xr[:, 256:512], sd[:, 0:256], sd[:, 256:512], ALU.subtract).then_inc(s_g, 1)
                        dve.wait_ge(s_gh, g * 2 + (i + 1))
                        lo_part(dve, gl[i][:].rearrange("p n c -> p (n c)"), xr[:],
                                gh[i][:].rearrange("p n c -> p (n c)")).then_inc(s_gl, 1)
                        for j, (_, b, off, v) in enumerate(SETS):
                            u = i * 4 + j
                            dve.wait_ge(s_uvf, g * 8 + (PRE + u + 1))
                            if j in FIXED:
                                c0 = uvf[u % 2][:, 0, 0:1]
                                dve.tensor_tensor(c0, c0, sdc[:, bass.ds(g * 2 + i, 1), v], ALU.add).then_inc(s_fix, 1)
                            dve.wait_ge(s_uvh, g * 8 + (u + 1))
                            lo_part(dve, uvl[:, b, i, :, off:off + 256], uvf[u % 2][:],
                                    uvh[:, b, i, :, off:off + 256]).then_inc(s_uvl, 1)
                    for m in range(2):
                        lo = nl[:, bass.ds(g * 2 + m, 1), :].rearrange("p a s -> p (a s)")
                        hi = f32(nh[:, bass.ds(g * 2 + m, 1), :]).rearrange("p a s -> p (a s)")
                        dlo, dhi = (a[:, 0:LAT].rearrange("p (s f) -> p f s", f=4) for a in (lo, hi))
                        dve.wait_ge(s_yh, g * 6 + (3 * m + 1))
                        dve.scalar_tensor_tensor(out=dlo[:, 0::2, :], in0=y_ps[0][:].rearrange("p (a s) -> p a s", a=2),
                                                 scalar=2.0 ** -9, in1=dhi[:, 0::2, :],
                                                 op0=ALU.mult, op1=ALU.subtract).then_inc(s_yl, 1)
                        dve.wait_ge(s_bt, g * 2 + (m + 1))
                        dve.wait_ge(s_yl, g * 6 + (PRE + 3 * m - 1))
                        dve.tensor_tensor(yt[:, 0:256], y_ps[1][:, 0:256], bt[:], ALU.add)
                        dve.tensor_tensor(yt[:, 256:512][:, ::-1], y_ps[1][:, 0:256], bt[:], ALU.subtract).then_inc(s_yt, 1)
                        dve.wait_ge(s_yh, g * 6 + (3 * m + 2))
                        dve.scalar_tensor_tensor(out=dlo[:, 1, :], in0=yt[:, 0:256], scalar=2.0 ** -9, in1=dhi[:, 1, :],
                                                 op0=ALU.mult, op1=ALU.subtract)
                        dve.scalar_tensor_tensor(out=dlo[:, 3, :], in0=yt[:, 256:512], scalar=2.0 ** -9,
                                                 in1=dhi[:, 3, :], op0=ALU.mult, op1=ALU.subtract).then_inc(s_yl, 1)
                        dve.wait_ge(s_yh, g * 6 + (3 * m + 3))
                        dve.scalar_tensor_tensor(out=lo[:, LAT:T], in0=y_ps[2][:, 0:256], scalar=2.0 ** -8,
                                                 in1=hi[:, LAT:T], op0=ALU.mult, op1=ALU.subtract).then_inc(s_yl, 1)

            @block.tensor
            def _(pe):
                pe.wait_ge(s_tl, 4)
                with pe.Fori(0, GR) as g:
                    for i in range(2):
                        pe.wait_ge(s_gl, g * 2 + (PRE + i + 1))
                        for j, (prods, b, off, v) in enumerate(SETS):
                            pe.wait_ge(s_uvf, g * 8 + (PRE + 4 * i + j - 3))
                            terms = [(tab, tile, kt) for tab, tile in prods for kt in range(2)]
                            for n, (tab, tile, kt) in enumerate(terms):
                                last = mm3(pe, seq_ps[j][:], (gh[i][:, tile + kt, :], gl[i][:, tile + kt, :]),
                                           (tabh[:, tab, kt, :], tabl[:, tab, kt, :]), n == 0, n == len(terms) - 1)
                            last.then_inc(s_seq, 1)
                    pe.wait_ge(s_uvl, g * 8 + (PRE + 8))
                    TERMS = [(cs, kt) for cs in range(2) for kt in range(2)]
                    for m in range(2):
                        def tab(cs, kt):
                            cols = slice(256 * cs + m * P, 256 * cs + (m + 1) * P)
                            return tabh[:, 0, kt, cols], tabl[:, 0, kt, cols]

                        def uv(b, kt, cs, lo, hi):
                            return uvh[:, b, kt, cs, lo:hi], uvl[:, b, kt, cs, lo:hi]
                        pe.wait_ge(s_yl, g * 6 + (PRE + 3 * m - 2))
                        for n, (cs, kt) in enumerate(TERMS):
                            last = mm3(pe, y_ps[0][:], tab(cs, kt), uv(0, kt, cs, 0, 512), n == 0, n == 3)
                        last.then_inc(s_y, 1)
                        pe.wait_ge(s_yt, g * 2 + (PRE + m))
                        for cs, kt in TERMS:
                            last = mm3(pe, y_ps[1][:, 256 * cs:256 * cs + 256], tab(cs, kt), uv(1, kt, cs, 0, 256),
                                       kt == 0, kt == 1)
                        last.then_inc(s_y, 1)
                        pe.wait_ge(s_yl, g * 6 + (PRE + 3 * m))
                        for n, (cs, kt) in enumerate(TERMS):
                            last = mm3(pe, y_ps[2][:, 0:256], tab(cs, kt), uv(1, kt, cs, 256, 512), n == 0, n == 3)
                        last.then_inc(s_y, 1)


def fnet_out(nc, sem, sb, banks, x, ctxt, fnet_w, mod, g1b, ident, nh, nl, ht):
    with ExitStack() as ph:
        xt = [sb(f"fx{i}", [P, D], where=ph) for i in range(2)]
        wf = [sb(f"fw{i}", [P, KC, P], where=ph) for i in range(2)]
        wh = [sb(f"fwh{i}", [P, KC, P], F32R, where=ph) for i in range(2)]
        wl = [sb(f"fwl{i}", [P, KC, P], F32R, where=ph) for i in range(2)]
        yb = [sb(f"fy{i}", [P, 512], where=ph) for i in range(3)]
        gate, bias = sb("gate", [P, 2, 2], where=ph), sb("gbias", [P, 2, 2], where=ph)
        tr_ps, o_ps = banks("tr_ps", 4, ph), banks("o_ps", 3, ph)
        s_gate = sem("o_gate")
        s_x = [sem(f"o_x{i}") for i in range(2)]
        s_w = [sem(f"o_w{i}") for i in range(2)]
        s_wh, s_wl, s_tr, s_eva, s_evd, s_o, s_yb, s_add = (sem(n) for n in (
            "o_wh", "o_wl", "o_tr", "o_ev_act", "o_ev_dve", "o_prod", "o_yb", "o_add"))
        with nc.Block() as block:
            @block.gpsimd
            def _(pool):
                for s in (s_wl, s_o, s_yb, s_add):
                    pool.sem_inc(s, PRE)

            @block.sync
            def _(sp):
                for t in range(NT):
                    if t >= 2:
                        sp.wait_ge(s_tr, 2 * (t - 1))
                    src = x[t * P:(t + 1) * P, :] if t < QB else ctxt[(t - QB) * P:(t - QB + 1) * P, :]
                    sp.dma_start(xt[t % 2][:], src).then_inc(s_x[t % 2], 16)
                with sp.Fori(0, KC // 2) as r:
                    for i in range(2):
                        sp.wait_ge(s_wl, r * 2 + (PRE + i - 1))
                        sp.dma_start(wf[i][:], fnet_w[bass.ds(r * 2 + i, 1)].rearrange("a p k n -> p (a k) n")).then_inc(s_w[i], 16)

            @block.scalar
            def _(act):
                for t in range(NT):
                    act.wait_ge(s_tr, 2 * t + 1)
                    act.activation(ht[:, 0:4, t * P:(t + 1) * P], tr_ps[2 * (t % 2)][:].rearrange("p (k c) -> p k c", k=4),
                                   ACT.Copy).then_inc(s_eva, 1)
                with act.Fori(0, KC // 2) as r:
                    act.wait_ge(s_gate, r + 1)
                    for i in range(2):
                        act.wait_ge(s_w[i], r * 16 + 16)
                        act.wait_ge(s_o, r * 6 + (PRE + 3 * i - 3))
                        act.activation(wh[i][:], wf[i][:], ACT.Copy).then_inc(s_wh, 1)
                        for b, (t0, n) in enumerate(BLOCKS):
                            act.wait_ge(s_o, r * 6 + (PRE + 3 * i + b + 1))
                            act.wait_ge(s_add, r * 6 + (PRE + 3 * i + b - 2))
                            v = int(t0 >= LAT)
                            act.activation(yb[b][:, 0:n], o_ps[b][:, 0:n], ACT.Identity, scale=gate[:, i, v:v + 1],
                                           bias=bias[:, i, v:v + 1]).then_inc(s_yb, 1)

            @block.vector
            def _(dve):
                for t in range(NT):
                    dve.wait_ge(s_tr, 2 * t + 2)
                    dve.tensor_copy(ht[:, 4:8, t * P:(t + 1) * P],
                                    tr_ps[2 * (t % 2) + 1][:].rearrange("p (k c) -> p k c", k=4)).then_inc(s_evd, 1)
                dve.wait_ge(s_evd, NT)
                dve.wait_ge(s_eva, NT)
                with dve.Fori(0, KC // 2) as r:
                    dve.wait_ge(s_yb, r * 6 + PRE)
                    dve.tensor_copy(gate[:], mod[:, 0, G1, bass.ds(r * 2, 2), :])
                    dve.tensor_copy(bias[:], g1b[:, bass.ds(r * 2, 2), :]).then_inc(s_gate, 1)
                    for i in range(2):
                        dve.wait_ge(s_wh, r * 2 + (i + 1))
                        lo_part(dve, wl[i][:], wf[i][:], wh[i][:]).then_inc(s_wl, 1)
                        for b, (t0, n) in enumerate(BLOCKS):
                            dve.wait_ge(s_yb, r * 6 + (PRE + 3 * i + b + 1))
                            h = ht[:, bass.ds(r * 2 + i, 1), t0:t0 + n].rearrange("p a s -> p (a s)")
                            dve.tensor_tensor(h, h, yb[b][:, 0:n], ALU.add).then_inc(s_add, 1)

            @block.tensor
            def _(pe):
                for t in range(NT):
                    pe.wait_ge(s_x[t % 2], 16 * (t // 2 + 1))
                    if t >= 2:
                        pe.wait_ge(s_eva, t - 1)
                        pe.wait_ge(s_evd, t - 1)
                    for half in range(2):
                        for k in range(4):
                            kk = 4 * half + k
                            last = pe.transpose(tr_ps[2 * (t % 2) + half][:, k * P:(k + 1) * P],
                                                xt[t % 2][:, kk * P:(kk + 1) * P], ident[:])
                        last.then_inc(s_tr, 1)
                with pe.Fori(0, KC // 2) as r:
                    for i in range(2):
                        pe.wait_ge(s_wl, r * 2 + (PRE + i + 1))
                        for b, (t0, n) in enumerate(BLOCKS):
                            pe.wait_ge(s_yb, r * 6 + (PRE + 3 * i + b - 2))
                            for k in range(KC):
                                last = mm3(pe, o_ps[b][:, 0:n], (wh[i][:, k, :], wl[i][:, k, :]),
                                           (nh[:, k, t0:t0 + n], nl[:, k, t0:t0 + n]), k == 0, k == KC - 1)
                            last.then_inc(s_o, 1)


def mlp(nc, sem, sb, banks, layer, nblocks, w1, w2, mod, meanw, eps, nh, nl, ht):
    PAIRS = DFF // (2 * P)
    TB = BLOCKS[:nblocks]
    NB = nblocks
    N = f"l{layer}_"
    U1, U2 = 2 * NB, KC * NB
    with ExitStack() as ph:
        ah = sb(N + "ah", [P, 2, T], F32R, where=ph)
        al = sb(N + "al", [P, 2, T], F32R, where=ph)
        w1f, w2f = sb(N + "w1f", [P, KC, 2 * P], where=ph), sb(N + "w2f", [P, 2, D], where=ph)
        w1h, w2h = sb(N + "w1h", [P, KC, 2 * P], F32R, where=ph), sb(N + "w2h", [P, 2, D], F32R, where=ph)
        w1l, w2l = sb(N + "w1l", [P, KC, 2 * P], F32R, where=ph), sb(N + "w2l", [P, 2, D], F32R, where=ph)
        rel = [sb(f"{N}rel{i}", [P, 512], where=ph) for i in range(2)]
        sq = [sb(f"{N}sq{i}", [P, 512], where=ph) for i in range(2)]
        rb = sb(N + "rb", [P, 512], where=ph)
        z_ps, y_ps = banks(N + "z_ps", 2, ph), banks(N + "yy_ps", 4, ph)
        ms_ps = banks(N + "ms_ps", 2, ph)
        s_w1, s_w2 = sem(N + "w1"), sem(N + "w2")
        s_sq, s_ms, s_std, s_rb, s_t, s_n, s_nh, s_nl = (sem(N + n) for n in ("nsq", "nms", "nstd", "nrb", "nt", "nn", "nnh", "nnl"))
        s_w1h, s_w1l, s_w2h, s_w2l = (sem(N + n) for n in ("w1h", "w1l", "w2h", "w2l"))
        s_z, s_rel, s_ah, s_al, s_sqr, s_y, s_acc = (sem(N + n) for n in ("z", "rel", "ah", "al", "sqr", "y", "acc"))
        with nc.Block() as block:
            @block.sync
            def _(sp):
                with sp.Fori(0, PAIRS) as p:
                    sp.wait_ge(s_w1l, p + PRE)
                    sp.dma_start(w1f[:], w1[layer, bass.ds(p, 1)].rearrange("a p k n -> p (a k) n")).then_inc(s_w1, 16)
                    sp.wait_ge(s_w2l, p + PRE)
                    sp.dma_start(w2f[:], w2[layer, bass.ds(p * 2, 2)].rearrange("c p n -> p c n")).then_inc(s_w2, 16)

            @block.gpsimd
            def _(pool):
                for s in (s_w1l, s_w2l, s_z, s_rel, s_al, s_y, s_acc):
                    pool.sem_inc(s, PRE)
                with pool.Fori(0, PAIRS) as p:
                    pool.wait_ge(s_w1h, p + 1)
                    lo_part(pool, w1l[:], w1f[:], w1h[:]).then_inc(s_w1l, 1)
                    pool.wait_ge(s_w2h, p + 1)
                    lo_part(pool, w2l[:], w2f[:], w2h[:]).then_inc(s_w2l, 1)

            @block.scalar
            def _(act):
                u = 0
                for b, (t0, n) in enumerate(TB):
                    for k in range(KC):
                        if b * KC + k >= 2:
                            act.wait_ge(s_ms, b * KC + k - 1)
                        act.activation(rel[k % 2][:, 0:n], ht[:, k, t0:t0 + n], ACT.Square).then_inc(s_sq, 1)
                    act.wait_ge(s_ms, (b + 1) * KC)
                    if b:
                        act.wait_ge(s_t, b * KC)
                    act.activation(rb[:, 0:n], ms_ps[b % 2][:, 0:n], ACT.Sqrt, bias=eps[:]).then_inc(s_std, 1)
                    for k in range(KC):
                        v = int(t0 >= LAT)
                        act.wait_ge(s_t, u + 1)
                        act.activation(sq[k % 2][:, 0:n], sq[k % 2][:, 0:n], ACT.Identity, scale=mod[:, layer, SC2, k, v:v + 1],
                                       bias=mod[:, layer, SH2, k, v:v + 1]).then_inc(s_n, 1)
                        act.wait_ge(s_n, u + 1)
                        act.activation(nh[:, k, t0:t0 + n], sq[k % 2][:, 0:n], ACT.Copy).then_inc(s_nh, 1)
                        u += 1
                act.wait_ge(s_nl, u)
                with act.Fori(0, PAIRS) as p:
                    act.wait_ge(s_w1, p * 16 + 16)
                    act.wait_ge(s_z, p * U1 + PRE)
                    act.activation(w1h[:], w1f[:], ACT.Copy).then_inc(s_w1h, 1)
                    act.wait_ge(s_w2, p * 16 + 16)
                    act.wait_ge(s_y, p * U2 + PRE)
                    act.activation(w2h[:], w2f[:], ACT.Copy).then_inc(s_w2h, 1)
                    for c in range(2):
                        for b, (t0, n) in enumerate(TB):
                            u = c * NB + b
                            act.wait_ge(s_z, p * U1 + (PRE + u + 1))
                            act.wait_ge(s_al, p * U1 + (PRE + u - 1))
                            act.activation(rel[u % 2][:, 0:n], z_ps[u % 2][:, 0:n], ACT.Relu).then_inc(s_rel, 1)
                            act.wait_ge(s_rel, p * U1 + (PRE + u + 1))
                            act.activation(ah[:, c, t0:t0 + n], rel[u % 2][:, 0:n], ACT.Square).then_inc(s_ah, 1)

            @block.vector
            def _(dve):
                u = 0
                for b, (t0, n) in enumerate(TB):
                    dve.wait_ge(s_std, b + 1)
                    dve.reciprocal(rb[:, 0:n], rb[:, 0:n]).then_inc(s_rb, 1)
                    dve.wait_ge(s_rb, b + 1)
                    for k in range(KC):
                        if u >= 2:
                            dve.wait_ge(s_nl, u - 1)
                        dve.tensor_tensor(sq[k % 2][:, 0:n], ht[:, k, t0:t0 + n], rb[:, 0:n], ALU.mult).then_inc(s_t, 1)
                        if u >= 1:
                            pb, pk = divmod(u - 1, KC)
                            p0, pn = TB[pb]
                            dve.wait_ge(s_nh, u)
                            lo_part(dve, nl[:, pk, p0:p0 + pn], sq[pk % 2][:, 0:pn], nh[:, pk, p0:p0 + pn]).then_inc(s_nl, 1)
                        u += 1
                p0, pn = TB[-1]
                dve.wait_ge(s_nh, u)
                lo_part(dve, nl[:, KC - 1, p0:p0 + pn], sq[(KC - 1) % 2][:, 0:pn], nh[:, KC - 1, p0:p0 + pn]).then_inc(s_nl, 1)
                with dve.Fori(0, PAIRS) as p:
                    for c in range(2):
                        for b, (t0, n) in enumerate(TB):
                            u = c * NB + b
                            dve.wait_ge(s_rel, p * U1 + (PRE + u + 1))
                            dve.tensor_tensor(sq[u % 2][:, 0:n], rel[u % 2][:, 0:n], rel[u % 2][:, 0:n], ALU.mult).then_inc(s_sqr, 1)
                            dve.wait_ge(s_sqr, p * U1 + (u + 1))
                            dve.wait_ge(s_ah, p * U1 + (u + 1))
                            lo_part(dve, al[:, c, t0:t0 + n], sq[u % 2][:, 0:n], ah[:, c, t0:t0 + n]).then_inc(s_al, 1)
                    dve.wait_ge(s_acc, p * U2 + PRE)
                    for b, (t0, n) in enumerate(TB):
                        for m in range(KC):
                            u = b * KC + m
                            dve.wait_ge(s_y, p * U2 + (PRE + u + 1))
                            h = ht[:, m, t0:t0 + n]
                            v = int(t0 >= LAT)
                            dve.scalar_tensor_tensor(out=h, in0=y_ps[u % 4][:, 0:n], scalar=mod[:, layer, G2, m, v:v + 1], in1=h,
                                                     op0=ALU.mult, op1=ALU.add).then_inc(s_acc, 1)

            @block.tensor
            def _(pe):
                for b, (t0, n) in enumerate(TB):
                    if b >= 2:
                        pe.wait_ge(s_std, b - 1)
                    for k in range(KC):
                        pe.wait_ge(s_sq, b * KC + k + 1)
                        pe.matmul(ms_ps[b % 2][:, 0:n], meanw[:], rel[k % 2][:, 0:n], start=(k == 0), stop=(k == KC - 1)).then_inc(s_ms, 1)
                pe.wait_ge(s_nl, NB * KC)
                with pe.Fori(0, PAIRS) as p:
                    pe.wait_ge(s_w1l, p + (PRE + 1))
                    for c in range(2):
                        for b, (t0, n) in enumerate(TB):
                            u = c * NB + b
                            pe.wait_ge(s_rel, p * U1 + (PRE + u - 1))
                            for k in range(KC):
                                cols = slice(c * P, (c + 1) * P)
                                last = mm3(pe, z_ps[u % 2][:, 0:n], (w1h[:, k, cols], w1l[:, k, cols]),
                                           (nh[:, k, t0:t0 + n], nl[:, k, t0:t0 + n]), k == 0, k == KC - 1)
                            last.then_inc(s_z, 1)
                    pe.wait_ge(s_w2l, p + (PRE + 1))
                    for b, (t0, n) in enumerate(TB):
                        pe.wait_ge(s_al, p * U1 + (PRE + NB + b + 1))
                        for m in range(KC):
                            u = b * KC + m
                            pe.wait_ge(s_acc, p * U2 + (PRE + u - 3))
                            for c in range(2):
                                last = mm3(pe, y_ps[u % 4][:, 0:n], (w2h[:, c, m * P:(m + 1) * P], w2l[:, c, m * P:(m + 1) * P]),
                                           (ah[:, c, t0:t0 + n], al[:, c, t0:t0 + n]), c == 0, c == 1)
                            last.then_inc(s_y, 1)


def norm_out(nc, sem, sb, banks, layer, park, mod, meanw, eps, nh, nl, ht):
    with ExitStack() as ph:
        sq = [sb(f"nsq{i}", [P, 512], where=ph) for i in range(2)]
        tn = [sb(f"ntn{i}", [P, 512], where=ph) for i in range(2)]
        rb = [sb(f"nrb{i}", [P, 512], where=ph) for i in range(2)]
        ms_ps = banks("nms_ps", 3, ph)
        s_park, s_sq, s_ms, s_std, s_rb, s_t, s_n, s_nh, s_nl = (sem("q_" + n) for n in (
            "park", "sq", "ms", "std", "rb", "t", "n", "nh", "nl"))
        UN = [(b, t0, n, k) for b, (t0, n) in enumerate(BLOCKS) for k in range(KC)]
        with nc.Block() as block:
            @block.sync
            def _(sp):
                sp.dma_start(park, ht[:, :, 0:LAT]).then_inc(s_park, 16)
                sp.wait_ge(s_park, 16)

            @block.scalar
            def _(act):
                def squares(b):
                    t0, n = BLOCKS[b]
                    for k in range(KC):
                        if b * KC + k >= 2:
                            act.wait_ge(s_ms, b * KC + k - 1)
                        act.activation(sq[k % 2][:, 0:n], ht[:, k, t0:t0 + n], ACT.Square).then_inc(s_sq, 1)
                    act.wait_ge(s_ms, (b + 1) * KC)
                    if b >= 2:
                        act.wait_ge(s_t, (b - 1) * KC)
                    act.activation(rb[b % 2][:, 0:n], ms_ps[b][:, 0:n], ACT.Sqrt, bias=eps[:]).then_inc(s_std, 1)
                squares(0)
                for u, (b, t0, n, k) in enumerate(UN):
                    if k == 0 and b + 1 < len(BLOCKS):
                        squares(b + 1)
                    v = int(t0 >= LAT)
                    act.wait_ge(s_t, u + 1)
                    act.activation(tn[u % 2][:, 0:n], tn[u % 2][:, 0:n], ACT.Identity, scale=mod[:, layer, SC1, k, v:v + 1],
                                   bias=mod[:, layer, SH1, k, v:v + 1]).then_inc(s_n, 1)
                    act.wait_ge(s_n, u + 1)
                    act.activation(nh[:, k, t0:t0 + n], tn[u % 2][:, 0:n], ACT.Copy).then_inc(s_nh, 1)

            @block.vector
            def _(dve):
                def low(u):
                    _, t0, n, k = UN[u]
                    dve.wait_ge(s_nh, u + 1)
                    lo_part(dve, nl[:, k, t0:t0 + n], tn[u % 2][:, 0:n], nh[:, k, t0:t0 + n]).then_inc(s_nl, 1)
                for u, (b, t0, n, k) in enumerate(UN):
                    if k == 0:
                        dve.wait_ge(s_std, b + 1)
                        dve.reciprocal(rb[b % 2][:, 0:n], rb[b % 2][:, 0:n]).then_inc(s_rb, 1)
                        dve.wait_ge(s_rb, b + 1)
                    if u >= 2:
                        dve.wait_ge(s_nl, u - 1)
                    dve.tensor_tensor(tn[u % 2][:, 0:n], ht[:, k, t0:t0 + n], rb[b % 2][:, 0:n], ALU.mult).then_inc(s_t, 1)
                    if u >= 1:
                        low(u - 1)
                low(len(UN) - 1)

            @block.tensor
            def _(pe):
                for u, (b, t0, n, k) in enumerate(UN):
                    pe.wait_ge(s_sq, u + 1)
                    pe.matmul(ms_ps[b][:, 0:n], meanw[:], sq[k % 2][:, 0:n], start=(k == 0), stop=(k == KC - 1)).then_inc(s_ms, 1)


def qkv(nc, sem, sb, banks, wqkv, qkg, rope, ident, eps, nh, nl, qd, kh, kl, vs):
    KV0 = D
    COLS = [(KV0, 2 * KVH * HD), (0, 512), (512, 512)]
    UNITS = [(0, t) for t in range(NT)] + [(c, t) for c in (1, 2) for t in range(QB)]
    HB = 8
    first = {c: min(u for u, (cc, _) in enumerate(UNITS) if cc == c) for c in range(3)}
    with ExitStack() as ph:
        wf = sb("qwf", [P, KC // 2, 512], where=ph)
        wh = sb("qwh", [P, KC, 512], F32R, where=ph)
        wl = sb("qwl", [P, KC, 512], F32R, where=ph)
        g = sb("qkg_sb", [P, 2, HD], where=ph)
        ct = sb("ct", [P, 2, NT, HD], where=ph)
        st = sb("st", [P, 2, NT, HD], where=ph)
        raw = [sb(f"raw{i}", [P, 512], where=ph) for i in range(2)]
        tmp = sb("qtmp", [P, 512], where=ph)
        qo = [sb(f"qo{i}", [P, 512], where=ph) for i in range(2)]
        kr = sb("kr", [P, NT, KVH, 2, HD], where=ph)
        ss = sb("ss", [P, 2, HB], where=ph)
        p_ps, tr_ps = banks("qkv_ps", 3, ph), banks("ktr_ps", 2, ph)
        s_rope, s_g, s_tabs, s_w, s_wh, s_wl = (sem("k_" + n) for n in ("rope", "g", "tabs", "w", "wh", "wl"))
        s_p, s_raw, s_sq, s_ss, s_std, s_dv, s_done, s_vh, s_vl = (sem("k_" + n) for n in (
            "prod", "raw", "sq", "ss", "std", "dv", "done", "vh", "vl"))
        s_tr, s_kh, s_kl, s_pad = (sem("k_" + n) for n in ("tr", "kh", "kl", "pad"))
        s_q = [sem(f"k_q{i}") for i in range(2)]
        ropev = wf[:].rearrange("p a b -> p (a b)")[:, 0:2 * NT * HD].rearrange("p (a t d) -> p a t d", a=2, t=NT)

        def halves(ap):
            return ap.rearrange("p h (a s c) -> p h a s c", a=2, s=2)

        with nc.Block() as block:
            @block.sync
            def _(sp):
                sp.dma_start(ropev, rope).then_inc(s_rope, 16)
                sp.dma_start(g[:].rearrange("p a d -> p (a d)"), qkg).then_inc(s_g, 16)
                sp.wait_ge(s_tabs, 10)
                n = 0
                for c0, w in COLS:
                    for hf in range(2):
                        if n:
                            sp.wait_ge(s_wl, n)
                        src = wqkv[512 * hf:512 * hf + 512, c0:c0 + w].rearrange("(k p) n -> p k n", p=P)
                        sp.dma_start(wf[:, :, 0:w], src).then_inc(s_w, 16)
                        n += 1

            @block.gpsimd
            def _(pool):
                for b in (0, QB + 1):
                    pool.memset(f32(kh[:, :, b * P:(b + 1) * P]), 0.0).then_inc(s_pad, 1)
                    pool.memset(f32(kl[:, :, b * P:(b + 1) * P]), 0.0).then_inc(s_pad, 1)
                    pool.memset(f32(vs[:, b]), 0.0).then_inc(s_pad, 1)
                for u in range(NT, len(UNITS)):
                    c, t = UNITS[u]
                    pool.wait_ge(s_done, u + 1)
                    pool.dma_start(qd[t, 2 * (c - 1):2 * c].rearrange("a p n -> p a n"),
                                   qo[u % 2][:].rearrange("p (a n) -> p a n", a=2)).then_inc(s_q[u % 2], 16)
                for i in range(2):
                    pool.wait_ge(s_q[i], 16 * QB)

            @block.scalar
            def _(act):
                def weights(c):
                    w = COLS[c][1]
                    for hf in range(2):
                        act.wait_ge(s_w, 16 * (2 * c + hf + 1))
                        if c and hf == 0:
                            act.wait_ge(s_p, first[c])
                        act.activation(wh[:, 4 * hf:4 * hf + 4, 0:w], wf[:, :, 0:w], ACT.Copy).then_inc(s_wh, 1)
                weights(0)
                for u, (c, t) in enumerate(UNITS):
                    if u == first[c] and c:
                        weights(c)
                    w = COLS[c][1]
                    nq = KVH * HD if c == 0 else 512
                    H = nq // HD
                    act.wait_ge(s_p, u + 1)
                    if u >= 2:
                        act.wait_ge(s_done, u - 1)
                    act.activation(raw[u % 2][:, 0:w], p_ps[u % 3][:, 0:w], ACT.Copy).then_inc(s_raw, 1)
                    if u >= 1:
                        act.wait_ge(s_done, u)
                    act.activation(tmp[:, 0:nq], p_ps[u % 3][:, 0:nq], ACT.Square).then_inc(s_sq, 1)
                    if c == 0:
                        tb = t + 1 if t < QB else t + 2
                        v = raw[u % 2][:, 128:256].rearrange("p (a d) -> p a d", a=KVH)
                        act.wait_ge(s_raw, u + 1)
                        act.activation(vs[:, tb, :, 0:HD], v, ACT.Copy).then_inc(s_vh, 1)
                    act.wait_ge(s_ss, u + 1)
                    act.activation(ss[:, u % 2, 0:H], ss[:, u % 2, 0:H], ACT.Sqrt, bias=eps[:], scale=1.0 / HD).then_inc(s_std, 1)
                for t in range(NT):
                    for gg in range(KVH):
                        i = t * KVH + gg
                        tb = t + 1 if t < QB else t + 2
                        act.wait_ge(s_tr, i + 1)
                        act.activation(kh[:, gg, tb * P:(tb + 1) * P], tr_ps[i % 2][:, 0:P], ACT.Copy).then_inc(s_kh, 1)

            @block.vector
            def _(dve):
                chain = [0]

                def link(ins):
                    chain[0] += 1
                    ins.then_inc(s_dv, 1)
                    dve.wait_ge(s_dv, chain[0])

                dve.wait_ge(s_rope, 16)
                dve.wait_ge(s_g, 16)
                link(dve.tensor_scalar_mul(g[:, 0], g[:, 0], -HD ** -0.5))
                for a in range(2):
                    gb = g[:, a:a + 1, :].to_broadcast([P, NT, HD])
                    dve.tensor_tensor(ct[:, a], ropev[:, 0], gb, ALU.mult).then_inc(s_tabs, 1)
                    for ax in range(2):
                        for s in range(2):
                            lanes = slice(32 * ax + 16 * s, 32 * ax + 16 * s + 16)
                            partner = slice(32 * ax + 16 * (1 - s), 32 * ax + 16 * (1 - s) + 16)
                            dve.tensor_tensor(st[:, a, :, lanes], ropev[:, 1, :, lanes], g[:, a:a + 1, partner].to_broadcast([P, NT, 16]),
                                              ALU.mult).then_inc(s_tabs, 1)
                dve.wait_ge(s_tabs, 10)

                def weights(c):
                    w = COLS[c][1]
                    for hf in range(2):
                        dve.wait_ge(s_wh, 2 * c + hf + 1)
                        lo_part(dve, wl[:, 4 * hf:4 * hf + 4, 0:w], wf[:, :, 0:w], wh[:, 4 * hf:4 * hf + 4, 0:w]).then_inc(s_wl, 1)
                weights(0)
                for u, (c, t) in enumerate(UNITS):
                    if u == first[c] and c:
                        weights(c)
                    nq = KVH * HD if c == 0 else 512
                    H = nq // HD
                    q = raw[u % 2][:, 0:nq].rearrange("p (h d) -> p h d", d=HD)
                    m = tmp[:, 0:nq].rearrange("p (h d) -> p h d", d=HD)
                    a = 1 if c == 0 else 0
                    dve.wait_ge(s_sq, u + 1)
                    dve.reduce_sum(ss[:, u % 2, 0:H], m, axis=AX.X).then_inc(s_ss, 1)
                    if c == 0:
                        tb = t + 1 if t < QB else t + 2
                        dve.wait_ge(s_vh, u + 1)
                        lo_part(dve, vs[:, tb, :, HD:2 * HD], raw[u % 2][:, 128:256].rearrange("p (a d) -> p a d", a=KVH),
                                vs[:, tb, :, 0:HD]).then_inc(s_vl, 1)
                    dve.wait_ge(s_std, u + 1)
                    link(dve.reciprocal(ss[:, u % 2, 0:H], ss[:, u % 2, 0:H]))
                    dve.wait_ge(s_raw, u + 1)
                    link(dve.tensor_tensor(q, q, ss[:, u % 2, 0:H].rearrange("p (h o) -> p h o", o=1).to_broadcast([P, H, HD]), ALU.mult))
                    for s in range(2):
                        r = st[:, a, t:t + 1, :].to_broadcast([P, H, HD])
                        ins = dve.tensor_tensor(halves(m)[:, :, :, s, :], halves(q)[:, :, :, 1 - s, :], halves(r)[:, :, :, s, :], ALU.mult)
                    link(ins)
                    dst = kr[:, t, :, 0, :] if c == 0 else qo[u % 2][:].rearrange("p (h d) -> p h d", d=HD)
                    if c and u - NT >= 2:
                        dve.wait_ge(s_q[u % 2], 16 * ((u - NT) // 2))
                    link(dve.tensor_tensor(dst, q, ct[:, a, t:t + 1, :].to_broadcast([P, H, HD]), ALU.mult))
                    if c == 0:
                        dve.tensor_tensor(kr[:, t, :, 1, :], dst, m, ALU.add)
                    dve.tensor_tensor(dst, dst, m, ALU.add).then_inc(s_done, 1)
                for t in range(NT):
                    for gg in range(KVH):
                        i = t * KVH + gg
                        tb = t + 1 if t < QB else t + 2
                        dve.wait_ge(s_kh, i + 1)
                        lo_part(dve, kl[:, gg, tb * P:(tb + 1) * P], tr_ps[i % 2][:, 0:P], kh[:, gg, tb * P:(tb + 1) * P]).then_inc(s_kl, 1)

            @block.tensor
            def _(pe):
                for u, (c, t) in enumerate(UNITS):
                    if u == first[c]:
                        pe.wait_ge(s_wl, 2 * c + 2)
                    if u >= 3:
                        pe.wait_ge(s_sq, u - 2)
                    w = COLS[c][1]
                    for k in range(KC):
                        cols = slice(t * P, (t + 1) * P)
                        last = mm3(pe, p_ps[u % 3][:, 0:w], (nh[:, k, cols], nl[:, k, cols]), (wh[:, k, 0:w], wl[:, k, 0:w]),
                                   k == 0, k == KC - 1)
                    last.then_inc(s_p, 1)
                pe.wait_ge(s_done, NT)
                for t in range(NT):
                    for gg in range(KVH):
                        i = t * KVH + gg
                        if i >= 2:
                            pe.wait_ge(s_kl, i - 1)
                        pe.transpose(tr_ps[i % 2][:, 0:P], kr[:, t, gg].rearrange("p a d -> p (a d)"), ident[:]).then_inc(s_tr, 1)


def attention(nc, sem, sb, banks, masks, sink, ident, qd, kh, kl, vs, nh, nl):
    PAIRS = QB // 2
    NQ = 8
    KB = KEYS // P
    W = 3 * P
    with ExitStack() as ph:
        mstore = sb("mstore", [P, QB, 2, P], where=ph)
        mask = sb("mask", [P, KEYS], where=ph)
        nsink, zero4 = sb("nsink", [P, HEADS], where=ph), sb("zero4", [P, 4], where=ph)
        qb = sb("qb", [P, 4, 4, 2, HD], where=ph)
        qs = [sb(f"qs{i}", [P, 512], F32R, where=ph) for i in range(2)]
        vw = [sb(f"vw{i}", [P, 3, KVH, 2 * HD], F32R, where=ph) for i in range(2)]
        sc = sb("sc", [P, 2, 4, KEYS + 1], where=ph)
        mn, den = sb("mn", [P, 2, 4], where=ph), sb("den", [P, 2, 4], where=ph)
        pth = [sb(f"pth{i}", [P, 512], F32R, where=ph) for i in range(2)]
        ptl = [sb(f"ptl{i}", [P, 512], F32R, where=ph) for i in range(2)]
        ot, of = sb("ot", [HD, 512], where=ph), sb("of", [P, 2, P], where=ph)
        s_ps = [ph.enter_context(nc.psum_tensor(f"s_ps{i}", [P, 1024], F32)) for i in range(2)]
        q_ps, t_ps, o_ps = banks("q_ps", 1, ph)[0], banks("t_ps", 2, ph), banks("pv_ps", 1, ph)[0]
        s_ms, s_sk, s_ns, s_z, s_m0, s_mask, s_vw, s_held = (sem("t_" + n) for n in (
            "mstore", "sink", "nsink", "zero", "mask0", "mask", "vw", "held"))
        s_qb = [sem(f"t_qb{i}") for i in range(4)]
        s_qtr, s_qh, s_qs, s_sc, s_s, s_col, s_e, s_rd, s_p = (sem("t_" + n) for n in (
            "qtr", "qh", "qs", "scores", "masked", "sinkcol", "exp", "rden", "prob"))
        s_pt, s_ph, s_pl, s_o, s_ot, s_of, s_oh, s_ol = (sem("t_" + n) for n in ("ptr", "pth", "ptl", "pv", "ot", "of", "oh", "ol"))

        def at(jj, n, c, k):
            return jj * (NQ * c) + (PRE + c * n + k)

        def schedule(eng, steps_q, steps_a, steps_b):
            steps_q(0, 0)
            steps_a(0, 0)
            steps_q(0, 1)
            with eng.Fori(0, PAIRS - 1) as jj:
                for n in range(NQ):
                    steps_a(jj, n + 1)
                    steps_q(jj, n + 2)
                    steps_b(jj, n)
            for n in range(NQ):
                if n + 1 < NQ:
                    steps_a(PAIRS - 1, n + 1)
                if n + 2 < NQ:
                    steps_q(PAIRS - 1, n + 2)
                steps_b(PAIRS - 1, n)

        with nc.Block() as block:
            @block.sync
            def _(sp):
                sp.dma_start(mstore[:], masks).then_inc(s_ms, 16)
                sp.dma_start(nsink[:], sink).then_inc(s_sk, 16)
                with sp.Fori(0, QB) as j:
                    for i in range(4):
                        sp.wait_ge(s_qtr, j * 4 + (PRE + i - 3))
                        for twice in range(2):
                            sp.dma_start(qb[:, i, :, twice, :], qd[bass.ds(j, 1), i].rearrange("a p (h d) -> p (a h) d", d=HD)).then_inc(s_qb[i], 16)

            @block.gpsimd
            def _(pool):
                pool.memset(zero4[:], 0.0).then_inc(s_z, 1)
                for s in (s_qtr, s_qh, s_qs, s_sc, s_s, s_col, s_e, s_rd, s_p, s_pt, s_ph, s_pl, s_o, s_ot, s_of, s_oh, s_ol):
                    pool.sem_inc(s, PRE)
                pool.wait_ge(s_z, 1)
                pool.wait_ge(s_ns, 1)

                def step_a(jj, n):
                    i, h0 = n % 2, 4 * (n % 4)
                    pool.wait_ge(s_pt, at(jj, n, KB, -KB))
                    pool.tensor_tensor(sc[:, i, :, KEYS], nsink[:, h0:h0 + 4], zero4[:], ALU.add).then_inc(s_col, 1)
                    pool.wait_ge(s_rd, at(jj, n, 1, 1))
                    for h in range(4):
                        pool.tensor_tensor(sc[:, i, h, 0:KEYS], sc[:, i, h, 0:KEYS], den[:, i, h:h + 1].to_broadcast([P, KEYS]),
                                           ALU.mult).then_inc(s_p, 1)
                schedule(pool, lambda jj, n: None, step_a, lambda jj, n: None)

            @block.scalar
            def _(act):
                def step_q(jj, n):
                    act.wait_ge(s_qtr, at(jj, n, 1, 1))
                    act.wait_ge(s_sc, at(jj, n, 4, -4))
                    act.activation(qs[n % 2][:], q_ps[:], ACT.Copy).then_inc(s_qh, 1)

                def step_a(jj, n):
                    i = n % 2
                    act.wait_ge(s_col, at(jj, n, 1, 1))
                    for h in range(4):
                        act.wait_ge(s_s, at(jj, n, 4, h + 1))
                        act.activation(sc[:, i, h, :], sc[:, i, h, :], ACT.Exp, scale=-1.0, bias=mn[:, i, h:h + 1],
                                       accum_out=den[:, i, h:h + 1]).then_inc(s_e, 1)

                def step_b(jj, n):
                    for kb in range(KB):
                        slot = (n + kb) % 2
                        act.wait_ge(s_pt, at(jj, n, KB, kb + 1))
                        act.wait_ge(s_o, at(jj, n, KB, kb - 1))
                        act.activation(pth[slot][:], t_ps[slot][:], ACT.Copy).then_inc(s_ph, 1)
                    act.wait_ge(s_o, at(jj, n, KB, KB))
                    act.wait_ge(s_of, at(jj, n, 1, 0))
                    act.activation(ot[:], o_ps[0:HD, :], ACT.Copy).then_inc(s_ot, 1)
                schedule(act, step_q, step_a, step_b)

            @block.vector
            def _(dve):
                dve.wait_ge(s_sk, 16)
                dve.tensor_scalar_mul(nsink[:], nsink[:], -1.0).then_inc(s_ns, 1)
                dve.memset(mask[:], 0.0).then_inc(s_m0, 1)
                dve.wait_ge(s_m0, 1)
                dve.wait_ge(s_ns, 1)
                dve.wait_ge(s_ms, 16)

                def step_q(jj, n):
                    low = qs[n % 2][HD:P, :]
                    dve.wait_ge(s_qh, at(jj, n, 1, 1))
                    dve.tensor_tensor(low, q_ps[HD:P, :], f32(low), ALU.subtract).then_inc(s_qs, 1)

                def step_a(jj, n):
                    i, h0, dj = n % 2, 4 * (n % 4), n // 4
                    if n % 4 == 0:
                        dve.wait_ge(s_s, at(jj, n, 4, 0))
                        dve.wait_ge(s_o, at(jj, n, KB, -4 * KB))
                        dve.tensor_scalar_mul(vw[dj % 2][:], f32(vs[:, bass.ds(jj * 2 + dj, 3)]), 1.0).then_inc(s_vw, 1)
                        for side in range(2):
                            dve.tensor_scalar_mul(mask[:, 2 * side * P:(2 * side + 1) * P],
                                                  mstore[:, bass.ds(jj * 2 + dj, 1), side].rearrange("p a n -> p (a n)"), 1.0).then_inc(s_mask, 1)
                        dve.wait_ge(s_mask, jj * 4 + (2 * dj + 2))
                    for h in range(4):
                        dve.wait_ge(s_sc, at(jj, n, 4, h + 1))
                        dve.wait_ge(s_pt, at(jj, n, KB, -KB))
                        dve.sem_inc(s_held, 1)
                        dve.tensor_tensor_reduce(out=sc[:, i, h, 0:KEYS], in0=s_ps[h % 2][:, P:P + KEYS], in1=mask[:], scale=1.0,
                                                 scalar=nsink[:, h0 + h:h0 + h + 1], op0=ALU.add, op1=ALU.min,
                                                 accum_out=mn[:, i, h:h + 1]).then_inc(s_s, 1)
                    if n == 0:
                        recip(jj, n)

                def recip(jj, n):
                    i = n % 2
                    dve.wait_ge(s_e, at(jj, n, 4, 4))
                    dve.reciprocal(den[:, i], den[:, i]).then_inc(s_rd, 1)

                def step_b(jj, n):
                    for kb in range(KB):
                        slot = (n + kb) % 2
                        if kb == 1 and not (jj is PAIRS - 1 and n == NQ - 1):
                            recip(jj, n + 1)
                        dve.wait_ge(s_ph, at(jj, n, KB, kb + 1))
                        lo_part(dve, ptl[slot][:], t_ps[slot][:], pth[slot][:]).then_inc(s_pl, 1)
                    dve.wait_ge(s_ot, at(jj, n, 1, 1))
                    hi, lo = ot[:].rearrange("p (c s q) -> p c s q", c=2, s=2), o_ps[HD:P, :].rearrange("p (c s q) -> p c s q", c=2, s=2)
                    for s in range(2):
                        ins = dve.tensor_tensor(of[HD * s:HD * s + HD], lo[:, :, s, :], hi[:, :, s, :], ALU.add)
                    ins.then_inc(s_of, 1)
                    c0 = 2 * (n % 4)
                    cols = bass.ds(jj * (2 * P) + (n // 4) * P, P)
                    dve.wait_ge(s_of, at(jj, n, 1, 1))
                    dve.tensor_scalar_mul(nh[:, c0:c0 + 2, cols], of[:], 1.0).then_inc(s_oh, 1)
                    dve.wait_ge(s_oh, at(jj, n, 1, 1))
                    lo_part(dve, nl[:, c0:c0 + 2, cols], of[:], nh[:, c0:c0 + 2, cols]).then_inc(s_ol, 1)
                schedule(dve, step_q, step_a, step_b)

            @block.tensor
            def _(pe):
                def step_q(jj, n):
                    i = n % 4
                    pe.wait_ge(s_qb[i], jj * 64 + (n // 4 + 1) * 32)
                    pe.wait_ge(s_qs, at(jj, n, 1, 0))
                    for h in range(4):
                        last = pe.transpose(q_ps[:, h * P:(h + 1) * P], qb[:, i, h].rearrange("p a d -> p (a d)"), ident[:])
                    last.then_inc(s_qtr, 1)

                def step_a(jj, n):
                    i, g, dj = n % 2, (n % 4) // 2, n // 4
                    pe.wait_ge(s_qs, at(jj, n, 1, 1))
                    for h in range(4):
                        pe.wait_ge(s_s, at(jj, n, 4, h - 1))
                        q = qs[i][:, h * P:(h + 1) * P]
                        win = bass.ds(jj * (2 * P) + dj * P, W)
                        ctxk = slice((QB + 2) * P, (QB + 4) * P)
                        pe.matmul(s_ps[h % 2][:, P:P + W], q, kh[:, g, win], start=True, stop=False)
                        pe.matmul(s_ps[h % 2][:, P:P + W], q, kl[:, g, win], start=False, stop=True)
                        pe.matmul(s_ps[h % 2][:, P + W:P + KEYS], q, kh[:, g, ctxk], start=True, stop=False)
                        pe.matmul(s_ps[h % 2][:, P + W:P + KEYS], q, kl[:, g, ctxk], start=False, stop=True).then_inc(s_sc, 1)

                def step_b(jj, n):
                    i, g, par = n % 2, (n % 4) // 2, (n // 4) % 2

                    def values(kb):
                        slot = (n + kb) % 2
                        pe.wait_ge(s_pl, at(jj, n, KB, kb + 1))
                        v = vw[par][:, kb, g, :] if kb < 3 else vs[:, QB + 2 + kb - 3, g, :]
                        pe.matmul(o_ps[:], v, pth[slot][:], start=(kb == 0), stop=False)
                        pe.matmul(o_ps[:], v, ptl[slot][:], start=False, stop=(kb == KB - 1)).then_inc(s_o, 1)
                    pe.wait_ge(s_p, at(jj, n, 4, 4))
                    pe.wait_ge(s_vw, jj * 2 + (n // 4 + 1))
                    for kb in range(KB):
                        slot = (n + kb) % 2
                        pe.wait_ge(s_pl, at(jj, n, KB, kb - 1))
                        for h in range(4):
                            last = pe.transpose(t_ps[slot][:, h * P:(h + 1) * P], sc[:, i, h, kb * P:(kb + 1) * P], ident[:])
                        last.then_inc(s_pt, 1)
                        if kb == 0:
                            pe.wait_ge(s_of, at(jj, n, 1, 0))
                        else:
                            values(kb - 1)
                    values(KB - 1)
                schedule(pe, step_q, step_a, step_b)


def attn_out(nc, sem, sb, banks, wo, park, mod, nh, nl, ht):
    TB = BLOCKS[:2]
    with ExitStack() as ph:
        wf = [sb(f"of{i}", [P, KC, P], where=ph) for i in range(2)]
        wh = [sb(f"owh{i}", [P, KC, P], F32R, where=ph) for i in range(2)]
        wl = [sb(f"owl{i}", [P, KC, P], F32R, where=ph) for i in range(2)]
        o_ps = banks("oo_ps", 4, ph)
        s_h, s_wh, s_wl, s_o, s_add = (sem("w_" + n) for n in ("ht", "wh", "wl", "prod", "add"))
        s_w = [sem(f"w_w{i}") for i in range(2)]
        with nc.Block() as block:
            @block.gpsimd
            def _(pool):
                for s in (s_wl, s_o, s_add):
                    pool.sem_inc(s, PRE)

            @block.sync
            def _(sp):
                with sp.Fori(0, KC // 2) as r:
                    for i in range(2):
                        sp.wait_ge(s_wl, r * 2 + (PRE + i - 1))
                        sp.dma_start(wf[i][:], wo[bass.ds(r * 2 + i, 1)].rearrange("a p k n -> p (a k) n")).then_inc(s_w[i], 16)

            @block.scalar
            def _(act):
                act.dma_start(ht[:], park).then_inc(s_h, 16)
                with act.Fori(0, KC // 2) as r:
                    for i in range(2):
                        act.wait_ge(s_w[i], r * 16 + 16)
                        act.wait_ge(s_o, r * 4 + (PRE + 2 * i - 2))
                        act.activation(wh[i][:], wf[i][:], ACT.Copy).then_inc(s_wh, 1)

            @block.vector
            def _(dve):
                dve.wait_ge(s_h, 16)
                with dve.Fori(0, KC // 2) as r:
                    for i in range(2):
                        dve.wait_ge(s_wh, r * 2 + (i + 1))
                        lo_part(dve, wl[i][:], wf[i][:], wh[i][:]).then_inc(s_wl, 1)
                        for b, (t0, n) in enumerate(TB):
                            h = ht[:, bass.ds(r * 2 + i, 1), t0:t0 + n].rearrange("p a s -> p (a s)")
                            dve.wait_ge(s_o, r * 4 + (PRE + 2 * i + b + 1))
                            dve.scalar_tensor_tensor(out=h, in0=o_ps[2 * i + b][:, 0:n], scalar=mod[:, 1, G1, bass.ds(r * 2 + i, 1), 0],
                                                     in1=h, op0=ALU.mult, op1=ALU.add).then_inc(s_add, 1)

            @block.tensor
            def _(pe):
                with pe.Fori(0, KC // 2) as r:
                    for i in range(2):
                        pe.wait_ge(s_wl, r * 2 + (PRE + i + 1))
                        for b, (t0, n) in enumerate(TB):
                            pe.wait_ge(s_add, r * 4 + (PRE + 2 * i + b - 3))
                            for k in range(KC):
                                last = mm3(pe, o_ps[2 * i + b][:, 0:n], (wh[i][:, k, :], wl[i][:, k, :]),
                                           (nh[:, k, t0:t0 + n], nl[:, k, t0:t0 + n]), k == 0, k == KC - 1)
                            last.then_inc(s_o, 1)


def write_out(nc, sem, sb, banks, ident, ht, out):
    with ExitStack() as ph:
        ob = [sb(f"ob{i}", [P, D], where=ph) for i in range(2)]
        ps = banks("w_ps", 4, ph)
        s_tr, s_a, s_d = sem("z_tr"), sem("z_act"), sem("z_dve")
        s_out = [sem(f"z_out{i}") for i in range(2)]
        with nc.Block() as block:
            @block.sync
            def _(sp):
                for t in range(QB):
                    sp.wait_ge(s_a, t + 1)
                    sp.wait_ge(s_d, t + 1)
                    sp.dma_start(out[t * P:(t + 1) * P, :], ob[t % 2][:]).then_inc(s_out[t % 2], 16)
                for i in range(2):
                    sp.wait_ge(s_out[i], 16 * QB // 2)

            @block.scalar
            def _(act):
                for t in range(QB):
                    if t >= 2:
                        act.wait_ge(s_out[t % 2], 16 * (t // 2))
                    act.wait_ge(s_tr, 2 * t + 1)
                    act.activation(ob[t % 2][:, 0:512], ps[2 * (t % 2)][:], ACT.Copy).then_inc(s_a, 1)

            @block.vector
            def _(dve):
                for t in range(QB):
                    if t >= 2:
                        dve.wait_ge(s_out[t % 2], 16 * (t // 2))
                    dve.wait_ge(s_tr, 2 * t + 2)
                    dve.tensor_copy(ob[t % 2][:, 512:1024], ps[2 * (t % 2) + 1][:]).then_inc(s_d, 1)

            @block.tensor
            def _(pe):
                for t in range(QB):
                    if t >= 2:
                        pe.wait_ge(s_a, t - 1)
                        pe.wait_ge(s_d, t - 1)
                    for half in range(2):
                        for k in range(4):
                            last = pe.transpose(ps[2 * (t % 2) + half][:, k * P:(k + 1) * P],
                                                ht[:, 4 * half + k, t * P:(t + 1) * P], ident[:])
                        last.then_inc(s_tr, 1)


def dft_tables():
    t, s = np.arange(256)[:, None], np.arange(256)[None, :]
    out = []
    for s1 in (0, 2, 1):
        a = 2 * np.pi * (((4 * s + s1) * t) % LAT) / LAT
        out.append(np.concatenate([np.cos(a), np.sin(a)], axis=1))
    c, s_ = out[2][:, :256], out[2][:, 256:]
    out.append(np.concatenate([-s_, c], axis=1))
    return np.stack([o.reshape(2, P, 512).transpose(1, 0, 2) for o in out]).astype(np.float32)


def rope_tables():
    inv = 10000.0 ** (-np.arange(16, dtype=np.float32) / np.float32(16))
    pos = np.arange(LAT)
    ar = (pos // 64).astype(np.float32)[:, None] * inv[None, :]
    ac = (pos % 64).astype(np.float32)[:, None] * inv[None, :]
    cos = np.concatenate([np.cos(ar), np.cos(ar), np.cos(ac), np.cos(ac)], axis=1)
    sin = np.concatenate([-np.sin(ar), np.sin(ar), -np.sin(ac), np.sin(ac)], axis=1)
    cos = np.concatenate([cos, np.ones((CTX, HD))]).reshape(NT, P, HD)
    sin = np.concatenate([sin, np.zeros((CTX, HD))]).reshape(NT, P, HD)
    return np.stack([cos, sin]).transpose(2, 0, 1, 3).astype(np.float32)


def band_masks():
    q, k = np.arange(P)[:, None], np.arange(P)[None, :]
    m = np.stack([np.where(k >= q, 0, BIG), np.where(k <= q, 0, BIG)])
    m = np.repeat(m[None], QB, axis=0)
    m[0, 0] = BIG
    m[QB - 1, 1] = BIG
    return m.transpose(2, 0, 1, 3).astype(np.float32)


def kernel(**inputs):
    import concourse.bacc as bacc
    from concourse.bass_utils import run_bass_kernel_spmd

    a = {k: np.ascontiguousarray(v) for k, v in inputs.items()}

    def columns(v):
        return v.reshape(-1, P).T

    cc = np.stack([columns(a["c"]), columns(a["c_ctx"])], axis=2).reshape(P, 2 * KC)
    vecs = np.concatenate([columns(a["norm1_g"]), columns(a["norm2_g"]), columns(a["ada_b"]), columns(a["fnet_b"]), cc], axis=1)
    negated = (np.arange(D) // GW) * GW + (-np.arange(D)) % GW
    fnet_w = a["fnet_w"][0][negated].reshape(KC, P, KC, P).transpose(2, 1, 0, 3)
    arrays = {
        "x": a["x"][0], "ctx": a["ctx"][0], "vecs": vecs, 
        "ada_w": a["ada_w"].reshape(DEPTH, KC, P, 6 * D // PIECE, PIECE).transpose(0, 3, 2, 1, 4).reshape(-1, P, KC, PIECE),
        "w1": a["mlp_w1"].reshape(DEPTH, KC, P, DFF // (2 * P), 2 * P).transpose(0, 3, 2, 1, 4),
        "w2": a["mlp_w2"].reshape(DEPTH, DFF // P, P, D),
        "fnet_w": fnet_w, "wqkv": a["attn_w_qkv"][0],
        "wo": a["attn_w_o"][0].reshape(KC, P, KC, P).transpose(2, 1, 0, 3),
        "qkg": np.broadcast_to(np.concatenate([a["attn_q_g"][0], a["attn_k_g"][0]]), (P, 2 * HD)),
        "sink": np.broadcast_to(a["attn_sink"][0], (P, HEADS)),
        "dft": dft_tables(), "rope": rope_tables(), "masks": band_masks(), "eye": np.eye(P, dtype=np.float32),
    }
    arrays = {k: np.ascontiguousarray(v) for k, v in arrays.items()}
    nc = bacc.Bacc("TRN2", target_bir_lowering=False, num_devices=1)
    args = [nc.dram_tensor(n, v.shape, mybir.dt.from_np(v.dtype), kind="ExternalInput").ap() for n, v in arrays.items()]
    out = nc.dram_tensor("out", (LAT, D), F32, kind="ExternalOutput").ap()
    park = nc.dram_tensor("park", (P, KC, LAT), F32, kind="Internal").ap()
    qd = nc.dram_tensor("queries", (QB, HEADS // 4, P, 4 * HD), F32, kind="Internal").ap()
    hybrid_kernel(nc, *args, out, park, qd)
    r = run_bass_kernel_spmd(nc, [arrays], core_ids=[0])
    return r.results[0]["out"].reshape(1, LAT, D)
```

```python
import numpy as np
import concourse.bass as bass
from concourse import mybir
from contextlib import ExitStack

F32 = mybir.dt.float32
F32R = mybir.dt.float32r
ALU = mybir.AluOpType
ACT = mybir.ActivationFunctionType
AX = mybir.AxisListType

P = 128
D = 1024
KC = D // P
LAT, CTX = 1024, 256
T = LAT + CTX
NT = T // P
DEPTH = 2
DFF = 4 * D
EPS = 1e-6
HD = 64
HEADS, KVH = 16, 2
QB = LAT // P
KEYS = 3 * P + CTX
GW = 256
BIG = 1e30
PRE = 64
BLOCKS = [(0, 512), (512, 512), (1024, 256)]

V_N1, V_N2, V_ADAB, V_FB, V_C = 0, 16, 32, 128, 136
V_ALL = 152
PIECE = 512
SH1, SC1, G1, SH2, SC2, G2 = range(6)


def f32(ap):
    return ap.bitcast(F32)


def mm3(pe, out, lhs, rhs, first, last):
    (lh, ll), (rh, rl) = lhs, rhs
    pe.matmul(out, lh, rh, start=first, stop=False)
    pe.matmul(out, lh, rl, start=False, stop=False)
    return pe.matmul(out, ll, rh, start=False, stop=last)


def lo_part(eng, lo, full, hi):
    return eng.tensor_tensor(lo, full, f32(hi), ALU.subtract)


def hybrid_kernel(nc, x, ctxt, vecs, ada0, ada1, w1, w2, fnet_w, wqkv, wo, qkg, sink, dft, rope, masks, eye, out, park, qd):
    ctx = ExitStack()
    with ctx:
        held = ExitStack()
        numbers = []

        def sem(name):
            s = held.enter_context(nc.semaphore(name))
            numbers.append(s.num)
            return s

        def recycle_semaphores():
            with nc.Block() as block:
                @block.gpsimd
                def _(pool):
                    pool.sem_clear(range(min(numbers), max(numbers) + 1))
            held.close()
            numbers.clear()

        def sb(name, shape, dt=F32, where=ctx):
            return where.enter_context(nc.sbuf_tensor(name, shape, dt))

        def banks(name, n, where):
            return [where.enter_context(nc.psum_tensor(f"{name}{i}", [P, 512], F32)) for i in range(n)]

        vec = sb("vec", [P, V_ALL])
        mod = sb("mod", [P, DEPTH, 6, KC, 2])
        g1b = sb("g1b", [P, KC, 2])
        svec = sb("svec", [P, KC, 2])
        ident = sb("ident", [P, P])
        meanw = sb("meanw", [P, P])
        eps = sb("eps", [P, 1])
        ones = sb("ones", [P, 1])
        rstd_tm = sb("rstd_tm", [P, NT])

        def shift(l, n, k, v):
            return mod[:, l, (SH1, SH2)[n], k, v:v + 1]

        def scale(l, n, k, v):
            return mod[:, l, (SC1, SC2)[n], k, v:v + 1]

        RING = 4
        PIECES = 6 * D // PIECE
        M = PIECE // P
        with ExitStack() as ph:
            wbuf = [sb(f"ada_w{i}", [P, KC, PIECE], where=ph) for i in range(RING)]
            rows = [sb(f"ada_row{i}", [2, PIECE], where=ph) for i in range(2)]
            xt = [sb(f"xt{i}", [P, D], where=ph) for i in range(2)]
            xsq = sb("xsq", [P, D], where=ph)
            sig = sb("sig", [P, KC, 2], where=ph)
            ssq = sb("ssq", [P, NT], where=ph)
            row_ps, col_ps = banks("ada_ps", 2, ph), banks("adac_ps", 1, ph)[0]
            s_small, s_eps, s_e, s_d, s_silu = sem("a_small"), sem("a_eps"), sem("a_exp"), sem("a_d"), sem("a_silu")
            s_w = [sem(f"a_w{i}") for i in range(RING)]
            s_x = [sem(f"a_x{i}") for i in range(2)]
            s_id, s_row, s_ev, s_col, s_ssq, s_std = sem("a_id"), sem("a_row"), sem("a_ev"), sem("a_col"), sem("a_ssq"), sem("a_std")
            with nc.Block() as block:
                @block.sync
                def _(sp):
                    sp.dma_start(vec[:], vecs).then_inc(s_small, 16)
                    for i in range(PIECES):
                        if i >= RING:
                            sp.wait_ge(s_row, i + 1 - RING)
                        sp.dma_start(wbuf[i % RING][:], ada0[i]).then_inc(s_w[i % RING], 16)
                        if i == 0:
                            sp.dma_start(ident[:], eye).then_inc(s_id, 16)

                @block.gpsimd
                def _(pool):
                    pool.memset(eps[:], EPS).then_inc(s_eps, 1)
                    pool.memset(meanw[:], 1.0 / D).then_inc(s_eps, 1)
                    pool.memset(ones[:], 1.0).then_inc(s_eps, 1)

                @block.scalar
                def _(act):
                    act.wait_ge(s_small, 16)
                    act.activation(sig[:], vec[:, V_C:V_C + 2 * KC], ACT.Exp, scale=-1.0).then_inc(s_e, 1)
                    act.dma_start(xt[0][:], x[0:P, :]).then_inc(s_x[0], 16)
                    act.dma_start(xt[1][:], x[P:2 * P, :]).then_inc(s_x[1], 16)
                    for t in range(NT):
                        act.wait_ge(s_x[t % 2], 16 * (t // 2 + 1))
                        if t:
                            act.wait_ge(s_ssq, t)
                        act.activation(xsq[:], xt[t % 2][:], ACT.Square, accum_out=ssq[:, t:t + 1]).then_inc(s_ssq, 1)
                        if t + 2 < NT:
                            act.wait_ge(s_ssq, t + 1)
                            src = x[(t + 2) * P:(t + 3) * P, :] if t + 2 < QB else ctxt[(t + 2 - QB) * P:(t + 3 - QB) * P, :]
                            act.dma_start(xt[t % 2][:], src).then_inc(s_x[t % 2], 16)
                    act.wait_ge(s_eps, 3)
                    act.wait_ge(s_ssq, NT)
                    act.activation(ssq[:], ssq[:], ACT.Sqrt, bias=eps[:], scale=1.0 / D).then_inc(s_std, 1)

                @block.vector
                def _(dve):
                    dve.wait_ge(s_e, 1)
                    dve.tensor_scalar_add(sig[:], sig[:], 1.0).then_inc(s_d, 1)
                    dve.wait_ge(s_d, 1)
                    dve.reciprocal(sig[:], sig[:]).then_inc(s_d, 1)
                    dve.wait_ge(s_d, 2)
                    dve.tensor_tensor(svec[:], sig[:], vec[:, V_C:V_C + 2 * KC].rearrange("p (k v) -> p k v", v=2),
                                      ALU.mult).then_inc(s_silu, 1)
                    for i in range(PIECES):
                        dve.wait_ge(s_row, i + 1)
                        if i >= 2:
                            dve.wait_ge(s_col, i - 1)
                        dve.tensor_copy(rows[i % 2][:], row_ps[i % 2][0:2, :]).then_inc(s_ev, 1)
                    dve.wait_ge(s_std, 1)
                    dve.reciprocal(rstd_tm[:], ssq[:]).then_inc(s_d, 1)
                    dve.wait_ge(s_col, PIECES)
                    bias = vec[:, V_ADAB:V_ADAB + 6 * KC].rearrange("p (m v) -> p m v", v=1)
                    dve.tensor_tensor(mod[:, 0].rearrange("p s k v -> p (s k) v"),
                                      col_ps[:, 0:12 * KC].rearrange("p (m v) -> p m v", v=2),
                                      bias.to_broadcast([P, 6 * KC, 2]), ALU.add).then_inc(s_d, 1)
                    dve.wait_ge(s_d, 4)
                    for which, col in ((SC1, V_N1), (SC2, V_N2)):
                        for v in range(2):
                            m = mod[:, 0, which, :, v]
                            dve.scalar_tensor_tensor(out=m, in0=m, scalar=1.0, in1=vec[:, col:col + KC],
                                                     op0=ALU.add, op1=ALU.mult).then_inc(s_d, 1)
                    for v in range(2):
                        dve.tensor_tensor(g1b[:, :, v], mod[:, 0, G1, :, v], vec[:, V_FB:V_FB + KC], ALU.mult).then_inc(s_d, 1)

                @block.tensor
                def _(pe):
                    pe.wait_ge(s_silu, 1)

                    def columns(i):
                        pe.wait_ge(s_ev, i + 1)
                        for m in range(M):
                            c = 2 * (i * M + m)
                            last = pe.transpose(col_ps[:, c:c + 2], rows[i % 2][:, m * P:(m + 1) * P], ident[0:2, 0:2])
                        last.then_inc(s_col, 1)
                    for i in range(PIECES):
                        pe.wait_ge(s_w[i % RING], 16 * (i // RING + 1))
                        if i >= 2:
                            pe.wait_ge(s_ev, i - 1)
                        for k in range(KC):
                            last = pe.matmul(row_ps[i % 2][0:2, :], svec[:, k, :], wbuf[i % RING][:, k, :],
                                             start=(k == 0), stop=(k == KC - 1))
                        last.then_inc(s_row, 1)
                        if i == 0:
                            pe.wait_ge(s_id, 16)
                        else:
                            columns(i - 1)
                    columns(PIECES - 1)

        nh = sb("nh", [P, KC, T], F32R)
        nl = sb("nl", [P, KC, T], F32R)

        fnet_mix(nc, sem, sb, banks, x, ctxt, dft, rstd_tm, mod, nh, nl)
        with ExitStack() as layer0:
            ht = sb("ht0", [P, KC, T], where=layer0)
            fnet_out(nc, sem, sb, banks, x, ctxt, fnet_w, ada1, vec, svec, ones, mod, g1b, ident, nh, nl, ht)
            mlp(nc, sem, sb, banks, 0, 3, w1, w2, mod, meanw, eps, nh, nl, ht)
            norm_out(nc, sem, sb, banks, 1, park, mod, meanw, eps, nh, nl, ht)
        recycle_semaphores()
        with ExitStack() as att:
            kh = sb("kh", [P, KVH, (QB + 4) * P], F32R, where=att)
            kl = sb("kl", [P, KVH, (QB + 4) * P], F32R, where=att)
            vs = sb("vs", [P, QB + 4, KVH, 2 * HD], F32R, where=att)
            qkv(nc, sem, sb, banks, wqkv, qkg, rope, ident, eps, nh, nl, qd, kh, kl, vs)
            attention(nc, sem, sb, banks, masks, sink, ident, qd, kh, kl, vs, nh, nl)
        ht = sb("ht1", [P, KC, LAT])
        attn_out(nc, sem, sb, banks, wo, park, mod, nh, nl, ht)
        mlp(nc, sem, sb, banks, 1, 2, w1, w2, mod, meanw, eps, nh, nl, ht)
        write_out(nc, sem, sb, banks, ident, ht, out)


def fnet_mix(nc, sem, sb, banks, x, ctxt, dft, rstd_tm, mod, nh, nl):
    GR = D // GW
    SETS = [([(0, 0)], 0, 0, 0), ([(1, 2)], 0, 256, 0), ([(2, 4), (3, 6)], 1, 0, 0), ([(0, 8)], 1, 256, 1)]
    FIXED = {0: 0, 3: 1}
    with ExitStack() as ph:
        tabf = sb("tabf", [P, 2, 512], where=ph)
        tabh = sb("tabh", [P, 4, 2, 512], F32R, where=ph)
        tabl = sb("tabl", [P, 4, 2, 512], F32R, where=ph)
        xg = [sb(f"xg{i}", [P, NT, P], where=ph) for i in range(2)]
        xr = sb("xr", [P, NT * P], where=ph)
        sd = sb("sd", [P, 512], where=ph)
        gh = [sb(f"gh{i}", [P, NT, P], F32R, where=ph) for i in range(2)]
        gl = [sb(f"gl{i}", [P, NT, P], F32R, where=ph) for i in range(2)]
        uvh = sb("uvh", [P, 2, 2, 2, 512], F32R, where=ph)
        uvl = sb("uvl", [P, 2, 2, 2, 512], F32R, where=ph)
        uvf = [sb(f"uvf{i}", [P, 2, 256], where=ph) for i in range(2)]
        sdc = sb("sdc", [P, KC, 2], where=ph)
        gain = sb("gain", [P, 2, 2], where=ph)
        yt = sb("yt", [P, 512], where=ph)
        bt = sb("bt", [P, 256], where=ph)
        seq_ps, y_ps = banks("seq_ps", 4, ph), banks("y_ps", 3, ph)
        s_tab, s_th, s_tl, s_c, s_gain = sem("m_tab"), sem("m_tabh"), sem("m_tabl"), sem("m_sdc"), sem("m_gain")
        s_x = [sem(f"m_x{i}") for i in range(2)]
        s_xr, s_bf, s_g, s_gh, s_gl = sem("m_xr"), sem("m_butterfly"), sem("m_g"), sem("m_gh"), sem("m_gl")
        s_seq, s_uvf, s_fix, s_uvh, s_uvl = sem("m_seq"), sem("m_uvf"), sem("m_fix"), sem("m_uvh"), sem("m_uvl")
        s_y, s_bt, s_yt, s_yh, s_yl = sem("m_y"), sem("m_bt"), sem("m_yt"), sem("m_yh"), sem("m_yl")
        xv = x.rearrange("(n p) d -> p n d", p=P)
        cv = ctxt.rearrange("(n p) d -> p n d", p=P)
        with nc.Block() as block:
            @block.gpsimd
            def _(pool):
                for s in (s_xr, s_gl, s_seq, s_uvf, s_uvl, s_y, s_yt, s_yl):
                    pool.sem_inc(s, PRE)

            @block.sync
            def _(sp):
                for i in range(4):
                    if i:
                        sp.wait_ge(s_tl, i)
                    sp.dma_start(tabf[:], dft[i]).then_inc(s_tab, 16)
                with sp.Fori(0, GR) as g:
                    for i in range(2):
                        sp.wait_ge(s_xr, g * 2 + (PRE + i - 1))
                        col = bass.ds(g * GW + i * P, P)
                        sp.dma_start(xg[i][:, 0:QB, :], xv[:, :, col]).then_inc(s_x[i], 16)
                        sp.dma_start(xg[i][:, QB:NT, :], cv[:, :, col]).then_inc(s_x[i], 16)

            @block.scalar
            def _(act):
                for i in range(4):
                    act.wait_ge(s_tab, 16 * (i + 1))
                    act.activation(tabh[:, i], tabf[:], ACT.Copy).then_inc(s_th, 1)
                for v, n in ((0, LAT), (1, CTX)):
                    act.activation(sdc[:, :, v], mod[:, 0, SH1, :, v], ACT.Copy, scale=float(n)).then_inc(s_c, 1)
                with act.Fori(0, GR) as g:
                    act.wait_ge(s_gain, g + 1)
                    for i in range(2):
                        act.wait_ge(s_g, g * 2 + (i + 1))
                        act.wait_ge(s_seq, g * 8 + (PRE + 4 * i - 4))
                        act.activation(gh[i][:].rearrange("p n c -> p (n c)"), xr[:], ACT.Copy).then_inc(s_gh, 1)
                        if i == 0:
                            act.wait_ge(s_y, g * 6 + PRE)
                        for j, (_, b, off, v) in enumerate(SETS):
                            u = i * 4 + j
                            act.wait_ge(s_seq, g * 8 + (PRE + u + 1))
                            act.wait_ge(s_uvl, g * 8 + (PRE + u - 1))
                            act.activation(uvf[u % 2][:].rearrange("p a s -> p (a s)"), seq_ps[j][:], ACT.Copy,
                                           scale=gain[:, i, v:v + 1]).then_inc(s_uvf, 1)
                            if j in FIXED:
                                act.wait_ge(s_fix, g * 4 + (i * 2 + v + 1))
                            else:
                                act.wait_ge(s_uvf, g * 8 + (PRE + u + 1))
                            act.activation(uvh[:, b, i, :, off:off + 256], uvf[u % 2][:], ACT.Copy).then_inc(s_uvh, 1)
                    for m in range(2):
                        chunk = nh[:, bass.ds(g * 2 + m, 1), :].rearrange("p a s -> p (a s)")
                        dst = chunk[:, 0:LAT].rearrange("p (s f) -> p f s", f=4)
                        act.wait_ge(s_y, g * 6 + (PRE + 3 * m + 1))
                        act.activation(dst[:, 0::2, :], y_ps[0][:].rearrange("p (a s) -> p a s", a=2), ACT.Copy,
                                       scale=2.0 ** -9).then_inc(s_yh, 1)
                        act.wait_ge(s_y, g * 6 + (PRE + 3 * m + 2))
                        act.wait_ge(s_yt, g * 2 + (PRE + m))
                        act.activation(bt[:], y_ps[1][:, 256:512], ACT.Copy).then_inc(s_bt, 1)
                        act.wait_ge(s_yt, g * 2 + (PRE + m + 1))
                        act.activation(dst[:, 1, :], yt[:, 0:256], ACT.Copy, scale=2.0 ** -9)
                        act.activation(dst[:, 3, :], yt[:, 256:512], ACT.Copy, scale=2.0 ** -9).then_inc(s_yh, 1)
                        act.wait_ge(s_y, g * 6 + (PRE + 3 * m + 3))
                        act.activation(chunk[:, LAT:T], y_ps[2][:, 0:256], ACT.Copy, scale=2.0 ** -8).then_inc(s_yh, 1)

            @block.vector
            def _(dve):
                for i in range(4):
                    dve.wait_ge(s_th, i + 1)
                    lo_part(dve, tabl[:, i], tabf[:], tabh[:, i]).then_inc(s_tl, 1)
                dve.wait_ge(s_c, 2)
                with dve.Fori(0, GR) as g:
                    dve.wait_ge(s_uvf, g * 8 + PRE)
                    dve.tensor_copy(gain[:], mod[:, 0, SC1, bass.ds(g * 2, 2), :]).then_inc(s_gain, 1)
                    for i in range(2):
                        dve.wait_ge(s_x[i], g * 32 + 32)
                        dve.wait_ge(s_gl, g * 2 + (PRE + i))
                        dve.tensor_tensor(xr[:].rearrange("p (n c) -> p n c", n=NT), xg[i][:],
                                          rstd_tm[:].rearrange("p (n c) -> p n c", c=1).to_broadcast([P, NT, P]),
                                          ALU.mult).then_inc(s_xr, 1)
                        dve.wait_ge(s_xr, g * 2 + (PRE + i + 1))
                        dve.tensor_tensor(sd[:], xr[:, 0:512], xr[:, 512:1024], ALU.add)
                        dve.tensor_tensor(xr[:, 512:1024], xr[:, 0:512], xr[:, 512:1024], ALU.subtract).then_inc(s_bf, 1)
                        dve.wait_ge(s_bf, g * 2 + (i + 1))
                        dve.tensor_tensor(xr[:, 0:256], sd[:, 0:256], sd[:, 256:512], ALU.add)
                        dve.tensor_tensor(xr[:, 256:512], sd[:, 0:256], sd[:, 256:512], ALU.subtract).then_inc(s_g, 1)
                        dve.wait_ge(s_gh, g * 2 + (i + 1))
                        lo_part(dve, gl[i][:].rearrange("p n c -> p (n c)"), xr[:],
                                gh[i][:].rearrange("p n c -> p (n c)")).then_inc(s_gl, 1)
                        for j, (_, b, off, v) in enumerate(SETS):
                            u = i * 4 + j
                            dve.wait_ge(s_uvf, g * 8 + (PRE + u + 1))
                            if j in FIXED:
                                c0 = uvf[u % 2][:, 0, 0:1]
                                dve.tensor_tensor(c0, c0, sdc[:, bass.ds(g * 2 + i, 1), v], ALU.add).then_inc(s_fix, 1)
                            dve.wait_ge(s_uvh, g * 8 + (u + 1))
                            lo_part(dve, uvl[:, b, i, :, off:off + 256], uvf[u % 2][:],
                                    uvh[:, b, i, :, off:off + 256]).then_inc(s_uvl, 1)
                    for m in range(2):
                        lo = nl[:, bass.ds(g * 2 + m, 1), :].rearrange("p a s -> p (a s)")
                        hi = f32(nh[:, bass.ds(g * 2 + m, 1), :]).rearrange("p a s -> p (a s)")
                        dlo, dhi = (a[:, 0:LAT].rearrange("p (s f) -> p f s", f=4) for a in (lo, hi))
                        dve.wait_ge(s_yh, g * 6 + (3 * m + 1))
                        dve.scalar_tensor_tensor(out=dlo[:, 0::2, :], in0=y_ps[0][:].rearrange("p (a s) -> p a s", a=2),
                                                 scalar=2.0 ** -9, in1=dhi[:, 0::2, :],
                                                 op0=ALU.mult, op1=ALU.subtract).then_inc(s_yl, 1)
                        dve.wait_ge(s_bt, g * 2 + (m + 1))
                        dve.wait_ge(s_yl, g * 6 + (PRE + 3 * m - 1))
                        dve.tensor_tensor(yt[:, 0:256], y_ps[1][:, 0:256], bt[:], ALU.add)
                        dve.tensor_tensor(yt[:, 256:512][:, ::-1], y_ps[1][:, 0:256], bt[:], ALU.subtract).then_inc(s_yt, 1)
                        dve.wait_ge(s_yh, g * 6 + (3 * m + 2))
                        dve.scalar_tensor_tensor(out=dlo[:, 1, :], in0=yt[:, 0:256], scalar=2.0 ** -9, in1=dhi[:, 1, :],
                                                 op0=ALU.mult, op1=ALU.subtract)
                        dve.scalar_tensor_tensor(out=dlo[:, 3, :], in0=yt[:, 256:512], scalar=2.0 ** -9,
                                                 in1=dhi[:, 3, :], op0=ALU.mult, op1=ALU.subtract).then_inc(s_yl, 1)
                        dve.wait_ge(s_yh, g * 6 + (3 * m + 3))
                        dve.scalar_tensor_tensor(out=lo[:, LAT:T], in0=y_ps[2][:, 0:256], scalar=2.0 ** -8,
                                                 in1=hi[:, LAT:T], op0=ALU.mult, op1=ALU.subtract).then_inc(s_yl, 1)

            @block.tensor
            def _(pe):
                pe.wait_ge(s_tl, 4)
                with pe.Fori(0, GR) as g:
                    for i in range(2):
                        pe.wait_ge(s_gl, g * 2 + (PRE + i + 1))
                        for j, (prods, b, off, v) in enumerate(SETS):
                            pe.wait_ge(s_uvf, g * 8 + (PRE + 4 * i + j - 3))
                            terms = [(tab, tile, kt) for tab, tile in prods for kt in range(2)]
                            for n, (tab, tile, kt) in enumerate(terms):
                                last = mm3(pe, seq_ps[j][:], (gh[i][:, tile + kt, :], gl[i][:, tile + kt, :]),
                                           (tabh[:, tab, kt, :], tabl[:, tab, kt, :]), n == 0, n == len(terms) - 1)
                            last.then_inc(s_seq, 1)
                    pe.wait_ge(s_uvl, g * 8 + (PRE + 8))
                    TERMS = [(cs, kt) for cs in range(2) for kt in range(2)]
                    for m in range(2):
                        def tab(cs, kt):
                            cols = slice(256 * cs + m * P, 256 * cs + (m + 1) * P)
                            return tabh[:, 0, kt, cols], tabl[:, 0, kt, cols]

                        def uv(b, kt, cs, lo, hi):
                            return uvh[:, b, kt, cs, lo:hi], uvl[:, b, kt, cs, lo:hi]
                        pe.wait_ge(s_yl, g * 6 + (PRE + 3 * m - 2))
                        for n, (cs, kt) in enumerate(TERMS):
                            last = mm3(pe, y_ps[0][:], tab(cs, kt), uv(0, kt, cs, 0, 512), n == 0, n == 3)
                        last.then_inc(s_y, 1)
                        pe.wait_ge(s_yt, g * 2 + (PRE + m))
                        for cs, kt in TERMS:
                            last = mm3(pe, y_ps[1][:, 256 * cs:256 * cs + 256], tab(cs, kt), uv(1, kt, cs, 0, 256),
                                       kt == 0, kt == 1)
                        last.then_inc(s_y, 1)
                        pe.wait_ge(s_yl, g * 6 + (PRE + 3 * m))
                        for n, (cs, kt) in enumerate(TERMS):
                            last = mm3(pe, y_ps[2][:, 0:256], tab(cs, kt), uv(1, kt, cs, 256, 512), n == 0, n == 3)
                        last.then_inc(s_y, 1)


def fnet_out(nc, sem, sb, banks, x, ctxt, fnet_w, ada1, vec, svec, ones, mod, g1b, ident, nh, nl, ht):
    UNITS, SLOTS, UW = 6, 3, 4 * PIECE
    M = PIECE // P
    STEPS = [(u, kk, c) for u in range(UNITS) for kk in range(4 if u < 2 else 2) for c in range(2)]
    NS = len(STEPS)
    STEPS_TO = [sum(1 for s in STEPS if s[0] <= u) for u in range(UNITS)]
    with ExitStack() as ph:
        wf = [sb(f"fw{i}", [P, KC, P], where=ph) for i in range(2)]
        wh = [sb(f"fwh{i}", [P, KC, P], F32R, where=ph) for i in range(2)]
        wl = [sb(f"fwl{i}", [P, KC, P], F32R, where=ph) for i in range(2)]
        yb = [sb(f"fy{i}", [P, 512], where=ph) for i in range(3)]
        gate, bias = sb("gate", [P, 2, 2], where=ph), sb("gbias", [P, 2, 2], where=ph)
        aw = [sb(f"aw{i}", [P, UW], where=ph) for i in range(SLOTS)]
        XS = SLOTS * UW // D
        xt = [aw[i * D // UW][:, i * D % UW:i * D % UW + D] for i in range(XS)]
        acc = sb("ada_acc", [P, 2, 2, PIECE], where=ph)
        tr_ps, o_ps = banks("tr_ps", 4, ph), banks("o_ps", 3, ph)
        ada_ps = banks("ada1_ps", 1, ph)[0]
        s_aw = [sem(f"o_aw{i}") for i in range(SLOTS)]
        s_st, s_red, s_m = sem("o_ada_step"), sem("o_ada_reduced"), sem("o_ada_mod")
        s_gate = sem("o_gate")
        s_x = [sem(f"o_x{i}") for i in range(XS)]
        s_w = [sem(f"o_w{i}") for i in range(2)]
        s_wh, s_wl, s_tr, s_eva, s_evd, s_o, s_yb, s_add = (sem(n) for n in (
            "o_wh", "o_wl", "o_tr", "o_ev_act", "o_ev_dve", "o_prod", "o_yb", "o_add"))
        with nc.Block() as block:
            @block.gpsimd
            def _(pool):
                for s in (s_wl, s_o, s_yb, s_add, s_st, s_red):
                    pool.sem_inc(s, PRE)
                pool.wait_ge(s_tr, 2 * NT)
                with pool.Fori(0, KC // 2) as r:
                    for u in range(UNITS):
                        pool.wait_ge(s_st, r * NS + (PRE + (STEPS_TO[u - SLOTS] if u >= SLOTS else STEPS_TO[u + UNITS - SLOTS] - NS)))
                        pool.dma_start(aw[u % SLOTS][:], ada1[bass.ds(r, 1), u].rearrange("a p n -> p (a n)")).then_inc(s_aw[u % SLOTS], 16)

            @block.sync
            def _(sp):
                def weights(c, i):
                    sp.dma_start(wf[i][:], fnet_w[c].rearrange("a p k n -> p (a k) n")).then_inc(s_w[i], 16)
                for t in range(NT):
                    if t >= XS:
                        sp.wait_ge(s_tr, 2 * (t - XS + 1))
                    src = x[t * P:(t + 1) * P, :] if t < QB else ctxt[(t - QB) * P:(t - QB + 1) * P, :]
                    sp.dma_start(xt[t % XS], src).then_inc(s_x[t % XS], 16)
                    if t == XS - 1:
                        weights(slice(0, 1), 0)
                        weights(slice(1, 2), 1)
                with sp.Fori(1, KC // 2) as r:
                    for i in range(2):
                        sp.wait_ge(s_wl, r * 2 + (PRE + i - 1))
                        weights(bass.ds(r * 2 + i, 1), i)

            @block.scalar
            def _(act):
                for t in range(NT):
                    act.wait_ge(s_tr, 2 * t + 1)
                    act.activation(ht[:, 0:4, t * P:(t + 1) * P], tr_ps[2 * (t % 2)][:].rearrange("p (k c) -> p k c", k=4),
                                   ACT.Copy).then_inc(s_eva, 1)

                def high(r, i):
                    act.wait_ge(s_w[i % 2], r * 16 + 16 * (i // 2 + 1))
                    act.wait_ge(s_o, r * 6 + (PRE + 3 * i - 3))
                    act.activation(wh[i % 2][:], wf[i % 2][:], ACT.Copy).then_inc(s_wh, 1)

                def pair(r, more):
                    act.wait_ge(s_gate, r + 1)
                    for i in range(2):
                        for b, (t0, n) in enumerate(BLOCKS):
                            act.wait_ge(s_o, r * 6 + (PRE + 3 * i + b + 1))
                            act.wait_ge(s_add, r * 6 + (PRE + 3 * i + b - 2))
                            v = int(t0 >= LAT)
                            act.activation(yb[b][:, 0:n], o_ps[b][:, 0:n], ACT.Identity, scale=gate[:, i, v:v + 1],
                                           bias=bias[:, i, v:v + 1]).then_inc(s_yb, 1)
                            if b == 0 and (more or i == 0):
                                high(r, i + 1)
                high(0, 0)
                with act.Fori(0, KC // 2 - 1) as r:
                    pair(r, True)
                pair(KC // 2 - 1, False)

            @block.vector
            def _(dve):
                for t in range(NT):
                    dve.wait_ge(s_tr, 2 * t + 2)
                    dve.tensor_copy(ht[:, 4:8, t * P:(t + 1) * P],
                                    tr_ps[2 * (t % 2) + 1][:].rearrange("p (k c) -> p k c", k=4)).then_inc(s_evd, 1)
                dve.wait_ge(s_evd, NT)
                dve.wait_ge(s_eva, NT)

                def ada_steps(r, i0, i1):
                    for i in range(i0, i1):
                        u, kk, c = STEPS[i]
                        grp = int(u >= 2)
                        k = 4 * u + kk if u < 2 else 2 * (u - 2) + kk
                        w = aw[u % SLOTS][:, kk * PIECE:(kk + 1) * PIECE] if grp == 0 else \
                            aw[u % SLOTS][:, (2 * kk + c) * PIECE:(2 * kk + c + 1) * PIECE]
                        s = svec[:, k, 0:1] if grp else svec[:, k, c:c + 1]
                        if kk == 0 and c == 0:
                            dve.wait_ge(s_aw[u % SLOTS], r * (16 * UNITS // SLOTS) + 16 * (u // SLOTS + 1))
                        if k == 0:
                            dve.wait_ge(s_red, r * 2 + (PRE + grp - 1))
                            dve.tensor_scalar_mul(acc[:, grp, c], w, s).then_inc(s_st, 1)
                        else:
                            dve.wait_ge(s_st, r * NS + (PRE + i - 1))
                            dve.scalar_tensor_tensor(out=acc[:, grp, c], in0=w, scalar=s, in1=acc[:, grp, c],
                                                     op0=ALU.mult, op1=ALU.add).then_inc(s_st, 1)

                def low(r, i):
                    dve.wait_ge(s_wh, r * 2 + (i + 1))
                    lo_part(dve, wl[i % 2][:], wf[i % 2][:], wh[i % 2][:]).then_inc(s_wl, 1)

                def pair(r, more):
                    dve.wait_ge(s_yb, r * 6 + PRE)
                    dve.tensor_copy(gate[:], mod[:, 0, G1, bass.ds(r * 2, 2), :])
                    dve.tensor_copy(bias[:], g1b[:, bass.ds(r * 2, 2), :]).then_inc(s_gate, 1)
                    for i in range(2):
                        ada_steps(r, i * NS // 2, i * NS // 2 + NS // 4)
                        for b, (t0, n) in enumerate(BLOCKS):
                            dve.wait_ge(s_yb, r * 6 + (PRE + 3 * i + b + 1))
                            h = ht[:, bass.ds(r * 2 + i, 1), t0:t0 + n].rearrange("p a s -> p (a s)")
                            dve.tensor_tensor(h, h, yb[b][:, 0:n], ALU.add).then_inc(s_add, 1)
                            if b == 0:
                                if more or i == 0:
                                    low(r, i + 1)
                                ada_steps(r, i * NS // 2 + NS // 4, (i + 1) * NS // 2)
                low(0, 0)
                with dve.Fori(0, KC // 2 - 1) as r:
                    pair(r, True)
                pair(KC // 2 - 1, False)
                dve.wait_ge(s_red, PRE + 2 * (KC // 2))
                ada_b = vec[:, V_ADAB + 6 * KC:V_ADAB + 12 * KC]
                both = 2 * KC
                dve.tensor_tensor(mod[:, 1, 0:2].rearrange("p s k v -> p (s k) v"),
                                  ada_ps[:, 0:2 * both].rearrange("p (m v) -> p m v", v=2),
                                  ada_b[:, 0:both].rearrange("p (m v) -> p m v", v=1).to_broadcast([P, both, 2]), ALU.add).then_inc(s_m, 1)
                dve.tensor_tensor(mod[:, 1, 2:6, :, 0].rearrange("p s k -> p (s k)"), ada_ps[:, 2 * both:2 * both + 4 * KC],
                                  ada_b[:, both:], ALU.add).then_inc(s_m, 1)
                dve.wait_ge(s_m, 2)
                for which, col, v in ((SC1, V_N1, 0), (SC1, V_N1, 1), (SC2, V_N2, 0)):
                    m = mod[:, 1, which, :, v]
                    dve.scalar_tensor_tensor(out=m, in0=m, scalar=1.0, in1=vec[:, col + KC:col + 2 * KC],
                                             op0=ALU.add, op1=ALU.mult).then_inc(s_m, 1)

            @block.tensor
            def _(pe):
                for t in range(NT):
                    pe.wait_ge(s_x[t % XS], 16 * (t // XS + 1))
                    if t >= 2:
                        pe.wait_ge(s_eva, t - 1)
                        pe.wait_ge(s_evd, t - 1)
                    for half in range(2):
                        for k in range(4):
                            kk = 4 * half + k
                            last = pe.transpose(tr_ps[2 * (t % 2) + half][:, k * P:(k + 1) * P],
                                                xt[t % XS][:, kk * P:(kk + 1) * P], ident[:])
                        last.then_inc(s_tr, 1)
                with pe.Fori(0, KC // 2) as r:
                    for i in range(2):
                        pe.wait_ge(s_wl, r * 2 + (PRE + i + 1))
                        for b, (t0, n) in enumerate(BLOCKS):
                            pe.wait_ge(s_yb, r * 6 + (PRE + 3 * i + b - 2))
                            for k in range(KC):
                                last = mm3(pe, o_ps[b][:, 0:n], (wh[i][:, k, :], wl[i][:, k, :]),
                                           (nh[:, k, t0:t0 + n], nl[:, k, t0:t0 + n]), k == 0, k == KC - 1)
                            last.then_inc(s_o, 1)
                        pe.wait_ge(s_st, r * NS + (PRE + (i + 1) * NS // 2))
                        for m in range(M):
                            for c in range(2):
                                if i == 0:
                                    col = ada_ps[:, bass.ds(r * (2 * M) + (2 * m + c), 1)]
                                else:
                                    col = ada_ps[:, bass.ds(r * (2 * M) + (4 * KC + c * M + m), 1)]
                                last = pe.matmul(col, acc[:, i, c, m * P:(m + 1) * P], ones[:], start=True, stop=True)
                        last.then_inc(s_red, 1)


def mlp(nc, sem, sb, banks, layer, nblocks, w1, w2, mod, meanw, eps, nh, nl, ht):
    PAIRS = DFF // (2 * P)
    TB = BLOCKS[:nblocks]
    NB = nblocks
    N = f"l{layer}_"
    U1, U2 = 2 * NB, KC * NB
    with ExitStack() as ph:
        ah = sb(N + "ah", [P, 2, T], F32R, where=ph)
        al = sb(N + "al", [P, 2, T], F32R, where=ph)
        w1f, w2f = sb(N + "w1f", [P, KC, 2 * P], where=ph), sb(N + "w2f", [P, 2, D], where=ph)
        w1h, w2h = sb(N + "w1h", [P, KC, 2 * P], F32R, where=ph), sb(N + "w2h", [P, 2, D], F32R, where=ph)
        w1l, w2l = sb(N + "w1l", [P, KC, 2 * P], F32R, where=ph), sb(N + "w2l", [P, 2, D], F32R, where=ph)
        rel = [sb(f"{N}rel{i}", [P, 512], where=ph) for i in range(2)]
        sq = [sb(f"{N}sq{i}", [P, 512], where=ph) for i in range(2)]
        rb = sb(N + "rb", [P, 512], where=ph)
        z_ps, y_ps = banks(N + "z_ps", 2, ph), banks(N + "yy_ps", 4, ph)
        ms_ps = banks(N + "ms_ps", 2, ph)
        s_w1, s_w2 = sem(N + "w1"), sem(N + "w2")
        s_sq, s_ms, s_std, s_rb, s_t, s_n, s_nh, s_nl = (sem(N + n) for n in ("nsq", "nms", "nstd", "nrb", "nt", "nn", "nnh", "nnl"))
        s_w1h, s_w1l, s_w2h, s_w2l = (sem(N + n) for n in ("w1h", "w1l", "w2h", "w2l"))
        s_z, s_rel, s_ah, s_al, s_sqr, s_y, s_acc = (sem(N + n) for n in ("z", "rel", "ah", "al", "sqr", "y", "acc"))
        with nc.Block() as block:
            @block.sync
            def _(sp):
                with sp.Fori(0, PAIRS) as p:
                    sp.wait_ge(s_w1l, p + PRE)
                    sp.dma_start(w1f[:], w1[layer, bass.ds(p, 1)].rearrange("a p k n -> p (a k) n")).then_inc(s_w1, 16)
                    sp.wait_ge(s_w2l, p + PRE)
                    sp.dma_start(w2f[:], w2[layer, bass.ds(p * 2, 2)].rearrange("c p n -> p c n")).then_inc(s_w2, 16)

            @block.gpsimd
            def _(pool):
                for s in (s_w1l, s_w2l, s_z, s_rel, s_al, s_y, s_acc):
                    pool.sem_inc(s, PRE)
                with pool.Fori(0, PAIRS) as p:
                    pool.wait_ge(s_w1h, p + 1)
                    lo_part(pool, w1l[:], w1f[:], w1h[:]).then_inc(s_w1l, 1)
                    pool.wait_ge(s_w2h, p + 1)
                    lo_part(pool, w2l[:], w2f[:], w2h[:]).then_inc(s_w2l, 1)

            @block.scalar
            def _(act):
                u = 0
                for b, (t0, n) in enumerate(TB):
                    for k in range(KC):
                        if b * KC + k >= 2:
                            act.wait_ge(s_ms, b * KC + k - 1)
                        act.activation(rel[k % 2][:, 0:n], ht[:, k, t0:t0 + n], ACT.Square).then_inc(s_sq, 1)
                    act.wait_ge(s_ms, (b + 1) * KC)
                    if b:
                        act.wait_ge(s_t, b * KC)
                    act.activation(rb[:, 0:n], ms_ps[b % 2][:, 0:n], ACT.Sqrt, bias=eps[:]).then_inc(s_std, 1)
                    for k in range(KC):
                        v = int(t0 >= LAT)
                        act.wait_ge(s_t, u + 1)
                        act.activation(sq[k % 2][:, 0:n], sq[k % 2][:, 0:n], ACT.Identity, scale=mod[:, layer, SC2, k, v:v + 1],
                                       bias=mod[:, layer, SH2, k, v:v + 1]).then_inc(s_n, 1)
                        act.wait_ge(s_n, u + 1)
                        act.activation(nh[:, k, t0:t0 + n], sq[k % 2][:, 0:n], ACT.Copy).then_inc(s_nh, 1)
                        u += 1
                act.wait_ge(s_nl, u)
                with act.Fori(0, PAIRS) as p:
                    act.wait_ge(s_w1, p * 16 + 16)
                    act.wait_ge(s_z, p * U1 + PRE)
                    act.activation(w1h[:], w1f[:], ACT.Copy).then_inc(s_w1h, 1)
                    act.wait_ge(s_w2, p * 16 + 16)
                    act.wait_ge(s_y, p * U2 + PRE)
                    act.activation(w2h[:], w2f[:], ACT.Copy).then_inc(s_w2h, 1)
                    for c in range(2):
                        for b, (t0, n) in enumerate(TB):
                            u = c * NB + b
                            act.wait_ge(s_z, p * U1 + (PRE + u + 1))
                            act.wait_ge(s_al, p * U1 + (PRE + u - 1))
                            act.activation(rel[u % 2][:, 0:n], z_ps[u % 2][:, 0:n], ACT.Relu).then_inc(s_rel, 1)
                            act.wait_ge(s_rel, p * U1 + (PRE + u + 1))
                            act.activation(ah[:, c, t0:t0 + n], rel[u % 2][:, 0:n], ACT.Square).then_inc(s_ah, 1)

            @block.vector
            def _(dve):
                u = 0
                for b, (t0, n) in enumerate(TB):
                    dve.wait_ge(s_std, b + 1)
                    dve.reciprocal(rb[:, 0:n], rb[:, 0:n]).then_inc(s_rb, 1)
                    dve.wait_ge(s_rb, b + 1)
                    for k in range(KC):
                        if u >= 2:
                            dve.wait_ge(s_nl, u - 1)
                        dve.tensor_tensor(sq[k % 2][:, 0:n], ht[:, k, t0:t0 + n], rb[:, 0:n], ALU.mult).then_inc(s_t, 1)
                        if u >= 1:
                            pb, pk = divmod(u - 1, KC)
                            p0, pn = TB[pb]
                            dve.wait_ge(s_nh, u)
                            lo_part(dve, nl[:, pk, p0:p0 + pn], sq[pk % 2][:, 0:pn], nh[:, pk, p0:p0 + pn]).then_inc(s_nl, 1)
                        u += 1
                p0, pn = TB[-1]
                dve.wait_ge(s_nh, u)
                lo_part(dve, nl[:, KC - 1, p0:p0 + pn], sq[(KC - 1) % 2][:, 0:pn], nh[:, KC - 1, p0:p0 + pn]).then_inc(s_nl, 1)
                with dve.Fori(0, PAIRS) as p:
                    for c in range(2):
                        for b, (t0, n) in enumerate(TB):
                            u = c * NB + b
                            dve.wait_ge(s_rel, p * U1 + (PRE + u + 1))
                            dve.tensor_tensor(sq[u % 2][:, 0:n], rel[u % 2][:, 0:n], rel[u % 2][:, 0:n], ALU.mult).then_inc(s_sqr, 1)
                            dve.wait_ge(s_sqr, p * U1 + (u + 1))
                            dve.wait_ge(s_ah, p * U1 + (u + 1))
                            lo_part(dve, al[:, c, t0:t0 + n], sq[u % 2][:, 0:n], ah[:, c, t0:t0 + n]).then_inc(s_al, 1)
                    dve.wait_ge(s_acc, p * U2 + PRE)
                    for b, (t0, n) in enumerate(TB):
                        for m in range(KC):
                            u = b * KC + m
                            dve.wait_ge(s_y, p * U2 + (PRE + u + 1))
                            h = ht[:, m, t0:t0 + n]
                            v = int(t0 >= LAT)
                            dve.scalar_tensor_tensor(out=h, in0=y_ps[u % 4][:, 0:n], scalar=mod[:, layer, G2, m, v:v + 1], in1=h,
                                                     op0=ALU.mult, op1=ALU.add).then_inc(s_acc, 1)

            @block.tensor
            def _(pe):
                for b, (t0, n) in enumerate(TB):
                    if b >= 2:
                        pe.wait_ge(s_std, b - 1)
                    for k in range(KC):
                        pe.wait_ge(s_sq, b * KC + k + 1)
                        pe.matmul(ms_ps[b % 2][:, 0:n], meanw[:], rel[k % 2][:, 0:n], start=(k == 0), stop=(k == KC - 1)).then_inc(s_ms, 1)
                pe.wait_ge(s_nl, NB * KC)
                with pe.Fori(0, PAIRS) as p:
                    pe.wait_ge(s_w1l, p + (PRE + 1))
                    for c in range(2):
                        for b, (t0, n) in enumerate(TB):
                            u = c * NB + b
                            pe.wait_ge(s_rel, p * U1 + (PRE + u - 1))
                            for k in range(KC):
                                cols = slice(c * P, (c + 1) * P)
                                last = mm3(pe, z_ps[u % 2][:, 0:n], (w1h[:, k, cols], w1l[:, k, cols]),
                                           (nh[:, k, t0:t0 + n], nl[:, k, t0:t0 + n]), k == 0, k == KC - 1)
                            last.then_inc(s_z, 1)
                    pe.wait_ge(s_w2l, p + (PRE + 1))
                    for b, (t0, n) in enumerate(TB):
                        pe.wait_ge(s_al, p * U1 + (PRE + NB + b + 1))
                        for m in range(KC):
                            u = b * KC + m
                            pe.wait_ge(s_acc, p * U2 + (PRE + u - 3))
                            for c in range(2):
                                last = mm3(pe, y_ps[u % 4][:, 0:n], (w2h[:, c, m * P:(m + 1) * P], w2l[:, c, m * P:(m + 1) * P]),
                                           (ah[:, c, t0:t0 + n], al[:, c, t0:t0 + n]), c == 0, c == 1)
                            last.then_inc(s_y, 1)


def norm_out(nc, sem, sb, banks, layer, park, mod, meanw, eps, nh, nl, ht):
    with ExitStack() as ph:
        sq = [sb(f"nsq{i}", [P, 512], where=ph) for i in range(2)]
        tn = [sb(f"ntn{i}", [P, 512], where=ph) for i in range(2)]
        rb = [sb(f"nrb{i}", [P, 512], where=ph) for i in range(2)]
        ms_ps = banks("nms_ps", 3, ph)
        s_park, s_sq, s_ms, s_std, s_rb, s_t, s_n, s_nh, s_nl = (sem("q_" + n) for n in (
            "park", "sq", "ms", "std", "rb", "t", "n", "nh", "nl"))
        UN = [(b, t0, n, k) for b, (t0, n) in enumerate(BLOCKS) for k in range(KC)]
        with nc.Block() as block:
            @block.sync
            def _(sp):
                sp.dma_start(park, ht[:, :, 0:LAT]).then_inc(s_park, 16)
                sp.wait_ge(s_park, 16)

            @block.scalar
            def _(act):
                def squares(b):
                    t0, n = BLOCKS[b]
                    for k in range(KC):
                        if b * KC + k >= 2:
                            act.wait_ge(s_ms, b * KC + k - 1)
                        act.activation(sq[k % 2][:, 0:n], ht[:, k, t0:t0 + n], ACT.Square).then_inc(s_sq, 1)
                    act.wait_ge(s_ms, (b + 1) * KC)
                    if b >= 2:
                        act.wait_ge(s_t, (b - 1) * KC)
                    act.activation(rb[b % 2][:, 0:n], ms_ps[b][:, 0:n], ACT.Sqrt, bias=eps[:]).then_inc(s_std, 1)
                squares(0)
                for u, (b, t0, n, k) in enumerate(UN):
                    if k == 0 and b + 1 < len(BLOCKS):
                        squares(b + 1)
                    v = int(t0 >= LAT)
                    act.wait_ge(s_t, u + 1)
                    act.activation(tn[u % 2][:, 0:n], tn[u % 2][:, 0:n], ACT.Identity, scale=mod[:, layer, SC1, k, v:v + 1],
                                   bias=mod[:, layer, SH1, k, v:v + 1]).then_inc(s_n, 1)
                    act.wait_ge(s_n, u + 1)
                    act.activation(nh[:, k, t0:t0 + n], tn[u % 2][:, 0:n], ACT.Copy).then_inc(s_nh, 1)

            @block.vector
            def _(dve):
                def low(u):
                    _, t0, n, k = UN[u]
                    dve.wait_ge(s_nh, u + 1)
                    lo_part(dve, nl[:, k, t0:t0 + n], tn[u % 2][:, 0:n], nh[:, k, t0:t0 + n]).then_inc(s_nl, 1)
                for u, (b, t0, n, k) in enumerate(UN):
                    if k == 0:
                        dve.wait_ge(s_std, b + 1)
                        dve.reciprocal(rb[b % 2][:, 0:n], rb[b % 2][:, 0:n]).then_inc(s_rb, 1)
                        dve.wait_ge(s_rb, b + 1)
                    if u >= 2:
                        dve.wait_ge(s_nl, u - 1)
                    dve.tensor_tensor(tn[u % 2][:, 0:n], ht[:, k, t0:t0 + n], rb[b % 2][:, 0:n], ALU.mult).then_inc(s_t, 1)
                    if u >= 1:
                        low(u - 1)
                low(len(UN) - 1)

            @block.tensor
            def _(pe):
                for u, (b, t0, n, k) in enumerate(UN):
                    pe.wait_ge(s_sq, u + 1)
                    pe.matmul(ms_ps[b][:, 0:n], meanw[:], sq[k % 2][:, 0:n], start=(k == 0), stop=(k == KC - 1)).then_inc(s_ms, 1)


def qkv(nc, sem, sb, banks, wqkv, qkg, rope, ident, eps, nh, nl, qd, kh, kl, vs):
    KV0 = D
    COLS = [(KV0, 2 * KVH * HD), (0, 512), (512, 512)]
    UNITS = [(0, t) for t in range(NT)] + [(c, t) for c in (1, 2) for t in range(QB)]
    HB = 8
    first = {c: min(u for u, (cc, _) in enumerate(UNITS) if cc == c) for c in range(3)}
    with ExitStack() as ph:
        wf = sb("qwf", [P, KC, 512], where=ph)
        ropev = sb("rope_sb", [P, 2, NT, HD], where=ph)
        wh = sb("qwh", [P, KC, 512], F32R, where=ph)
        wl = sb("qwl", [P, KC, 512], F32R, where=ph)
        g = sb("qkg_sb", [P, 2, HD], where=ph)
        ct = sb("ct", [P, 2, NT, HD], where=ph)
        st = sb("st", [P, 2, NT, HD], where=ph)
        raw = [sb(f"raw{i}", [P, 512], where=ph) for i in range(2)]
        tmp = [sb(f"qtmp{i}", [P, 512], where=ph) for i in range(2)]
        qo = [sb(f"qo{i}", [P, 512], where=ph) for i in range(2)]
        kr = sb("kr", [P, NT, KVH, 2, HD], where=ph)
        ss = sb("ss", [P, 2, HB], where=ph)
        p_ps, tr_ps = banks("qkv_ps", 3, ph), banks("ktr_ps", 2, ph)
        s_rope, s_g, s_tabs, s_used, s_wh, s_wl = (sem("k_" + n) for n in ("rope", "g", "tabs", "wused", "wh", "wl"))
        s_w = [sem(f"k_w{i}") for i in range(2)]
        s_p, s_raw, s_sq, s_ss, s_std, s_dv, s_done, s_vh, s_vl = (sem("k_" + n) for n in (
            "prod", "raw", "sq", "ss", "std", "dv", "done", "vh", "vl"))
        s_tr, s_kh, s_kl, s_pad = (sem("k_" + n) for n in ("tr", "kh", "kl", "pad"))
        s_q = [sem(f"k_q{i}") for i in range(2)]
        def keys_after(u):
            x, per = u - NT, KVH * NT / (2 * QB)
            return [(i, i // KVH, i % KVH) for i in range(int(x * per), int((x + 1) * per))] if u >= NT else []

        def halves(ap):
            return ap.rearrange("p h (a s c) -> p h a s c", a=2, s=2)

        with nc.Block() as block:
            @block.sync
            def _(sp):
                for c, (c0, w) in enumerate(COLS):
                    for hf in range(2):
                        if c:
                            sp.wait_ge(s_wl, KC * (c - 1) + 4 * hf + 4)
                        src = wqkv[512 * hf:512 * hf + 512, c0:c0 + w].rearrange("(k p) n -> p k n", p=P)
                        sp.dma_start(wf[:, 4 * hf:4 * hf + 4, 0:w], src).then_inc(s_w[hf], 16)
                    if c == 0:
                        sp.dma_start(ropev[:], rope).then_inc(s_rope, 16)
                        sp.dma_start(g[:].rearrange("p a d -> p (a d)"), qkg).then_inc(s_g, 16)

            @block.gpsimd
            def _(pool):
                for b in (0, QB + 1):
                    pool.memset(f32(kh[:, :, b * P:(b + 1) * P]), 0.0).then_inc(s_pad, 1)
                    pool.memset(f32(kl[:, :, b * P:(b + 1) * P]), 0.0).then_inc(s_pad, 1)
                    pool.memset(f32(vs[:, b]), 0.0).then_inc(s_pad, 1)
                for u in range(NT, len(UNITS)):
                    c, t = UNITS[u]
                    pool.wait_ge(s_done, u + 1)
                    pool.dma_start(qd[t, 2 * (c - 1):2 * c].rearrange("a p n -> p a n"),
                                   qo[u % 2][:].rearrange("p (a n) -> p a n", a=2)).then_inc(s_q[u % 2], 16)
                for i in range(2):
                    pool.wait_ge(s_q[i], 16 * QB)

            @block.scalar
            def _(act):
                def weights(c):
                    w = COLS[c][1]
                    for k in range(KC):
                        act.wait_ge(s_w[k // 4], 16 * (c + 1))
                        if c:
                            if k < KC - 1:
                                act.wait_ge(s_used, (KC - 1) * (c - 1) + k + 1)
                            else:
                                act.wait_ge(s_p, first[c])
                        act.activation(wh[:, k, 0:w], wf[:, k, 0:w], ACT.Copy).then_inc(s_wh, 1)
                weights(0)
                for u, (c, t) in enumerate(UNITS):
                    w = COLS[c][1]
                    nq = KVH * HD if c == 0 else 512
                    H = nq // HD
                    act.wait_ge(s_p, u + 1)
                    if u >= 2:
                        act.wait_ge(s_done, u - 1)
                    act.activation(raw[u % 2][:, 0:w], p_ps[u % 3][:, 0:w], ACT.Copy).then_inc(s_raw, 1)
                    act.activation(tmp[u % 2][:, 0:nq], p_ps[u % 3][:, 0:nq], ACT.Square).then_inc(s_sq, 1)
                    if c == 0:
                        tb = t + 1 if t < QB else t + 2
                        v = raw[u % 2][:, 128:256].rearrange("p (a d) -> p a d", a=KVH)
                        act.wait_ge(s_raw, u + 1)
                        act.activation(vs[:, tb, :, 0:HD], v, ACT.Copy).then_inc(s_vh, 1)
                    act.wait_ge(s_ss, u + 1)
                    act.activation(ss[:, u % 2, 0:H], ss[:, u % 2, 0:H], ACT.Sqrt, bias=eps[:], scale=1.0 / HD).then_inc(s_std, 1)
                    for i, kt, gg in keys_after(u):
                        tb = kt + 1 if kt < QB else kt + 2
                        act.wait_ge(s_tr, i + 1)
                        act.activation(kh[:, gg, tb * P:(tb + 1) * P], tr_ps[i % 2][:, 0:P], ACT.Copy).then_inc(s_kh, 1)
                    if c < 2 and u + 2 == first[c + 1]:
                        weights(c + 1)

            @block.vector
            def _(dve):
                chain = [0]

                def link(ins):
                    chain[0] += 1
                    ins.then_inc(s_dv, 1)
                    dve.wait_ge(s_dv, chain[0])

                def weights(c):
                    w = COLS[c][1]
                    for k in range(KC):
                        dve.wait_ge(s_wh, KC * c + k + 1)
                        lo_part(dve, wl[:, k, 0:w], wf[:, k, 0:w], wh[:, k, 0:w]).then_inc(s_wl, 1)
                weights(0)
                dve.wait_ge(s_rope, 16)
                dve.wait_ge(s_g, 16)
                link(dve.tensor_scalar_mul(g[:, 0], g[:, 0], -HD ** -0.5))
                for a in range(2):
                    gb = g[:, a:a + 1, :].to_broadcast([P, NT, HD])
                    dve.tensor_tensor(ct[:, a], ropev[:, 0], gb, ALU.mult).then_inc(s_tabs, 1)
                    for ax in range(2):
                        for s in range(2):
                            lanes = slice(32 * ax + 16 * s, 32 * ax + 16 * s + 16)
                            partner = slice(32 * ax + 16 * (1 - s), 32 * ax + 16 * (1 - s) + 16)
                            dve.tensor_tensor(st[:, a, :, lanes], ropev[:, 1, :, lanes], g[:, a:a + 1, partner].to_broadcast([P, NT, 16]),
                                              ALU.mult).then_inc(s_tabs, 1)
                dve.wait_ge(s_tabs, 10)
                for u, (c, t) in enumerate(UNITS):
                    nq = KVH * HD if c == 0 else 512
                    H = nq // HD
                    q = raw[u % 2][:, 0:nq].rearrange("p (h d) -> p h d", d=HD)
                    m = tmp[u % 2][:, 0:nq].rearrange("p (h d) -> p h d", d=HD)
                    a = 1 if c == 0 else 0
                    dve.wait_ge(s_sq, u + 1)
                    dve.reduce_sum(ss[:, u % 2, 0:H], m, axis=AX.X).then_inc(s_ss, 1)
                    if c == 0:
                        tb = t + 1 if t < QB else t + 2
                        dve.wait_ge(s_vh, u + 1)
                        lo_part(dve, vs[:, tb, :, HD:2 * HD], raw[u % 2][:, 128:256].rearrange("p (a d) -> p a d", a=KVH),
                                vs[:, tb, :, 0:HD]).then_inc(s_vl, 1)
                    dve.wait_ge(s_std, u + 1)
                    link(dve.reciprocal(ss[:, u % 2, 0:H], ss[:, u % 2, 0:H]))
                    dve.wait_ge(s_raw, u + 1)
                    link(dve.tensor_tensor(q, q, ss[:, u % 2, 0:H].rearrange("p (h o) -> p h o", o=1).to_broadcast([P, H, HD]), ALU.mult))
                    for s in range(2):
                        r = st[:, a, t:t + 1, :].to_broadcast([P, H, HD])
                        ins = dve.tensor_tensor(halves(m)[:, :, :, s, :], halves(q)[:, :, :, 1 - s, :], halves(r)[:, :, :, s, :], ALU.mult)
                    link(ins)
                    dst = kr[:, t, :, 0, :] if c == 0 else qo[u % 2][:].rearrange("p (h d) -> p h d", d=HD)
                    if c and u - NT >= 2:
                        dve.wait_ge(s_q[u % 2], 16 * ((u - NT) // 2))
                    link(dve.tensor_tensor(dst, q, ct[:, a, t:t + 1, :].to_broadcast([P, H, HD]), ALU.mult))
                    if c == 0:
                        dve.tensor_tensor(kr[:, t, :, 1, :], dst, m, ALU.add)
                    dve.tensor_tensor(dst, dst, m, ALU.add).then_inc(s_done, 1)
                    for i, kt, gg in keys_after(u):
                        tb = kt + 1 if kt < QB else kt + 2
                        dve.wait_ge(s_kh, i + 1)
                        lo_part(dve, kl[:, gg, tb * P:(tb + 1) * P], tr_ps[i % 2][:, 0:P], kh[:, gg, tb * P:(tb + 1) * P]).then_inc(s_kl, 1)
                    if c < 2 and u + 2 == first[c + 1]:
                        weights(c + 1)

            @block.tensor
            def _(pe):
                for u, (c, t) in enumerate(UNITS):
                    if u >= 3:
                        pe.wait_ge(s_sq, u - 2)
                    w = COLS[c][1]
                    leaving = c < 2 and u + 1 == first[c + 1]
                    for k in range(KC):
                        cols = slice(t * P, (t + 1) * P)
                        if u == first[c]:
                            pe.wait_ge(s_wl, KC * c + k + 1)
                        last = mm3(pe, p_ps[u % 3][:, 0:w], (nh[:, k, cols], nl[:, k, cols]), (wh[:, k, 0:w], wl[:, k, 0:w]),
                                   k == 0, k == KC - 1)
                        if k == KC - 1:
                            last.then_inc(s_p, 1)
                        elif leaving:
                            last.then_inc(s_used, 1)
                    for i, kt, gg in keys_after(u):
                        pe.wait_ge(s_done, kt + 1)
                        if i >= 2:
                            pe.wait_ge(s_kl, i - 1)
                        pe.transpose(tr_ps[i % 2][:, 0:P], kr[:, kt, gg].rearrange("p a d -> p (a d)"), ident[:]).then_inc(s_tr, 1)


def attention(nc, sem, sb, banks, masks, sink, ident, qd, kh, kl, vs, nh, nl):
    PAIRS = QB // 2
    NQ = 8
    KB = KEYS // P
    W = 3 * P
    O_AT = (1, 2, 3)
    SETS = 4
    with ExitStack() as ph:
        mstore = sb("mstore", [P, QB, 2, P], where=ph)
        mask = sb("mask", [P, KEYS], where=ph)
        nsink, zero4 = sb("nsink", [P, HEADS], where=ph), sb("zero4", [P, 4], where=ph)
        qb = sb("qb", [P, 4, 4, 2, HD], where=ph)
        qs = [sb(f"qs{i}", [P, 512], F32R, where=ph) for i in range(2)]
        vw = [sb(f"vw{i}", [P, 3, KVH, 2 * HD], F32R, where=ph) for i in range(2)]
        sc = sb("sc", [P, SETS, 4, KEYS + 1], where=ph)
        mn, den = sb("mn", [P, SETS, 4], where=ph), sb("den", [P, SETS, 4], where=ph)
        pth = [sb(f"pth{i}", [P, 512], F32R, where=ph) for i in range(2)]
        ptl = [sb(f"ptl{i}", [P, 512], F32R, where=ph) for i in range(2)]
        ot, of = sb("ot", [HD, 512], where=ph), sb("of", [P, 2, P], where=ph)
        s_ps = [ph.enter_context(nc.psum_tensor(f"s_ps{i}", [P, 1024], F32)) for i in range(2)]
        t_ps, o_ps = banks("t_ps", 2, ph), banks("pv_ps", 2, ph)
        q_ps = t_ps[0]

        def bank(kb):
            return t_ps[kb % 2 if kb < 4 else 1]

        s_ms, s_sk, s_ns, s_z, s_m0, s_mask, s_vw, s_held = (sem("t_" + n) for n in (
            "mstore", "sink", "nsink", "zero", "mask0", "mask", "vw", "held"))
        s_qb = [sem(f"t_qb{i}") for i in range(4)]
        s_qtr, s_qh, s_qs, s_sc, s_s, s_col, s_e, s_rd, s_p = (sem("t_" + n) for n in (
            "qtr", "qh", "qs", "scores", "masked", "sinkcol", "exp", "rden", "prob"))
        s_pt, s_ph, s_pl, s_o, s_ot, s_of, s_oh, s_ol = (sem("t_" + n) for n in ("ptr", "pth", "ptl", "pv", "ot", "of", "oh", "ol"))

        def at(jj, n, c, k):
            return jj * (NQ * c) + (PRE + c * n + k)

        def schedule(eng, whole_a, part_q, step):
            for n in range(2):
                part_q(0, n)
                whole_a(0, n)
            part_q(0, 2)
            step(0, 0, True, True, start=True)
            with eng.Fori(0, PAIRS - 1) as jj:
                for n in range(1, NQ + 1):
                    step(jj, n, True, True)
            for n in range(1, NQ):
                step(PAIRS - 1, n, n + 2 < NQ, n + 3 < NQ)

        with nc.Block() as block:
            @block.sync
            def _(sp):
                sp.dma_start(mstore[:], masks).then_inc(s_ms, 16)
                sp.dma_start(nsink[:], sink).then_inc(s_sk, 16)
                with sp.Fori(0, QB) as j:
                    for i in range(4):
                        sp.wait_ge(s_qtr, j * 4 + (PRE + i - 3))
                        for twice in range(2):
                            sp.dma_start(qb[:, i, :, twice, :], qd[bass.ds(j, 1), i].rearrange("a p (h d) -> p (a h) d", d=HD)).then_inc(s_qb[i], 16)

            @block.gpsimd
            def _(pool):
                pool.memset(zero4[:], 0.0).then_inc(s_z, 1)
                for s in (s_qtr, s_qh, s_qs, s_sc, s_s, s_col, s_e, s_rd, s_p, s_pt, s_ph, s_pl, s_o, s_ot, s_of, s_oh, s_ol):
                    pool.sem_inc(s, PRE)
                pool.wait_ge(s_z, 1)
                pool.wait_ge(s_ns, 1)

                def column(jj, n):
                    i, h0 = n % SETS, 4 * (n % 4)
                    pool.wait_ge(s_pt, at(jj, n, KB, -(SETS - 1) * KB))
                    pool.tensor_tensor(sc[:, i, :, KEYS], nsink[:, h0:h0 + 4], zero4[:], ALU.add).then_inc(s_col, 1)

                def part_a(jj, n, more=True):
                    i = n % SETS
                    if more:
                        column(jj, n + 1)
                    pool.wait_ge(s_rd, at(jj, n, 1, 1))
                    for h in range(4):
                        pool.tensor_tensor(sc[:, i, h, 0:KEYS], sc[:, i, h, 0:KEYS], den[:, i, h:h + 1].to_broadcast([P, KEYS]),
                                           ALU.mult).then_inc(s_p, 1)

                def step(jj, n, with_a, with_q, start=False):
                    if with_a:
                        part_a(jj, n + 2, with_q)
                column(0, 0)
                schedule(pool, part_a, lambda jj, n: None, step)

            @block.scalar
            def _(act):
                def part_q(jj, n):
                    act.wait_ge(s_qtr, at(jj, n, 1, 1))
                    act.wait_ge(s_sc, at(jj, n, 4, -4))
                    act.activation(qs[n % 2][:], q_ps[:], ACT.Copy).then_inc(s_qh, 1)

                def head(jj, n, h):
                    i = n % SETS
                    if h == 0:
                        act.wait_ge(s_col, at(jj, n, 1, 1))
                    act.wait_ge(s_s, at(jj, n, 4, h + 1))
                    act.activation(sc[:, i, h, :], sc[:, i, h, :], ACT.Exp, scale=-1.0, bias=mn[:, i, h:h + 1],
                                   accum_out=den[:, i, h:h + 1]).then_inc(s_e, 1)

                def part_o(jj, n):
                    act.wait_ge(s_o, at(jj, n, KB, KB))
                    act.wait_ge(s_of, at(jj, n, 1, 0))
                    act.activation(ot[:], o_ps[n % 2][0:HD, :], ACT.Copy).then_inc(s_ot, 1)

                def step(jj, n, with_a, with_q, start=False):
                    for kb in range(KB):
                        slot = (n + kb) % 2
                        act.wait_ge(s_pt, at(jj, n, KB, kb + 1))
                        act.wait_ge(s_o, at(jj, n, KB, kb - 1))
                        act.activation(pth[slot][:], bank(kb)[:], ACT.Copy).then_inc(s_ph, 1)
                        if kb and with_a:
                            head(jj, n + 2, kb - 1)
                        if kb == O_AT[0] - 1 and not start:
                            part_o(jj, n - 1)
                        if kb == 3 and with_q:
                            part_q(jj, n + 3)
                schedule(act, lambda jj, n: [head(jj, n, h) for h in range(4)], part_q, step)
                part_o(PAIRS - 1, NQ - 1)

            @block.vector
            def _(dve):
                dve.wait_ge(s_sk, 16)
                dve.tensor_scalar_mul(nsink[:], nsink[:], -1.0).then_inc(s_ns, 1)
                dve.memset(mask[:], 0.0).then_inc(s_m0, 1)
                dve.wait_ge(s_m0, 1)
                dve.wait_ge(s_ns, 1)
                dve.wait_ge(s_ms, 16)

                def part_q(jj, n):
                    low = qs[n % 2][HD:P, :]
                    dve.wait_ge(s_qh, at(jj, n, 1, 1))
                    dve.tensor_tensor(low, q_ps[HD:P, :], f32(low), ALU.subtract).then_inc(s_qs, 1)

                def head(jj, n, h):
                    i, h0, dj = n % SETS, 4 * (n % 4), n // 4
                    if n % 4 == 0 and h == 0:
                        dve.wait_ge(s_s, at(jj, n, 4, 0))
                        dve.wait_ge(s_o, at(jj, n, KB, -4 * KB))
                        dve.tensor_scalar_mul(vw[dj % 2][:], f32(vs[:, bass.ds(jj * 2 + dj, 3)]), 1.0).then_inc(s_vw, 1)
                        for side in range(2):
                            dve.tensor_scalar_mul(mask[:, 2 * side * P:(2 * side + 1) * P],
                                                  mstore[:, bass.ds(jj * 2 + dj, 1), side].rearrange("p a n -> p (a n)"), 1.0).then_inc(s_mask, 1)
                        dve.wait_ge(s_mask, jj * 4 + (2 * dj + 2))
                    dve.wait_ge(s_sc, at(jj, n, 4, h + 1))
                    dve.wait_ge(s_pt, at(jj, n, KB, -(SETS - 1) * KB))
                    dve.sem_inc(s_held, 1)
                    dve.tensor_tensor_reduce(out=sc[:, i, h, 0:KEYS], in0=s_ps[h % 2][:, P:P + KEYS], in1=mask[:], scale=1.0,
                                             scalar=nsink[:, h0 + h:h0 + h + 1], op0=ALU.add, op1=ALU.min,
                                             accum_out=mn[:, i, h:h + 1]).then_inc(s_s, 1)

                def recip(jj, n):
                    i = n % SETS
                    dve.wait_ge(s_e, at(jj, n, 4, 4))
                    dve.reciprocal(den[:, i], den[:, i]).then_inc(s_rd, 1)

                def part_o(jj, n, stage):
                    c0 = 2 * (n % 4)
                    cols = bass.ds(jj * (2 * P) + (n // 4) * P, P)
                    if stage == 0:
                        dve.wait_ge(s_ot, at(jj, n, 1, 1))
                        hi = ot[:].rearrange("p (c s q) -> p c s q", c=2, s=2)
                        lo = o_ps[n % 2][HD:P, :].rearrange("p (c s q) -> p c s q", c=2, s=2)
                        for s in range(2):
                            ins = dve.tensor_tensor(of[HD * s:HD * s + HD], lo[:, :, s, :], hi[:, :, s, :], ALU.add)
                        ins.then_inc(s_of, 1)
                    elif stage == 1:
                        dve.wait_ge(s_of, at(jj, n, 1, 1))
                        dve.tensor_scalar_mul(nh[:, c0:c0 + 2, cols], of[:], 1.0).then_inc(s_oh, 1)
                    else:
                        dve.wait_ge(s_oh, at(jj, n, 1, 1))
                        lo_part(dve, nl[:, c0:c0 + 2, cols], of[:], nh[:, c0:c0 + 2, cols]).then_inc(s_ol, 1)

                def step(jj, n, with_a, with_q, start=False):
                    for kb in range(KB):
                        slot = (n + kb) % 2
                        dve.wait_ge(s_ph, at(jj, n, KB, kb + 1))
                        lo_part(dve, ptl[slot][:], bank(kb)[:], pth[slot][:]).then_inc(s_pl, 1)
                        if kb == 0 and (with_a or n + 1 < NQ):
                            recip(jj, n + 1)
                        if kb in O_AT and not start:
                            part_o(jj, n - 1, kb - O_AT[0])
                        if kb < 4 and with_a:
                            head(jj, n + 2, kb)
                        if kb == 3 and with_q:
                            part_q(jj, n + 3)

                def whole_a(jj, n):
                    for h in range(4):
                        head(jj, n, h)
                    if n == 0:
                        recip(jj, n)
                schedule(dve, whole_a, part_q, step)
                for stage in range(3):
                    part_o(PAIRS - 1, NQ - 1, stage)

            @block.tensor
            def _(pe):
                def part_q(jj, n):
                    i = n % 4
                    pe.wait_ge(s_qb[i], jj * 64 + (n // 4 + 1) * 32)
                    pe.wait_ge(s_qs, at(jj, n, 1, 0))
                    for h in range(4):
                        last = pe.transpose(q_ps[:, h * P:(h + 1) * P], qb[:, i, h].rearrange("p a d -> p (a d)"), ident[:])
                    last.then_inc(s_qtr, 1)

                def head(jj, n, h):
                    g, dj = (n % 4) // 2, n // 4
                    if h == 0:
                        pe.wait_ge(s_qs, at(jj, n, 1, 1))
                    pe.wait_ge(s_s, at(jj, n, 4, h - 1))
                    q = qs[n % 2][:, h * P:(h + 1) * P]
                    win = bass.ds(jj * (2 * P) + dj * P, W)
                    ctxk = slice((QB + 2) * P, (QB + 4) * P)
                    pe.matmul(s_ps[h % 2][:, P:P + W], q, kh[:, g, win], start=True, stop=False)
                    pe.matmul(s_ps[h % 2][:, P:P + W], q, kl[:, g, win], start=False, stop=True)
                    pe.matmul(s_ps[h % 2][:, P + W:P + KEYS], q, kh[:, g, ctxk], start=True, stop=False)
                    pe.matmul(s_ps[h % 2][:, P + W:P + KEYS], q, kl[:, g, ctxk], start=False, stop=True).then_inc(s_sc, 1)

                def values(jj, n, kb):
                    g, slot, o = (n % 4) // 2, (n + kb) % 2, o_ps[n % 2]
                    if kb == 0:
                        pe.wait_ge(s_of, at(jj, n, 1, -1))
                        pe.wait_ge(s_vw, jj * 2 + (n // 4 + 1))
                    pe.wait_ge(s_pl, at(jj, n, KB, kb + 1))
                    v = vw[(n // 4) % 2][:, kb, g, :] if kb < 3 else vs[:, QB + 2 + kb - 3, g, :]
                    pe.matmul(o[:], v, pth[slot][:], start=(kb == 0), stop=False)
                    pe.matmul(o[:], v, ptl[slot][:], start=False, stop=(kb == KB - 1)).then_inc(s_o, 1)

                def step(jj, n, with_a, with_q, start=False):
                    pe.wait_ge(s_p, at(jj, n, 4, 4))
                    for kb in range(KB):
                        if kb == 0 and with_a:
                            pe.wait_ge(s_qs, at(jj, n + 2, 1, 1))
                        elif kb == 0:
                            pe.wait_ge(s_pl, at(jj, n, KB, -2))
                        elif kb == 4:
                            pe.wait_ge(s_pl, at(jj, n, KB, 4))
                        else:
                            pe.wait_ge(s_pl, at(jj, n, KB, kb - 1))
                        for h in range(4):
                            last = pe.transpose(bank(kb)[:, h * P:(h + 1) * P], sc[:, n % SETS, h, kb * P:(kb + 1) * P], ident[:])
                        last.then_inc(s_pt, 1)
                        if kb < 4 and with_a:
                            head(jj, n + 2, kb)
                        if kb:
                            values(jj, n, kb - 1)
                        elif not start:
                            values(jj, n - 1, KB - 1)
                        if kb == 3 and with_q:
                            pe.wait_ge(s_pl, at(jj, n, KB, 3))
                            part_q(jj, n + 3)
                schedule(pe, lambda jj, n: [head(jj, n, h) for h in range(4)], part_q, step)
                values(PAIRS - 1, NQ - 1, KB - 1)


def attn_out(nc, sem, sb, banks, wo, park, mod, nh, nl, ht):
    TB = BLOCKS[:2]
    with ExitStack() as ph:
        wf = [sb(f"of{i}", [P, KC, P], where=ph) for i in range(2)]
        wh = [sb(f"owh{i}", [P, KC, P], F32R, where=ph) for i in range(2)]
        wl = [sb(f"owl{i}", [P, KC, P], F32R, where=ph) for i in range(2)]
        o_ps = banks("oo_ps", 4, ph)
        s_h, s_wh, s_wl, s_o, s_add = (sem("w_" + n) for n in ("ht", "wh", "wl", "prod", "add"))
        s_w = [sem(f"w_w{i}") for i in range(2)]
        with nc.Block() as block:
            @block.gpsimd
            def _(pool):
                for s in (s_wl, s_o, s_add):
                    pool.sem_inc(s, PRE)

            @block.sync
            def _(sp):
                with sp.Fori(0, KC // 2) as r:
                    for i in range(2):
                        sp.wait_ge(s_wl, r * 2 + (PRE + i - 1))
                        sp.dma_start(wf[i][:], wo[bass.ds(r * 2 + i, 1)].rearrange("a p k n -> p (a k) n")).then_inc(s_w[i], 16)

            @block.scalar
            def _(act):
                def high(r, i):
                    act.wait_ge(s_w[i % 2], r * 16 + 16 * (i // 2 + 1))
                    act.wait_ge(s_o, r * 4 + (PRE + 2 * i - 2))
                    act.activation(wh[i % 2][:], wf[i % 2][:], ACT.Copy).then_inc(s_wh, 1)
                act.dma_start(ht[:], park).then_inc(s_h, 16)
                with act.Fori(0, KC // 2) as r:
                    for i in range(2):
                        high(r, i)

            @block.vector
            def _(dve):
                def low(r, i):
                    dve.wait_ge(s_wh, r * 2 + (i + 1))
                    lo_part(dve, wl[i % 2][:], wf[i % 2][:], wh[i % 2][:]).then_inc(s_wl, 1)

                def pair(r, more):
                    for i in range(2):
                        for b, (t0, n) in enumerate(TB):
                            h = ht[:, bass.ds(r * 2 + i, 1), t0:t0 + n].rearrange("p a s -> p (a s)")
                            dve.wait_ge(s_o, r * 4 + (PRE + 2 * i + b + 1))
                            dve.scalar_tensor_tensor(out=h, in0=o_ps[2 * i + b][:, 0:n], scalar=mod[:, 1, G1, bass.ds(r * 2 + i, 1), 0],
                                                     in1=h, op0=ALU.mult, op1=ALU.add).then_inc(s_add, 1)
                            if b == 0 and (more or i == 0):
                                low(r, i + 1)
                low(0, 0)
                dve.wait_ge(s_h, 16)
                with dve.Fori(0, KC // 2 - 1) as r:
                    pair(r, True)
                pair(KC // 2 - 1, False)

            @block.tensor
            def _(pe):
                with pe.Fori(0, KC // 2) as r:
                    for i in range(2):
                        pe.wait_ge(s_wl, r * 2 + (PRE + i + 1))
                        for b, (t0, n) in enumerate(TB):
                            pe.wait_ge(s_add, r * 4 + (PRE + 2 * i + b - 3))
                            for k in range(KC):
                                last = mm3(pe, o_ps[2 * i + b][:, 0:n], (wh[i][:, k, :], wl[i][:, k, :]),
                                           (nh[:, k, t0:t0 + n], nl[:, k, t0:t0 + n]), k == 0, k == KC - 1)
                            last.then_inc(s_o, 1)


def write_out(nc, sem, sb, banks, ident, ht, out):
    with ExitStack() as ph:
        ob = [sb(f"ob{i}", [P, D], where=ph) for i in range(2)]
        ps = banks("w_ps", 4, ph)
        s_tr, s_a, s_d = sem("z_tr"), sem("z_act"), sem("z_dve")
        s_out = [sem(f"z_out{i}") for i in range(2)]
        with nc.Block() as block:
            @block.sync
            def _(sp):
                for t in range(QB):
                    sp.wait_ge(s_a, t + 1)
                    sp.wait_ge(s_d, t + 1)
                    sp.dma_start(out[t * P:(t + 1) * P, :], ob[t % 2][:]).then_inc(s_out[t % 2], 16)
                for i in range(2):
                    sp.wait_ge(s_out[i], 16 * QB // 2)

            @block.scalar
            def _(act):
                for t in range(QB):
                    if t >= 2:
                        act.wait_ge(s_out[t % 2], 16 * (t // 2))
                    act.wait_ge(s_tr, 2 * t + 1)
                    act.activation(ob[t % 2][:, 0:512], ps[2 * (t % 2)][:], ACT.Copy).then_inc(s_a, 1)

            @block.vector
            def _(dve):
                for t in range(QB):
                    if t >= 2:
                        dve.wait_ge(s_out[t % 2], 16 * (t // 2))
                    dve.wait_ge(s_tr, 2 * t + 2)
                    dve.tensor_copy(ob[t % 2][:, 512:1024], ps[2 * (t % 2) + 1][:]).then_inc(s_d, 1)

            @block.tensor
            def _(pe):
                for t in range(QB):
                    if t >= 2:
                        pe.wait_ge(s_a, t - 1)
                        pe.wait_ge(s_d, t - 1)
                    for half in range(2):
                        for k in range(4):
                            last = pe.transpose(ps[2 * (t % 2) + half][:, k * P:(k + 1) * P],
                                                ht[:, 4 * half + k, t * P:(t + 1) * P], ident[:])
                        last.then_inc(s_tr, 1)


def dft_tables():
    t, s = np.arange(256)[:, None], np.arange(256)[None, :]
    out = []
    for s1 in (0, 2, 1):
        a = 2 * np.pi * (((4 * s + s1) * t) % LAT) / LAT
        out.append(np.concatenate([np.cos(a), np.sin(a)], axis=1))
    c, s_ = out[2][:, :256], out[2][:, 256:]
    out.append(np.concatenate([-s_, c], axis=1))
    return np.stack([o.reshape(2, P, 512).transpose(1, 0, 2) for o in out]).astype(np.float32)


def rope_tables():
    inv = 10000.0 ** (-np.arange(16, dtype=np.float32) / np.float32(16))
    pos = np.arange(LAT)
    ar = (pos // 64).astype(np.float32)[:, None] * inv[None, :]
    ac = (pos % 64).astype(np.float32)[:, None] * inv[None, :]
    cos = np.concatenate([np.cos(ar), np.cos(ar), np.cos(ac), np.cos(ac)], axis=1)
    sin = np.concatenate([-np.sin(ar), np.sin(ar), -np.sin(ac), np.sin(ac)], axis=1)
    cos = np.concatenate([cos, np.ones((CTX, HD))]).reshape(NT, P, HD)
    sin = np.concatenate([sin, np.zeros((CTX, HD))]).reshape(NT, P, HD)
    return np.stack([cos, sin]).transpose(2, 0, 1, 3).astype(np.float32)


def band_masks():
    q, k = np.arange(P)[:, None], np.arange(P)[None, :]
    m = np.stack([np.where(k >= q, 0, BIG), np.where(k <= q, 0, BIG)])
    m = np.repeat(m[None], QB, axis=0)
    m[0, 0] = BIG
    m[QB - 1, 1] = BIG
    return m.transpose(2, 0, 1, 3).astype(np.float32)


def kernel(**inputs):
    import concourse.bacc as bacc
    from concourse.bass_utils import run_bass_kernel_spmd

    a = {k: np.ascontiguousarray(v) for k, v in inputs.items()}

    def columns(v):
        return v.reshape(-1, P).T

    cc = np.stack([columns(a["c"]), columns(a["c_ctx"])], axis=2).reshape(P, 2 * KC)
    vecs = np.concatenate([columns(a["norm1_g"]), columns(a["norm2_g"]), columns(a["ada_b"]), columns(a["fnet_b"]), cc], axis=1)
    negated = (np.arange(D) // GW) * GW + (-np.arange(D)) % GW
    fnet_w = a["fnet_w"][0][negated].reshape(KC, P, KC, P).transpose(2, 1, 0, 3)
    pieces = a["ada_w"].reshape(DEPTH, KC, P, 6 * D // PIECE, PIECE).transpose(0, 3, 2, 1, 4)
    both = pieces[1, 0:4].reshape(4, P, 2, 4 * PIECE).transpose(0, 2, 1, 3)
    lat = pieces[1, 4:12].reshape(4, 2, P, 4, 2, PIECE).transpose(0, 3, 2, 4, 1, 5).reshape(4, 4, P, 4 * PIECE)
    units = np.concatenate([both, lat], axis=1)
    arrays = {
        "x": a["x"][0], "ctx": a["ctx"][0], "vecs": vecs, 
        "ada0": pieces[0], "ada1": units,
        "w1": a["mlp_w1"].reshape(DEPTH, KC, P, DFF // (2 * P), 2 * P).transpose(0, 3, 2, 1, 4),
        "w2": a["mlp_w2"].reshape(DEPTH, DFF // P, P, D),
        "fnet_w": fnet_w, "wqkv": a["attn_w_qkv"][0],
        "wo": a["attn_w_o"][0].reshape(KC, P, KC, P).transpose(2, 1, 0, 3),
        "qkg": np.broadcast_to(np.concatenate([a["attn_q_g"][0], a["attn_k_g"][0]]), (P, 2 * HD)),
        "sink": np.broadcast_to(a["attn_sink"][0], (P, HEADS)),
        "dft": dft_tables(), "rope": rope_tables(), "masks": band_masks(), "eye": np.eye(P, dtype=np.float32),
    }
    arrays = {k: np.ascontiguousarray(v) for k, v in arrays.items()}
    nc = bacc.Bacc("TRN2", target_bir_lowering=False, num_devices=1)
    args = [nc.dram_tensor(n, v.shape, mybir.dt.from_np(v.dtype), kind="ExternalInput").ap() for n, v in arrays.items()]
    out = nc.dram_tensor("out", (LAT, D), F32, kind="ExternalOutput").ap()
    park = nc.dram_tensor("park", (P, KC, LAT), F32, kind="Internal").ap()
    qd = nc.dram_tensor("queries", (QB, HEADS // 4, P, 4 * HD), F32, kind="Internal").ap()
    hybrid_kernel(nc, *args, out, park, qd)
    r = run_bass_kernel_spmd(nc, [arrays], core_ids=[0])
    return r.results[0]["out"].reshape(1, LAT, D)
```

```python
import numpy as np
import concourse.bass as bass
from concourse import mybir
from contextlib import ExitStack

F32 = mybir.dt.float32
F32R = mybir.dt.float32r
ALU = mybir.AluOpType
ACT = mybir.ActivationFunctionType
AX = mybir.AxisListType

P = 128
D = 1024
KC = D // P
LAT, CTX = 1024, 256
T = LAT + CTX
NT = T // P
DEPTH = 2
DFF = 4 * D
EPS = 1e-6
HD = 64
HEADS, KVH = 16, 2
QB = LAT // P
KEYS = 3 * P + CTX
GW = 256
BIG = 1e30
PRE = 64
BLOCKS = [(0, 512), (512, 512), (1024, 256)]

V_N1, V_N2, V_ADAB, V_FB, V_C = 0, 16, 32, 128, 136
V_ALL = 152
PIECE = 512
SH1, SC1, G1, SH2, SC2, G2 = range(6)


def f32(ap):
    return ap.bitcast(F32)


def mm3(pe, out, lhs, rhs, first, last):
    (lh, ll), (rh, rl) = lhs, rhs
    pe.matmul(out, lh, rh, start=first, stop=False)
    pe.matmul(out, lh, rl, start=False, stop=False)
    return pe.matmul(out, ll, rh, start=False, stop=last)


def lo_part(eng, lo, full, hi):
    return eng.tensor_tensor(lo, full, f32(hi), ALU.subtract)


def hybrid_kernel(nc, x, ctxt, vecs, ada0, ada1, w1, w2, fnet_w, wqkv, wo, qkg, sink, dft, rope, masks, eye, out, park, qd):
    ctx = ExitStack()
    with ctx:
        held = ExitStack()
        numbers = []

        def sem(name):
            s = held.enter_context(nc.semaphore(name))
            numbers.append(s.num)
            return s

        def recycle_semaphores():
            with nc.Block() as block:
                @block.gpsimd
                def _(pool):
                    pool.sem_clear(range(min(numbers), max(numbers) + 1))
            held.close()
            numbers.clear()

        def sb(name, shape, dt=F32, where=ctx):
            return where.enter_context(nc.sbuf_tensor(name, shape, dt))

        def banks(name, n, where):
            return [where.enter_context(nc.psum_tensor(f"{name}{i}", [P, 512], F32)) for i in range(n)]

        vec = sb("vec", [P, V_ALL])
        mod = sb("mod", [P, DEPTH, 6, KC, 2])
        g1b = sb("g1b", [P, KC, 2])
        svec = sb("svec", [P, KC, 2])
        ident = sb("ident", [P, P])
        meanw = sb("meanw", [P, P])
        eps = sb("eps", [P, 1])
        ones = sb("ones", [P, 1])
        rstd_tm = sb("rstd_tm", [P, NT])

        def shift(l, n, k, v):
            return mod[:, l, (SH1, SH2)[n], k, v:v + 1]

        def scale(l, n, k, v):
            return mod[:, l, (SC1, SC2)[n], k, v:v + 1]

        nh = sb("nh", [P, KC, T], F32R)
        nl = sb("nl", [P, KC, T], F32R)
        tables = ExitStack()
        tabh = sb("tabh", [P, 4, 2, 512], F32R, where=tables)
        tabl = sb("tabl", [P, 4, 2, 512], F32R, where=tables)
        xg = [sb(f"xg{i}", [P, NT, P], where=tables) for i in range(2)]

        RING = 2
        XS = 6
        PIECES = 2 * D // PIECE
        M = PIECE // P
        with ExitStack() as ph:
            wbuf = [sb(f"ada_w{i}", [P, KC, PIECE], where=ph) for i in range(RING)]
            rows = [sb(f"ada_row{i}", [2, PIECE], where=ph) for i in range(2)]
            xt = [sb(f"xt{i}", [P, D], where=ph) for i in range(XS)]
            xsq = sb("xsq", [P, D], where=ph)
            tabf = [sb(f"tabf{i}", [P, 2, 512], where=ph) for i in range(2)]
            sig = sb("sig", [P, KC, 2], where=ph)
            ssq = sb("ssq", [P, NT], where=ph)
            row_ps, col_ps = banks("ada_ps", 2, ph), banks("adac_ps", 1, ph)[0]
            s_small, s_eps, s_e, s_d, s_silu = sem("a_small"), sem("a_eps"), sem("a_exp"), sem("a_d"), sem("a_silu")
            s_w = [sem(f"a_w{i}") for i in range(RING)]
            s_x = [sem(f"a_x{i}") for i in range(XS)]
            s_xg = sem("a_xg")
            s_id, s_row, s_ev, s_col, s_ssq, s_std = sem("a_id"), sem("a_row"), sem("a_ev"), sem("a_col"), sem("a_ssq"), sem("a_std")
            s_th, s_tl = sem("a_tabh"), sem("a_tabl")
            s_tab = [sem(f"a_tab{i}") for i in range(2)]
            TAB_AT = (0, 1, 4, 6)
            with nc.Block() as block:
                @block.sync
                def _(sp):
                    sp.dma_start(vec[:], vecs).then_inc(s_small, 16)
                    for i in range(PIECES):
                        if i >= RING:
                            sp.wait_ge(s_row, i + 1 - RING)
                        sp.dma_start(wbuf[i % RING][:], ada0[i]).then_inc(s_w[i % RING], 16)
                        if i == 0:
                            sp.dma_start(ident[:], eye).then_inc(s_id, 16)
                    for i in range(2):
                        col = slice(i * P, (i + 1) * P)
                        sp.dma_start(xg[i][:, 0:QB, :], x.rearrange("(n p) d -> p n d", p=P)[:, :, col]).then_inc(s_xg, 16)
                        sp.dma_start(xg[i][:, QB:NT, :], ctxt.rearrange("(n p) d -> p n d", p=P)[:, :, col]).then_inc(s_xg, 16)
                    sp.wait_ge(s_xg, 64)

                @block.gpsimd
                def _(pool):
                    pool.memset(eps[:], EPS).then_inc(s_eps, 1)
                    pool.memset(meanw[:], 1.0 / D).then_inc(s_eps, 1)
                    pool.memset(ones[:], 1.0).then_inc(s_eps, 1)
                    for i in range(4):
                        if i >= 2:
                            pool.wait_ge(s_tl, i - 1)
                        pool.dma_start(tabf[i % 2][:], dft[i]).then_inc(s_tab[i % 2], 16)

                @block.scalar
                def _(act):
                    act.wait_ge(s_small, 16)
                    act.activation(sig[:], vec[:, V_C:V_C + 2 * KC], ACT.Exp, scale=-1.0).then_inc(s_e, 1)

                    def tile(t):
                        src = x[t * P:(t + 1) * P, :] if t < QB else ctxt[(t - QB) * P:(t + 1 - QB) * P, :]
                        act.dma_start(xt[t % XS][:], src).then_inc(s_x[t % XS], 16)
                    for t in range(XS):
                        tile(t)
                    for t in range(NT):
                        act.wait_ge(s_x[t % XS], 16 * (t // XS + 1))
                        if t:
                            act.wait_ge(s_ssq, t)
                        act.activation(xsq[:], xt[t % XS][:], ACT.Square, accum_out=ssq[:, t:t + 1]).then_inc(s_ssq, 1)
                        if t + XS < NT:
                            act.wait_ge(s_ssq, t + 1)
                            tile(t + XS)
                        if t in TAB_AT:
                            i = TAB_AT.index(t)
                            act.wait_ge(s_tab[i % 2], 16 * (i // 2 + 1))
                            act.activation(tabh[:, i], tabf[i % 2][:], ACT.Copy).then_inc(s_th, 1)
                    act.wait_ge(s_eps, 3)
                    act.wait_ge(s_ssq, NT)
                    act.activation(ssq[:], ssq[:], ACT.Sqrt, bias=eps[:], scale=1.0 / D).then_inc(s_std, 1)

                @block.vector
                def _(dve):
                    dve.wait_ge(s_e, 1)
                    dve.tensor_scalar_add(sig[:], sig[:], 1.0).then_inc(s_d, 1)
                    dve.wait_ge(s_d, 1)
                    dve.reciprocal(sig[:], sig[:]).then_inc(s_d, 1)
                    dve.wait_ge(s_d, 2)
                    dve.tensor_tensor(svec[:], sig[:], vec[:, V_C:V_C + 2 * KC].rearrange("p (k v) -> p k v", v=2),
                                      ALU.mult).then_inc(s_silu, 1)
                    for i in range(PIECES):
                        dve.wait_ge(s_th, i + 1)
                        lo_part(dve, tabl[:, i], tabf[i % 2][:], tabh[:, i]).then_inc(s_tl, 1)
                        dve.wait_ge(s_row, i + 1)
                        if i >= 2:
                            dve.wait_ge(s_col, i - 1)
                        dve.tensor_copy(rows[i % 2][:], row_ps[i % 2][0:2, :]).then_inc(s_ev, 1)
                    dve.wait_ge(s_std, 1)
                    dve.reciprocal(rstd_tm[:], ssq[:]).then_inc(s_d, 1)
                    dve.wait_ge(s_col, PIECES)
                    bias = vec[:, V_ADAB:V_ADAB + 2 * KC].rearrange("p (m v) -> p m v", v=1)
                    dve.tensor_tensor(mod[:, 0, 0:2].rearrange("p s k v -> p (s k) v"),
                                      col_ps[:, 0:4 * KC].rearrange("p (m v) -> p m v", v=2),
                                      bias.to_broadcast([P, 2 * KC, 2]), ALU.add).then_inc(s_d, 1)
                    dve.wait_ge(s_d, 4)
                    for v in range(2):
                        m = mod[:, 0, SC1, :, v]
                        dve.scalar_tensor_tensor(out=m, in0=m, scalar=1.0, in1=vec[:, V_N1:V_N1 + KC],
                                                 op0=ALU.add, op1=ALU.mult).then_inc(s_d, 1)

                @block.tensor
                def _(pe):
                    pe.wait_ge(s_silu, 1)

                    def columns(i):
                        pe.wait_ge(s_ev, i + 1)
                        for m in range(M):
                            c = 2 * (i * M + m)
                            last = pe.transpose(col_ps[:, c:c + 2], rows[i % 2][:, m * P:(m + 1) * P], ident[0:2, 0:2])
                        last.then_inc(s_col, 1)
                    for i in range(PIECES):
                        pe.wait_ge(s_w[i % RING], 16 * (i // RING + 1))
                        if i >= 2:
                            pe.wait_ge(s_ev, i - 1)
                        for k in range(KC):
                            last = pe.matmul(row_ps[i % 2][0:2, :], svec[:, k, :], wbuf[i % RING][:, k, :],
                                             start=(k == 0), stop=(k == KC - 1))
                        last.then_inc(s_row, 1)
                        if i == 0:
                            pe.wait_ge(s_id, 16)
                        else:
                            columns(i - 1)
                    columns(PIECES - 1)

        fnet_mix(nc, sem, sb, banks, x, ctxt, xg, tabh, tabl, rstd_tm, ada0, vec, svec, ident, mod, g1b, nh, nl)
        tables.close()
        with ExitStack() as layer0:
            ht = sb("ht0", [P, KC, T], where=layer0)
            fnet_out(nc, sem, sb, banks, x, ctxt, fnet_w, ada1, vec, svec, ones, mod, g1b, ident, nh, nl, ht)
            mlp(nc, sem, sb, banks, 0, 3, w1, w2, mod, meanw, eps, nh, nl, ht)
            norm_out(nc, sem, sb, banks, 1, park, mod, meanw, eps, nh, nl, ht)
        recycle_semaphores()
        with ExitStack() as att:
            kh = sb("kh", [P, KVH, (QB + 4) * P], F32R, where=att)
            kl = sb("kl", [P, KVH, (QB + 4) * P], F32R, where=att)
            vs = sb("vs", [P, QB + 4, KVH, 2 * HD], F32R, where=att)
            nsink = sb("nsink", [P, HEADS], where=att)
            qkv(nc, sem, sb, banks, wqkv, qkg, rope, sink, ident, eps, nh, nl, qd, kh, kl, vs, nsink)
            attention(nc, sem, sb, banks, masks, nsink, ident, qd, kh, kl, vs, nh, nl)
        ht = sb("ht1", [P, KC, LAT])
        attn_out(nc, sem, sb, banks, wo, park, mod, nh, nl, ht)
        mlp(nc, sem, sb, banks, 1, 2, w1, w2, mod, meanw, eps, nh, nl, ht, ident, out)


def fnet_mix(nc, sem, sb, banks, x, ctxt, xg, tabh, tabl, rstd_tm, ada0, vec, svec, ident, mod, g1b, nh, nl):
    GR = D // GW
    SETS = [([(0, 0)], 0, 0, 0), ([(1, 2)], 0, 256, 0), ([(2, 4), (3, 6)], 1, 0, 0), ([(0, 8)], 1, 256, 1)]
    FIXED = {0: 0, 3: 1}
    with ExitStack() as ph:
        xr = sb("xr", [P, NT * P], where=ph)
        sd = sb("sd", [P, 512], where=ph)
        gh = [sb(f"gh{i}", [P, NT, P], F32R, where=ph) for i in range(2)]
        gl = [sb(f"gl{i}", [P, NT, P], F32R, where=ph) for i in range(2)]
        uvh = sb("uvh", [P, 2, 2, 2, 512], F32R, where=ph)
        uvl = sb("uvl", [P, 2, 2, 2, 512], F32R, where=ph)
        uvf = [sb(f"uvf{i}", [P, 2, 256], where=ph) for i in range(2)]
        sdc = sb("sdc", [P, KC, 2], where=ph)
        gain = sb("gain", [P, 2, 2], where=ph)
        yt = sb("yt", [P, 512], where=ph)
        bt = sb("bt", [P, 256], where=ph)
        RING = 4
        UNITS = 2 * KC
        aw = [sb(f"maw{i}", [P, PIECE], where=ph) for i in range(RING)]
        rows = sb("mrows", [2, PIECE], where=ph)
        seq_ps, y_banks = banks("seq_ps", 4, ph), banks("y_ps", 2, ph)
        row_ps, col_ps = banks("mrow_ps", 2, ph)

        def y_ps(m, n):
            return y_banks[(3 * m + n) % 2]

        s_aw = [sem(f"m_aw{i}") for i in range(RING)]
        s_unit, s_row, s_col, s_mod = sem("m_unit"), sem("m_row"), sem("m_col"), sem("m_mod")
        s_c, s_gain = sem("m_sdc"), sem("m_gain")
        s_x = [sem(f"m_x{i}") for i in range(2)]
        s_xr, s_bf, s_g, s_gh, s_gl = sem("m_xr"), sem("m_butterfly"), sem("m_g"), sem("m_gh"), sem("m_gl")
        s_seq, s_uvf, s_fix, s_uvh, s_uvl = sem("m_seq"), sem("m_uvf"), sem("m_fix"), sem("m_uvh"), sem("m_uvl")
        s_y, s_bt, s_yt, s_yh, s_yl = sem("m_y"), sem("m_bt"), sem("m_yt"), sem("m_yh"), sem("m_yl")
        xv = x.rearrange("(n p) d -> p n d", p=P)
        cv = ctxt.rearrange("(n p) d -> p n d", p=P)

        def schedule(eng, prep, sets, y_out):
            prep(0, 0)
            prep(0, 1)
            with eng.Fori(0, GR - 1) as g:
                for i in range(2):
                    sets(g, i)
                    prep(g + 1, i)
                y_out(g)
            for i in range(2):
                sets(GR - 1, i)
            y_out(GR - 1)

        with nc.Block() as block:
            @block.gpsimd
            def _(pool):
                for s in (s_unit, s_row, s_col, s_xr, s_gl, s_seq, s_uvf, s_uvl, s_y, s_yt, s_yl):
                    pool.sem_inc(s, PRE)
                pool.wait_ge(s_xr, PRE + 1)
                with pool.Fori(0, GR) as g:
                    for q in range(UNITS):
                        pool.wait_ge(s_unit, g * UNITS + (PRE + q + 1 - RING))
                        pool.dma_start(aw[q % RING][:], ada0[bass.ds(g * 2 + (4 + q // KC), 1), :, q % KC]
                                       .rearrange("a p n -> p (a n)")).then_inc(s_aw[q % RING], 16)

            @block.sync
            def _(sp):
                with sp.Fori(1, GR) as g:
                    for i in range(2):
                        sp.wait_ge(s_xr, g * 2 + (PRE + i - 1))
                        col = bass.ds(g * GW + i * P, P)
                        sp.dma_start(xg[i][:, 0:QB, :], xv[:, :, col]).then_inc(s_x[i], 16)
                        sp.dma_start(xg[i][:, QB:NT, :], cv[:, :, col]).then_inc(s_x[i], 16)

            @block.scalar
            def _(act):
                for v, n in ((0, LAT), (1, CTX)):
                    act.activation(sdc[:, :, v], mod[:, 0, SH1, :, v], ACT.Copy, scale=float(n)).then_inc(s_c, 1)
                def prep(g, i):
                    act.wait_ge(s_g, g * 2 + (i + 1))
                    act.wait_ge(s_seq, g * 8 + (PRE + 4 * i - 4))
                    act.activation(gh[i][:].rearrange("p n c -> p (n c)"), xr[:], ACT.Copy).then_inc(s_gh, 1)

                def sets(g, i):
                    if i == 0:
                        act.wait_ge(s_gain, g + 1)
                        act.wait_ge(s_y, g * 6 + PRE)
                    for j, (_, b, off, v) in enumerate(SETS):
                        u = i * 4 + j
                        act.wait_ge(s_seq, g * 8 + (PRE + u + 1))
                        act.wait_ge(s_uvl, g * 8 + (PRE + u - 1))
                        act.activation(uvf[u % 2][:].rearrange("p a s -> p (a s)"), seq_ps[j][:], ACT.Copy,
                                       scale=gain[:, i, v:v + 1]).then_inc(s_uvf, 1)
                        if j in FIXED:
                            act.wait_ge(s_fix, g * 4 + (i * 2 + v + 1))
                        else:
                            act.wait_ge(s_uvf, g * 8 + (PRE + u + 1))
                        act.activation(uvh[:, b, i, :, off:off + 256], uvf[u % 2][:], ACT.Copy).then_inc(s_uvh, 1)

                def ada_rows(g, piece):
                    act.wait_ge(s_unit, g * UNITS + (PRE + KC * (piece + 1)))
                    act.wait_ge(s_col, g * 2 + (PRE + piece))
                    act.activation(rows[:], row_ps[0:2, :], ACT.Copy).then_inc(s_row, 1)

                def y_out(g):
                    ada_rows(g, 0)
                    for m in range(2):
                        chunk = nh[:, bass.ds(g * 2 + m, 1), :].rearrange("p a s -> p (a s)")
                        dst = chunk[:, 0:LAT].rearrange("p (s f) -> p f s", f=4)
                        act.wait_ge(s_y, g * 6 + (PRE + 3 * m + 1))
                        act.activation(dst[:, 0::2, :], y_ps(m, 0)[:].rearrange("p (a s) -> p a s", a=2), ACT.Copy,
                                       scale=2.0 ** -9).then_inc(s_yh, 1)
                        act.wait_ge(s_y, g * 6 + (PRE + 3 * m + 2))
                        act.wait_ge(s_yt, g * 2 + (PRE + m))
                        act.activation(bt[:], y_ps(m, 1)[:, 256:512], ACT.Copy).then_inc(s_bt, 1)
                        act.wait_ge(s_yt, g * 2 + (PRE + m + 1))
                        act.activation(dst[:, 1, :], yt[:, 0:256], ACT.Copy, scale=2.0 ** -9)
                        act.activation(dst[:, 3, :], yt[:, 256:512], ACT.Copy, scale=2.0 ** -9).then_inc(s_yh, 1)
                        if m == 1:
                            ada_rows(g, 1)
                        act.wait_ge(s_y, g * 6 + (PRE + 3 * m + 3))
                        act.activation(chunk[:, LAT:T], y_ps(m, 2)[:, 0:256], ACT.Copy, scale=2.0 ** -8).then_inc(s_yh, 1)

                schedule(act, prep, sets, y_out)

            @block.vector
            def _(dve):
                dve.wait_ge(s_c, 2)
                def prep(g, i):
                    if not isinstance(g, int):
                        dve.wait_ge(s_x[i], g * 32)
                    dve.wait_ge(s_gl, g * 2 + (PRE + i))
                    dve.tensor_tensor(xr[:].rearrange("p (n c) -> p n c", n=NT), xg[i][:],
                                      rstd_tm[:].rearrange("p (n c) -> p n c", c=1).to_broadcast([P, NT, P]),
                                      ALU.mult).then_inc(s_xr, 1)
                    dve.wait_ge(s_xr, g * 2 + (PRE + i + 1))
                    dve.tensor_tensor(sd[:], xr[:, 0:512], xr[:, 512:1024], ALU.add)
                    dve.tensor_tensor(xr[:, 512:1024], xr[:, 0:512], xr[:, 512:1024], ALU.subtract).then_inc(s_bf, 1)
                    dve.wait_ge(s_bf, g * 2 + (i + 1))
                    dve.tensor_tensor(xr[:, 0:256], sd[:, 0:256], sd[:, 256:512], ALU.add)
                    dve.tensor_tensor(xr[:, 256:512], sd[:, 0:256], sd[:, 256:512], ALU.subtract).then_inc(s_g, 1)
                    dve.wait_ge(s_gh, g * 2 + (i + 1))
                    lo_part(dve, gl[i][:].rearrange("p n c -> p (n c)"), xr[:],
                            gh[i][:].rearrange("p n c -> p (n c)")).then_inc(s_gl, 1)

                def sets(g, i):
                    if i == 0:
                        dve.wait_ge(s_uvf, g * 8 + PRE)
                        dve.tensor_copy(gain[:], mod[:, 0, SC1, bass.ds(g * 2, 2), :]).then_inc(s_gain, 1)
                    for j, (_, b, off, v) in enumerate(SETS):
                        u = i * 4 + j
                        dve.wait_ge(s_uvf, g * 8 + (PRE + u + 1))
                        if j in FIXED:
                            c0 = uvf[u % 2][:, 0, 0:1]
                            dve.tensor_tensor(c0, c0, sdc[:, bass.ds(g * 2 + i, 1), v], ALU.add).then_inc(s_fix, 1)
                        dve.wait_ge(s_uvh, g * 8 + (u + 1))
                        lo_part(dve, uvl[:, b, i, :, off:off + 256], uvf[u % 2][:],
                                uvh[:, b, i, :, off:off + 256]).then_inc(s_uvl, 1)

                def y_out(g):
                    for m in range(2):
                        lo = nl[:, bass.ds(g * 2 + m, 1), :].rearrange("p a s -> p (a s)")
                        hi = f32(nh[:, bass.ds(g * 2 + m, 1), :]).rearrange("p a s -> p (a s)")
                        dlo, dhi = (a[:, 0:LAT].rearrange("p (s f) -> p f s", f=4) for a in (lo, hi))
                        dve.wait_ge(s_yh, g * 6 + (3 * m + 1))
                        dve.scalar_tensor_tensor(out=dlo[:, 0::2, :], in0=y_ps(m, 0)[:].rearrange("p (a s) -> p a s", a=2),
                                                 scalar=2.0 ** -9, in1=dhi[:, 0::2, :],
                                                 op0=ALU.mult, op1=ALU.subtract).then_inc(s_yl, 1)
                        dve.wait_ge(s_bt, g * 2 + (m + 1))
                        dve.wait_ge(s_yl, g * 6 + (PRE + 3 * m - 1))
                        dve.tensor_tensor(yt[:, 0:256], y_ps(m, 1)[:, 0:256], bt[:], ALU.add)
                        dve.tensor_tensor(yt[:, 256:512][:, ::-1], y_ps(m, 1)[:, 0:256], bt[:], ALU.subtract).then_inc(s_yt, 1)
                        dve.wait_ge(s_yh, g * 6 + (3 * m + 2))
                        dve.scalar_tensor_tensor(out=dlo[:, 1, :], in0=yt[:, 0:256], scalar=2.0 ** -9, in1=dhi[:, 1, :],
                                                 op0=ALU.mult, op1=ALU.subtract)
                        dve.scalar_tensor_tensor(out=dlo[:, 3, :], in0=yt[:, 256:512], scalar=2.0 ** -9,
                                                 in1=dhi[:, 3, :], op0=ALU.mult, op1=ALU.subtract).then_inc(s_yl, 1)
                        dve.wait_ge(s_yh, g * 6 + (3 * m + 3))
                        dve.scalar_tensor_tensor(out=lo[:, LAT:T], in0=y_ps(m, 2)[:, 0:256], scalar=2.0 ** -8,
                                                 in1=hi[:, LAT:T], op0=ALU.mult, op1=ALU.subtract).then_inc(s_yl, 1)
                schedule(dve, prep, sets, y_out)
                dve.wait_ge(s_col, PRE + 2 * GR)
                bias = vec[:, V_ADAB + 2 * KC:V_ADAB + 6 * KC].rearrange("p (m v) -> p m v", v=1)
                dve.tensor_tensor(mod[:, 0, 2:6].rearrange("p s k v -> p (s k) v"),
                                  col_ps[:, 0:8 * KC].rearrange("p (m v) -> p m v", v=2),
                                  bias.to_broadcast([P, 4 * KC, 2]), ALU.add).then_inc(s_mod, 1)
                dve.wait_ge(s_mod, 1)
                for v in range(2):
                    m = mod[:, 0, SC2, :, v]
                    dve.scalar_tensor_tensor(out=m, in0=m, scalar=1.0, in1=vec[:, V_N2:V_N2 + KC],
                                             op0=ALU.add, op1=ALU.mult).then_inc(s_mod, 1)
                    dve.tensor_tensor(g1b[:, :, v], mod[:, 0, G1, :, v], vec[:, V_FB:V_FB + KC], ALU.mult).then_inc(s_mod, 1)

            @block.tensor
            def _(pe):
                def ada(g, units):
                    for q in units:
                        piece, k = divmod(q, KC)
                        pe.wait_ge(s_aw[q % RING], g * (16 * UNITS // RING) + 16 * (q // RING + 1))
                        if k == 0:
                            pe.wait_ge(s_row, g * 2 + (PRE + piece))
                        pe.matmul(row_ps[0:2, :], svec[:, k, :], aw[q % RING][:], start=(k == 0), stop=(k == KC - 1)).then_inc(s_unit, 1)

                def ada_columns(g, piece):
                    pe.wait_ge(s_row, g * 2 + (PRE + piece + 1))
                    for m in range(PIECE // P):
                        last = pe.matmul(col_ps[:, bass.ds(g * 16 + (8 * piece + 2 * m), 2)],
                                         rows[:, m * P:(m + 1) * P], ident[0:2, 0:2], start=True, stop=True)
                    last.then_inc(s_col, 1)

                def token_sums(g, i, ada_g=None, q0=0, per=0):
                    pe.wait_ge(s_gl, g * 2 + (PRE + i + 1))
                    for j, (prods, b, off, v) in enumerate(SETS):
                        pe.wait_ge(s_uvf, g * 8 + (PRE + 4 * i + j - 3))
                        terms = [(tab, tile, kt) for tab, tile in prods for kt in range(2)]
                        for n, (tab, tile, kt) in enumerate(terms):
                            last = mm3(pe, seq_ps[j][:], (gh[i][:, tile + kt, :], gl[i][:, tile + kt, :]),
                                       (tabh[:, tab, kt, :], tabl[:, tab, kt, :]), n == 0, n == len(terms) - 1)
                        last.then_inc(s_seq, 1)
                        if per:
                            ada(ada_g, range(q0 + j * per, q0 + (j + 1) * per))

                def feature_sums(g):
                    pe.wait_ge(s_uvl, g * 8 + (PRE + 8))
                    TERMS = [(cs, kt) for cs in range(2) for kt in range(2)]
                    for m in range(2):
                        def tab(cs, kt):
                            cols = slice(256 * cs + m * P, 256 * cs + (m + 1) * P)
                            return tabh[:, 0, kt, cols], tabl[:, 0, kt, cols]

                        def uv(b, kt, cs, lo, hi):
                            return uvh[:, b, kt, cs, lo:hi], uvl[:, b, kt, cs, lo:hi]
                        pe.wait_ge(s_yt, g * 2 + (PRE + m))
                        for n, (cs, kt) in enumerate(TERMS):
                            last = mm3(pe, y_ps(m, 0)[:], tab(cs, kt), uv(0, kt, cs, 0, 512), n == 0, n == 3)
                        last.then_inc(s_y, 1)
                        ada(g, (8, 9) if m == 0 else (14,))
                        pe.wait_ge(s_yl, g * 6 + (PRE + 3 * m))
                        for cs, kt in TERMS:
                            last = mm3(pe, y_ps(m, 1)[:, 256 * cs:256 * cs + 256], tab(cs, kt), uv(1, kt, cs, 0, 256),
                                       kt == 0, kt == 1)
                        last.then_inc(s_y, 1)
                        ada(g, (10, 11) if m == 0 else (15,))
                        pe.wait_ge(s_yl, g * 6 + (PRE + 3 * m + 1))
                        for n, (cs, kt) in enumerate(TERMS):
                            last = mm3(pe, y_ps(m, 2)[:, 0:256], tab(cs, kt), uv(1, kt, cs, 256, 512), n == 0, n == 3)
                        last.then_inc(s_y, 1)
                        if m == 0:
                            ada(g, (12, 13))
                        ada_columns(g, m)

                token_sums(0, 0)
                with pe.Fori(0, GR - 1) as g:
                    token_sums(g, 1, g, 0, 1)
                    token_sums(g + 1, 0, g, 4, 1)
                    feature_sums(g)
                token_sums(GR - 1, 1, GR - 1, 0, 2)
                feature_sums(GR - 1)


def fnet_out(nc, sem, sb, banks, x, ctxt, fnet_w, ada1, vec, svec, ones, mod, g1b, ident, nh, nl, ht):
    UNITS, SLOTS, UW = 6, 3, 4 * PIECE
    M = PIECE // P
    STEPS = [(u, kk, c) for u in range(UNITS) for kk in range(4 if u < 2 else 2) for c in range(2)]
    NS = len(STEPS)
    STEPS_TO = [sum(1 for s in STEPS if s[0] <= u) for u in range(UNITS)]
    with ExitStack() as ph:
        wf = [sb(f"fw{i}", [P, KC, P], where=ph) for i in range(2)]
        wh = [sb(f"fwh{i}", [P, KC, P], F32R, where=ph) for i in range(2)]
        wl = [sb(f"fwl{i}", [P, KC, P], F32R, where=ph) for i in range(2)]
        yb = [sb(f"fy{i}", [P, 512], where=ph) for i in range(3)]
        gate, bias = sb("gate", [P, 2, 2], where=ph), sb("gbias", [P, 2, 2], where=ph)
        aw = [sb(f"aw{i}", [P, UW], where=ph) for i in range(SLOTS)]
        XS = 4
        X_FIRST = 4
        xt = [sb(f"fx{i}", [P, D], where=ph) for i in range(XS)]
        acc = sb("ada_acc", [P, 2, 2, PIECE], where=ph)
        tr_ps, o_ps = banks("tr_ps", 4, ph), banks("o_ps", 3, ph)
        ada_ps = banks("ada1_ps", 1, ph)[0]
        s_aw = [sem(f"o_aw{i}") for i in range(SLOTS)]
        s_st, s_red, s_m = sem("o_ada_step"), sem("o_ada_reduced"), sem("o_ada_mod")
        s_gate = sem("o_gate")
        s_x = [sem(f"o_x{i}") for i in range(XS)]
        s_w = [sem(f"o_w{i}") for i in range(2)]
        s_wh, s_wl, s_tr, s_eva, s_evd, s_o, s_yb, s_add = (sem(n) for n in (
            "o_wh", "o_wl", "o_tr", "o_ev_act", "o_ev_dve", "o_prod", "o_yb", "o_add"))
        with nc.Block() as block:
            @block.gpsimd
            def _(pool):
                for s in (s_wl, s_o, s_yb, s_add, s_st, s_red):
                    pool.sem_inc(s, PRE)
                pool.wait_ge(s_tr, 2 * X_FIRST)
                with pool.Fori(0, KC // 2) as r:
                    for u in range(UNITS):
                        pool.wait_ge(s_st, r * NS + (PRE + (STEPS_TO[u - SLOTS] if u >= SLOTS else STEPS_TO[u + UNITS - SLOTS] - NS)))
                        pool.dma_start(aw[u % SLOTS][:], ada1[bass.ds(r, 1), u].rearrange("a p n -> p (a n)")).then_inc(s_aw[u % SLOTS], 16)

            @block.sync
            def _(sp):
                def weights(c, i):
                    sp.dma_start(wf[i][:], fnet_w[c].rearrange("a p k n -> p (a k) n")).then_inc(s_w[i], 16)
                weights(slice(0, 1), 0)
                for t in range(NT):
                    if t >= XS:
                        sp.wait_ge(s_tr, 2 * (t - XS + 1))
                    src = x[t * P:(t + 1) * P, :] if t < QB else ctxt[(t - QB) * P:(t - QB + 1) * P, :]
                    sp.dma_start(xt[t % XS][:], src).then_inc(s_x[t % XS], 16)
                    if t == XS - 1:
                        weights(slice(1, 2), 1)
                with sp.Fori(1, KC // 2) as r:
                    for i in range(2):
                        sp.wait_ge(s_wl, r * 2 + (PRE + i - 1))
                        weights(bass.ds(r * 2 + i, 1), i)

            @block.scalar
            def _(act):
                def tiles(t0, n):
                    for t in range(t0 // P, (t0 + n) // P):
                        act.wait_ge(s_tr, 2 * t + 1)
                        act.activation(ht[:, 0:4, t * P:(t + 1) * P], tr_ps[2 * (t % 2)][:].rearrange("p (k c) -> p k c", k=4),
                                       ACT.Copy).then_inc(s_eva, 1)

                def high(r, i):
                    act.wait_ge(s_w[i % 2], r * 16 + 16 * (i // 2 + 1))
                    act.wait_ge(s_o, r * 6 + (PRE + 3 * i - 3))
                    act.activation(wh[i % 2][:], wf[i % 2][:], ACT.Copy).then_inc(s_wh, 1)

                def pair(r, more, start=False):
                    act.wait_ge(s_gate, r + 1)
                    for i in range(2):
                        for b, (t0, n) in enumerate(BLOCKS):
                            if start and i == 0:
                                tiles(t0, n)
                            act.wait_ge(s_o, r * 6 + (PRE + 3 * i + b + 1))
                            act.wait_ge(s_add, r * 6 + (PRE + 3 * i + b - 2))
                            v = int(t0 >= LAT)
                            act.activation(yb[b][:, 0:n], o_ps[b][:, 0:n], ACT.Identity, scale=gate[:, i, v:v + 1],
                                           bias=bias[:, i, v:v + 1]).then_inc(s_yb, 1)
                            if b == 0 and (more or i == 0):
                                high(r, i + 1)
                high(0, 0)
                pair(0, True, start=True)
                with act.Fori(1, KC // 2 - 1) as r:
                    pair(r, True)
                pair(KC // 2 - 1, False)

            @block.vector
            def _(dve):
                def tiles(t0, n):
                    for t in range(t0 // P, (t0 + n) // P):
                        dve.wait_ge(s_tr, 2 * t + 2)
                        dve.tensor_copy(ht[:, 4:8, t * P:(t + 1) * P],
                                        tr_ps[2 * (t % 2) + 1][:].rearrange("p (k c) -> p k c", k=4)).then_inc(s_evd, 1)
                    dve.wait_ge(s_evd, (t0 + n) // P)
                    dve.wait_ge(s_eva, (t0 + n) // P)

                def ada_steps(r, i0, i1):
                    for i in range(i0, i1):
                        u, kk, c = STEPS[i]
                        grp = int(u >= 2)
                        k = 4 * u + kk if u < 2 else 2 * (u - 2) + kk
                        w = aw[u % SLOTS][:, kk * PIECE:(kk + 1) * PIECE] if grp == 0 else \
                            aw[u % SLOTS][:, (2 * kk + c) * PIECE:(2 * kk + c + 1) * PIECE]
                        s = svec[:, k, 0:1] if grp else svec[:, k, c:c + 1]
                        if kk == 0 and c == 0:
                            dve.wait_ge(s_aw[u % SLOTS], r * (16 * UNITS // SLOTS) + 16 * (u // SLOTS + 1))
                        if k == 0:
                            dve.wait_ge(s_red, r * 2 + (PRE + grp - 1))
                            dve.tensor_scalar_mul(acc[:, grp, c], w, s).then_inc(s_st, 1)
                        else:
                            dve.wait_ge(s_st, r * NS + (PRE + i - 1))
                            dve.scalar_tensor_tensor(out=acc[:, grp, c], in0=w, scalar=s, in1=acc[:, grp, c],
                                                     op0=ALU.mult, op1=ALU.add).then_inc(s_st, 1)

                def low(r, i):
                    dve.wait_ge(s_wh, r * 2 + (i + 1))
                    lo_part(dve, wl[i % 2][:], wf[i % 2][:], wh[i % 2][:]).then_inc(s_wl, 1)

                def pair(r, more, start=False):
                    dve.wait_ge(s_yb, r * 6 + PRE)
                    dve.tensor_copy(gate[:], mod[:, 0, G1, bass.ds(r * 2, 2), :])
                    dve.tensor_copy(bias[:], g1b[:, bass.ds(r * 2, 2), :]).then_inc(s_gate, 1)
                    for i in range(2):
                        if not start or i:
                            ada_steps(r, i * NS // 2, i * NS // 2 + NS // 4)
                        for b, (t0, n) in enumerate(BLOCKS):
                            if start and i == 0:
                                tiles(t0, n)
                                if b:
                                    ada_steps(r, (b - 1) * NS // 4, b * NS // 4)
                            dve.wait_ge(s_yb, r * 6 + (PRE + 3 * i + b + 1))
                            h = ht[:, bass.ds(r * 2 + i, 1), t0:t0 + n].rearrange("p a s -> p (a s)")
                            dve.tensor_tensor(h, h, yb[b][:, 0:n], ALU.add).then_inc(s_add, 1)
                            if b == 0:
                                if more or i == 0:
                                    low(r, i + 1)
                                if not start or i:
                                    ada_steps(r, i * NS // 2 + NS // 4, (i + 1) * NS // 2)
                low(0, 0)
                pair(0, True, start=True)
                with dve.Fori(1, KC // 2 - 1) as r:
                    pair(r, True)
                pair(KC // 2 - 1, False)
                dve.wait_ge(s_red, PRE + 2 * (KC // 2))
                ada_b = vec[:, V_ADAB + 6 * KC:V_ADAB + 12 * KC]
                both = 2 * KC
                dve.tensor_tensor(mod[:, 1, 0:2].rearrange("p s k v -> p (s k) v"),
                                  ada_ps[:, 0:2 * both].rearrange("p (m v) -> p m v", v=2),
                                  ada_b[:, 0:both].rearrange("p (m v) -> p m v", v=1).to_broadcast([P, both, 2]), ALU.add).then_inc(s_m, 1)
                dve.tensor_tensor(mod[:, 1, 2:6, :, 0].rearrange("p s k -> p (s k)"), ada_ps[:, 2 * both:2 * both + 4 * KC],
                                  ada_b[:, both:], ALU.add).then_inc(s_m, 1)
                dve.wait_ge(s_m, 2)
                for which, col, v in ((SC1, V_N1, 0), (SC1, V_N1, 1), (SC2, V_N2, 0)):
                    m = mod[:, 1, which, :, v]
                    dve.scalar_tensor_tensor(out=m, in0=m, scalar=1.0, in1=vec[:, col + KC:col + 2 * KC],
                                             op0=ALU.add, op1=ALU.mult).then_inc(s_m, 1)

            @block.tensor
            def _(pe):
                def tiles(t0, n):
                    for t in range(t0 // P, (t0 + n) // P):
                        pe.wait_ge(s_x[t % XS], 16 * (t // XS + 1))
                        if t >= 2:
                            pe.wait_ge(s_eva, t - 1)
                            pe.wait_ge(s_evd, t - 1)
                        for half in range(2):
                            for k in range(4):
                                kk = 4 * half + k
                                last = pe.transpose(tr_ps[2 * (t % 2) + half][:, k * P:(k + 1) * P],
                                                    xt[t % XS][:, kk * P:(kk + 1) * P], ident[:])
                            last.then_inc(s_tr, 1)

                def reduce(r, i):
                    pe.wait_ge(s_st, r * NS + (PRE + (i + 1) * NS // 2))
                    for m in range(M):
                        for c in range(2):
                            if i == 0:
                                col = ada_ps[:, bass.ds(r * (2 * M) + (2 * m + c), 1)]
                            else:
                                col = ada_ps[:, bass.ds(r * (2 * M) + (4 * KC + c * M + m), 1)]
                            last = pe.matmul(col, acc[:, i, c, m * P:(m + 1) * P], ones[:], start=True, stop=True)
                    last.then_inc(s_red, 1)

                def pair(r, start=False):
                    for i in range(2):
                        pe.wait_ge(s_wl, r * 2 + (PRE + i + 1))
                        for b, (t0, n) in enumerate(BLOCKS):
                            if start and i == 0:
                                tiles(t0, n)
                            pe.wait_ge(s_yb, r * 6 + (PRE + 3 * i + b - 2))
                            for k in range(KC):
                                last = mm3(pe, o_ps[b][:, 0:n], (wh[i][:, k, :], wl[i][:, k, :]),
                                           (nh[:, k, t0:t0 + n], nl[:, k, t0:t0 + n]), k == 0, k == KC - 1)
                            last.then_inc(s_o, 1)
                            if start and i and b == 1:
                                reduce(r, 0)
                        if not start or i:
                            reduce(r, i)
                pair(0, start=True)
                with pe.Fori(1, KC // 2) as r:
                    pair(r)


def mlp(nc, sem, sb, banks, layer, nblocks, w1, w2, mod, meanw, eps, nh, nl, ht, ident=None, out=None):
    PAIRS = DFF // (2 * P)
    TB = BLOCKS[:nblocks]
    NB = nblocks
    N = f"l{layer}_"
    U1, U2 = 2 * NB, KC * NB
    NZ = 3 if NB == 3 else 4
    RMS_AT = 5
    SQ = 4
    with ExitStack() as ph:
        ah = sb(N + "ah", [P, 2, T], F32R, where=ph)
        al = sb(N + "al", [P, 2, T], F32R, where=ph)
        w1f, w2f = sb(N + "w1f", [P, KC, 2 * P], where=ph), sb(N + "w2f", [P, 2, D], where=ph)
        w1h, w2h = sb(N + "w1h", [P, KC, 2 * P], F32R, where=ph), sb(N + "w2h", [P, 2, D], F32R, where=ph)
        w1l, w2l = sb(N + "w1l", [P, KC, 2 * P], F32R, where=ph), sb(N + "w2l", [P, 2, D], F32R, where=ph)
        rel = [sb(f"{N}rel{i}", [P, 512], where=ph) for i in range(2)]
        sq = [sb(f"{N}sq{i}", [P, 512], where=ph) for i in range(2)]
        rb = [sb(f"{N}rb{i}", [P, 512], where=ph) for i in range(2)]
        z_ps, y_ps = banks(N + "z_ps", NZ, ph), banks(N + "yy_ps", 4, ph)
        ms_ps = y_ps
        psq = [w2f[:].rearrange("p c n -> p (c n)")[:, i * 512:(i + 1) * 512] for i in range(SQ)]
        s_w1, s_w2 = sem(N + "w1"), sem(N + "w2")
        OB = 4
        ob = [w1f[:].rearrange("p k n -> p (k n)")[:, i * D:(i + 1) * D] for i in range(2)] + [w2f[:, i] for i in range(2)]
        s_tr, s_oa, s_od = (sem(N + n) for n in ("otr", "oact", "odve"))
        s_out = [sem(f"{N}out{i}") for i in range(OB)]
        LOOPED = PAIRS - 1 if out is not None else PAIRS
        s_psq = sem(N + "npsq")
        s_sq, s_ms, s_std, s_rb, s_t, s_n, s_nh, s_nl = (sem(N + n) for n in ("nsq", "nms", "nstd", "nrb", "nt", "nn", "nnh", "nnl"))
        s_w1h, s_w1l, s_w2h, s_w2l = (sem(N + n) for n in ("w1h", "w1l", "w2h", "w2l"))
        s_z, s_rel, s_ah, s_al, s_sqr, s_y, s_acc = (sem(N + n) for n in ("z", "rel", "ah", "al", "sqr", "y", "acc"))
        with nc.Block() as block:
            @block.sync
            def _(sp):
                def load1(p, row):
                    sp.wait_ge(s_w1l, p + PRE)
                    sp.dma_start(w1f[:], w1[layer, row].rearrange("a p k n -> p (a k) n")).then_inc(s_w1, 16)

                def load2(p, rows):
                    sp.wait_ge(s_w2l, p + PRE)
                    sp.dma_start(w2f[:], w2[layer, rows].rearrange("c p n -> p c n")).then_inc(s_w2, 16)
                load1(0, slice(0, 1))
                sp.wait_ge(s_ms, NB * KC)
                load2(0, slice(0, 2))
                with sp.Fori(1, PAIRS) as p:
                    load1(p, bass.ds(p, 1))
                    load2(p, bass.ds(p * 2, 2))
                if out is not None:
                    for t in range(QB):
                        sp.wait_ge(s_oa, t + 1)
                        sp.wait_ge(s_od, t + 1)
                        sp.dma_start(out[t * P:(t + 1) * P, :], ob[t % OB]).then_inc(s_out[t % OB], 16)
                    for i in range(OB):
                        sp.wait_ge(s_out[i], 16 * QB // OB)

            @block.gpsimd
            def _(pool):
                for s in (s_w1l, s_w2l, s_z, s_rel, s_al, s_y, s_acc):
                    pool.sem_inc(s, PRE)

                def low1(p):
                    pool.wait_ge(s_w1h, p + 1)
                    lo_part(pool, w1l[:], w1f[:], w1h[:]).then_inc(s_w1l, 1)

                def low2(p):
                    pool.wait_ge(s_w2h, p + 1)
                    lo_part(pool, w2l[:], w2f[:], w2h[:]).then_inc(s_w2l, 1)
                v = 0
                for b, (t0, n) in list(enumerate(TB))[1:]:
                    for k in range(KC):
                        if v >= SQ:
                            pool.wait_ge(s_ms, KC + v - SQ + 1)
                        pool.tensor_tensor(psq[v % SQ][:, 0:n], ht[:, k, t0:t0 + n], ht[:, k, t0:t0 + n], ALU.mult).then_inc(s_psq, 1)
                        v += 1
                        if v == KC - 2:
                            low1(0)
                low2(0)
                with pool.Fori(1, PAIRS) as p:
                    low1(p)
                    low2(p)

            @block.scalar
            def _(act):
                def high1(p):
                    act.wait_ge(s_w1, p * 16 + 16)
                    act.wait_ge(s_z, p * U1 + PRE)
                    act.activation(w1h[:], w1f[:], ACT.Copy).then_inc(s_w1h, 1)

                def high2(p):
                    act.wait_ge(s_w2, p * 16 + 16)
                    act.wait_ge(s_y, p * U2 + PRE)
                    act.activation(w2h[:], w2f[:], ACT.Copy).then_inc(s_w2h, 1)

                def hidden(p, u):
                    b, c = divmod(u, 2)
                    t0, n = TB[b]
                    act.wait_ge(s_z, p * U1 + (PRE + u + 1))
                    act.wait_ge(s_al, p * U1 + (PRE + u - 1))
                    act.activation(rel[u % 2][:, 0:n], z_ps[u % NZ][:, 0:n], ACT.Relu).then_inc(s_rel, 1)
                    act.wait_ge(s_rel, p * U1 + (PRE + u + 1))
                    act.activation(ah[:, c, t0:t0 + n], rel[u % 2][:, 0:n], ACT.Square).then_inc(s_ah, 1)

                def rms(b):
                    n = TB[b][1]
                    act.wait_ge(s_ms, (b + 1) * KC)
                    if b >= 2:
                        act.wait_ge(s_t, (b - 1) * KC)
                    act.activation(rb[b % 2][:, 0:n], ms_ps[b][:, 0:n], ACT.Sqrt, bias=eps[:]).then_inc(s_std, 1)

                def norm(b):
                    t0, n = TB[b]
                    v = int(t0 >= LAT)
                    for k in range(KC):
                        u = b * KC + k
                        act.wait_ge(s_t, u + 1)
                        act.activation(sq[k % 2][:, 0:n], sq[k % 2][:, 0:n], ACT.Identity, scale=mod[:, layer, SC2, k, v:v + 1],
                                       bias=mod[:, layer, SH2, k, v:v + 1]).then_inc(s_n, 1)
                        act.wait_ge(s_n, u + 1)
                        act.activation(nh[:, k, t0:t0 + n], sq[k % 2][:, 0:n], ACT.Copy).then_inc(s_nh, 1)
                        if k == RMS_AT and b + 1 < NB:
                            rms(b + 1)
                t0, n = TB[0]
                for k in range(KC):
                    if k >= 2:
                        act.wait_ge(s_ms, k - 1)
                    act.activation(rel[k % 2][:, 0:n], ht[:, k, t0:t0 + n], ACT.Square).then_inc(s_sq, 1)
                rms(0)
                high1(0)
                norm(0)
                norm(1)
                high2(0)
                for b in range(NB):
                    hidden(0, 2 * b)
                    hidden(0, 2 * b + 1)
                    if b == 0 and NB > 2:
                        norm(2)
                with act.Fori(1, LOOPED) as p:
                    high1(p)
                    high2(p)
                    for u in range(U1):
                        hidden(p, u)
                if out is not None:
                    high1(LOOPED)
                    high2(LOOPED)
                    for u in range(U1):
                        hidden(LOOPED, u)
                    act.wait_ge(s_w1l, PRE + PAIRS)
                    act.wait_ge(s_w2l, PRE + PAIRS)
                    for t in range(QB):
                        if t >= OB:
                            act.wait_ge(s_out[t % OB], 16 * (t // OB))
                        act.wait_ge(s_tr, 2 * t + 1)
                        act.activation(ob[t % OB][:, 0:512], z_ps[2 * (t % 2)][:], ACT.Copy).then_inc(s_oa, 1)

            @block.vector
            def _(dve):
                def recip(b):
                    r = rb[b % 2][:, 0:TB[b][1]]
                    dve.wait_ge(s_std, b + 1)
                    dve.reciprocal(r, r).then_inc(s_rb, 1)

                def low(u):
                    b, k = divmod(u, KC)
                    t0, n = TB[b]
                    dve.wait_ge(s_nh, u + 1)
                    lo_part(dve, nl[:, k, t0:t0 + n], sq[k % 2][:, 0:n], nh[:, k, t0:t0 + n]).then_inc(s_nl, 1)

                def norm(b):
                    t0, n = TB[b]
                    dve.wait_ge(s_rb, b + 1)
                    for k in range(KC):
                        u = b * KC + k
                        if u >= 2:
                            dve.wait_ge(s_nl, u - 1)
                        if b >= 2 and k < 2:
                            dve.wait_ge(s_al, PRE + k + 1)
                        dve.tensor_tensor(sq[k % 2][:, 0:n], ht[:, k, t0:t0 + n], rb[b % 2][:, 0:n], ALU.mult).then_inc(s_t, 1)
                        if k:
                            low(u - 1)
                        if k == RMS_AT + 1 and b + 1 < NB:
                            recip(b + 1)
                    low(b * KC + KC - 1)

                def hidden(p, u):
                    b, c = divmod(u, 2)
                    t0, n = TB[b]
                    dve.wait_ge(s_rel, p * U1 + (PRE + u + 1))
                    dve.tensor_tensor(sq[u % 2][:, 0:n], rel[u % 2][:, 0:n], rel[u % 2][:, 0:n], ALU.mult).then_inc(s_sqr, 1)
                    dve.wait_ge(s_sqr, p * U1 + (u + 1))
                    dve.wait_ge(s_ah, p * U1 + (u + 1))
                    lo_part(dve, al[:, c, t0:t0 + n], sq[u % 2][:, 0:n], ah[:, c, t0:t0 + n]).then_inc(s_al, 1)

                def out_tile(t):
                    if t >= OB:
                        dve.wait_ge(s_out[t % OB], 16 * (t // OB))
                    dve.wait_ge(s_tr, 2 * t + 2)
                    dve.tensor_copy(ob[t % OB][:, 512:1024], z_ps[2 * (t % 2) + 1][:]).then_inc(s_od, 1)

                def outputs(p, last=False):
                    dve.wait_ge(s_acc, p * U2 + PRE)
                    for b, (t0, n) in enumerate(TB):
                        for m in range(KC):
                            u = b * KC + m
                            dve.wait_ge(s_y, p * U2 + (PRE + u + 1))
                            h = ht[:, m, t0:t0 + n]
                            v = int(t0 >= LAT)
                            dve.scalar_tensor_tensor(out=h, in0=y_ps[u % 4][:, 0:n], scalar=mod[:, layer, G2, m, v:v + 1], in1=h,
                                                     op0=ALU.mult, op1=ALU.add).then_inc(s_acc, 1)
                            if last and b and m % 2:
                                out_tile(4 * (b - 1) + m // 2)
                recip(0)
                norm(0)
                norm(1)
                for b in range(NB):
                    dve.wait_ge(s_nl, min(b + 2, NB) * KC)
                    hidden(0, 2 * b)
                    hidden(0, 2 * b + 1)
                    if b == 0 and NB > 2:
                        norm(2)
                outputs(0)
                with dve.Fori(1, LOOPED) as p:
                    for u in range(U1):
                        hidden(p, u)
                    outputs(p)
                if out is not None:
                    for u in range(U1):
                        hidden(LOOPED, u)
                    dve.wait_ge(s_w1l, PRE + PAIRS)
                    dve.wait_ge(s_w2l, PRE + PAIRS)
                    outputs(LOOPED, True)
                    for t in range(4, QB):
                        out_tile(t)

            @block.tensor
            def _(pe):
                for b, (t0, n) in enumerate(TB):
                    for k in range(KC):
                        if b == 0:
                            pe.wait_ge(s_sq, k + 1)
                            square = rel[k % 2]
                        else:
                            v = (b - 1) * KC + k
                            pe.wait_ge(s_psq, v + 1)
                            square = psq[v % SQ]
                        pe.matmul(ms_ps[b][:, 0:n], meanw[:], square[:, 0:n], start=(k == 0), stop=(k == KC - 1)).then_inc(s_ms, 1)

                def hidden(p, u, first):
                    b, c = divmod(u, 2)
                    t0, n = TB[b]
                    pe.wait_ge(s_rel, p * U1 + (PRE + u - NZ + 1))
                    for k in range(KC):
                        if first and c == 0:
                            pe.wait_ge(s_nl, b * KC + k + 1)
                        cols = slice(c * P, (c + 1) * P)
                        last = mm3(pe, z_ps[u % NZ][:, 0:n], (w1h[:, k, cols], w1l[:, k, cols]),
                                   (nh[:, k, t0:t0 + n], nl[:, k, t0:t0 + n]), k == 0, k == KC - 1)
                    last.then_inc(s_z, 1)

                def out_tile(t):
                    if t < 2:
                        pe.wait_ge(s_rel, LOOPED * U1 + (PRE + U1))
                    else:
                        pe.wait_ge(s_oa, t - 1)
                        pe.wait_ge(s_od, t - 1)
                    for half in range(2):
                        for k in range(4):
                            last = pe.transpose(z_ps[2 * (t % 2) + half][:, k * P:(k + 1) * P],
                                                ht[:, 4 * half + k, t * P:(t + 1) * P], ident[:])
                        last.then_inc(s_tr, 1)

                def pair(p, first, final=False):
                    pe.wait_ge(s_w1l, p + (PRE + 1))
                    for u in range(U1):
                        hidden(p, u, first)
                    pe.wait_ge(s_w2l, p + (PRE + 1))
                    if first:
                        pe.wait_ge(s_std, NB)
                    for b, (t0, n) in enumerate(TB):
                        pe.wait_ge(s_al, p * U1 + (PRE + 2 * b + 2))
                        for m in range(KC):
                            u = b * KC + m
                            pe.wait_ge(s_acc, p * U2 + (PRE + u - 3))
                            for c in range(2):
                                last = mm3(pe, y_ps[u % 4][:, 0:n], (w2h[:, c, m * P:(m + 1) * P], w2l[:, c, m * P:(m + 1) * P]),
                                           (ah[:, c, t0:t0 + n], al[:, c, t0:t0 + n]), c == 0, c == 1)
                            last.then_inc(s_y, 1)
                            if final and b and m % 2:
                                if m == 1:
                                    pe.wait_ge(s_acc, p * U2 + (PRE + b * KC))
                                out_tile(4 * (b - 1) + m // 2)
                pair(0, True)
                with pe.Fori(1, LOOPED) as p:
                    pair(p, False)
                if out is not None:
                    pair(LOOPED, False, True)
                    pe.wait_ge(s_acc, PAIRS * U2 + PRE)
                    for t in range(4, QB):
                        out_tile(t)


def norm_out(nc, sem, sb, banks, layer, park, mod, meanw, eps, nh, nl, ht):
    with ExitStack() as ph:
        SLOTS = 4
        RMS_AT = 3
        sq = [sb(f"nsq{i}", [P, 512], where=ph) for i in range(2)]
        psq = [sb(f"npsq{i}", [P, 512], where=ph) for i in range(SLOTS)]
        tn = [sb(f"ntn{i}", [P, 512], where=ph) for i in range(3)]
        rb = [sb(f"nrb{i}", [P, 512], where=ph) for i in range(3)]
        ms_ps = banks("nms_ps", 3, ph)
        s_park, s_sq, s_psq, s_ms, s_std, s_rb, s_t, s_n, s_nh, s_nl = (sem("q_" + n) for n in (
            "park", "sq", "psq", "ms", "std", "rb", "t", "n", "nh", "nl"))
        UN = [(b, t0, n, k) for b, (t0, n) in enumerate(BLOCKS) for k in range(KC)]
        with nc.Block() as block:
            @block.sync
            def _(sp):
                sp.dma_start(park, ht[:, :, 0:LAT]).then_inc(s_park, 16)
                sp.wait_ge(s_park, 16)

            @block.gpsimd
            def _(pool):
                for v, (b, t0, n, k) in enumerate(UN[KC:]):
                    if v >= SLOTS:
                        pool.wait_ge(s_ms, KC + v - SLOTS + 1)
                    pool.tensor_tensor(psq[v % SLOTS][:, 0:n], ht[:, k, t0:t0 + n], ht[:, k, t0:t0 + n], ALU.mult).then_inc(s_psq, 1)

            @block.scalar
            def _(act):
                def rms(b):
                    n = BLOCKS[b][1]
                    act.wait_ge(s_ms, (b + 1) * KC)
                    act.activation(rb[b][:, 0:n], ms_ps[b][:, 0:n], ACT.Sqrt, bias=eps[:]).then_inc(s_std, 1)
                t0, n = BLOCKS[0]
                for k in range(KC):
                    if k >= 2:
                        act.wait_ge(s_ms, k - 1)
                    act.activation(sq[k % 2][:, 0:n], ht[:, k, t0:t0 + n], ACT.Square).then_inc(s_sq, 1)
                rms(0)
                for u, (b, t0, n, k) in enumerate(UN):
                    v = int(t0 >= LAT)
                    t = tn[u % 3][:, 0:n]
                    act.wait_ge(s_t, u + 1)
                    act.activation(t, t, ACT.Identity, scale=mod[:, layer, SC1, k, v:v + 1],
                                   bias=mod[:, layer, SH1, k, v:v + 1]).then_inc(s_n, 1)
                    act.wait_ge(s_n, u + 1)
                    act.activation(nh[:, k, t0:t0 + n], t, ACT.Copy).then_inc(s_nh, 1)
                    if k == RMS_AT and b + 1 < len(BLOCKS):
                        rms(b + 1)

            @block.vector
            def _(dve):
                def recip(b):
                    n = BLOCKS[b][1]
                    dve.wait_ge(s_std, b + 1)
                    dve.reciprocal(rb[b][:, 0:n], rb[b][:, 0:n]).then_inc(s_rb, 1)

                def low(u):
                    _, t0, n, k = UN[u]
                    dve.wait_ge(s_nh, u + 1)
                    lo_part(dve, nl[:, k, t0:t0 + n], tn[u % 3][:, 0:n], nh[:, k, t0:t0 + n]).then_inc(s_nl, 1)
                recip(0)
                for u, (b, t0, n, k) in enumerate(UN):
                    if k == 0:
                        dve.wait_ge(s_rb, b + 1)
                    if u >= 3:
                        dve.wait_ge(s_nl, u - 2)
                    dve.tensor_tensor(tn[u % 3][:, 0:n], ht[:, k, t0:t0 + n], rb[b][:, 0:n], ALU.mult).then_inc(s_t, 1)
                    if u >= 2:
                        low(u - 2)
                    if k == RMS_AT + 1 and b + 1 < len(BLOCKS):
                        recip(b + 1)
                low(len(UN) - 2)
                low(len(UN) - 1)

            @block.tensor
            def _(pe):
                for u, (b, t0, n, k) in enumerate(UN):
                    if b == 0:
                        pe.wait_ge(s_sq, u + 1)
                        square = sq[k % 2]
                    else:
                        v = u - KC
                        pe.wait_ge(s_psq, v + 1)
                        square = psq[v % SLOTS]
                    pe.matmul(ms_ps[b][:, 0:n], meanw[:], square[:, 0:n], start=(k == 0), stop=(k == KC - 1)).then_inc(s_ms, 1)


def qkv(nc, sem, sb, banks, wqkv, qkg, rope, sink, ident, eps, nh, nl, qd, kh, kl, vs, nsink):
    KV0 = D
    COLS = [(KV0, 2 * KVH * HD), (0, 512), (512, 512)]
    UNITS = [(0, t) for t in range(NT)] + [(c, t) for c in (1, 2) for t in range(QB)]
    HB = 8
    first = {c: min(u for u, (cc, _) in enumerate(UNITS) if cc == c) for c in range(3)}
    with ExitStack() as ph:
        wf = sb("qwf", [P, KC, 512], where=ph)
        ropev = sb("rope_sb", [P, 2, NT, HD], where=ph)
        wh = sb("qwh", [P, KC, 512], F32R, where=ph)
        wl = sb("qwl", [P, KC, 512], F32R, where=ph)
        g = sb("qkg_sb", [P, 2, HD], where=ph)
        ct = sb("ct", [P, 2, NT, HD], where=ph)
        st = sb("st", [P, 2, NT, HD], where=ph)
        raw = [sb(f"raw{i}", [P, 512], where=ph) for i in range(2)]
        tmp = [sb(f"qtmp{i}", [P, 512], where=ph) for i in range(2)]
        qo = [sb(f"qo{i}", [P, 512], where=ph) for i in range(2)]
        kr = sb("kr", [P, NT, KVH, 2, HD], where=ph)
        ss = sb("ss", [P, 2, HB], where=ph)
        p_ps, tr_ps = banks("qkv_ps", 3, ph), banks("ktr_ps", 2, ph)
        s_rope, s_g, s_tabs, s_used, s_wh, s_wl = (sem("k_" + n) for n in ("rope", "g", "tabs", "wused", "wh", "wl"))
        s_w = [sem(f"k_w{i}") for i in range(2)]
        s_p, s_raw, s_sq, s_ss, s_std, s_dv, s_done, s_vh, s_vl = (sem("k_" + n) for n in (
            "prod", "raw", "sq", "ss", "std", "dv", "done", "vh", "vl"))
        s_tr, s_kh, s_kl, s_pad, s_sink = (sem("k_" + n) for n in ("tr", "kh", "kl", "pad", "sink"))
        s_q = [sem(f"k_q{i}") for i in range(2)]
        def keys_after(u):
            x, per = u - NT, KVH * NT / (2 * QB)
            return [(i, i // KVH, i % KVH) for i in range(int(x * per), int((x + 1) * per))] if u >= NT else []

        def halves(ap):
            return ap.rearrange("p h (a s c) -> p h a s c", a=2, s=2)

        with nc.Block() as block:
            @block.sync
            def _(sp):
                for c, (c0, w) in enumerate(COLS):
                    for hf in range(2):
                        if c:
                            sp.wait_ge(s_wl, KC * (c - 1) + 4 * hf + 4)
                        src = wqkv[512 * hf:512 * hf + 512, c0:c0 + w].rearrange("(k p) n -> p k n", p=P)
                        sp.dma_start(wf[:, 4 * hf:4 * hf + 4, 0:w], src).then_inc(s_w[hf], 16)
                    if c == 0:
                        sp.dma_start(ropev[:], rope).then_inc(s_rope, 16)
                        sp.dma_start(g[:].rearrange("p a d -> p (a d)"), qkg).then_inc(s_g, 16)
                sp.dma_start(nsink[:], sink).then_inc(s_sink, 16)
                sp.wait_ge(s_sink, 16)
                for u in range(NT, len(UNITS)):
                    c, t = UNITS[u]
                    sp.wait_ge(s_done, u + 1)
                    sp.dma_start(qd[t, 2 * (c - 1):2 * c].rearrange("a p n -> p a n"),
                                   qo[u % 2][:].rearrange("p (a n) -> p a n", a=2)).then_inc(s_q[u % 2], 16)
                for i in range(2):
                    sp.wait_ge(s_q[i], 16 * QB)

            @block.gpsimd
            def _(pool):
                for b in (0, QB + 1):
                    pool.memset(f32(kh[:, :, b * P:(b + 1) * P]), 0.0).then_inc(s_pad, 1)
                    pool.memset(f32(kl[:, :, b * P:(b + 1) * P]), 0.0).then_inc(s_pad, 1)
                    pool.memset(f32(vs[:, b]), 0.0).then_inc(s_pad, 1)

            @block.scalar
            def _(act):
                def weights(c):
                    w = COLS[c][1]
                    for k in range(KC):
                        act.wait_ge(s_w[k // 4], 16 * (c + 1))
                        if c:
                            if k < KC - 1:
                                act.wait_ge(s_used, (KC - 1) * (c - 1) + k + 1)
                            else:
                                act.wait_ge(s_p, first[c])
                        act.activation(wh[:, k, 0:w], wf[:, k, 0:w], ACT.Copy).then_inc(s_wh, 1)
                weights(0)
                for u, (c, t) in enumerate(UNITS):
                    w = COLS[c][1]
                    nq = KVH * HD if c == 0 else 512
                    H = nq // HD
                    act.wait_ge(s_p, u + 1)
                    if u >= 2:
                        act.wait_ge(s_done, u - 1)
                    act.activation(raw[u % 2][:, 0:w], p_ps[u % 3][:, 0:w], ACT.Copy).then_inc(s_raw, 1)
                    act.activation(tmp[u % 2][:, 0:nq], p_ps[u % 3][:, 0:nq], ACT.Square).then_inc(s_sq, 1)
                    if c == 0:
                        tb = t + 1 if t < QB else t + 2
                        v = raw[u % 2][:, 128:256].rearrange("p (a d) -> p a d", a=KVH)
                        act.wait_ge(s_raw, u + 1)
                        act.activation(vs[:, tb, :, 0:HD], v, ACT.Copy).then_inc(s_vh, 1)
                    act.wait_ge(s_ss, u + 1)
                    act.activation(ss[:, u % 2, 0:H], ss[:, u % 2, 0:H], ACT.Sqrt, bias=eps[:], scale=1.0 / HD).then_inc(s_std, 1)
                    for i, kt, gg in keys_after(u):
                        tb = kt + 1 if kt < QB else kt + 2
                        act.wait_ge(s_tr, i + 1)
                        act.activation(kh[:, gg, tb * P:(tb + 1) * P], tr_ps[i % 2][:, 0:P], ACT.Copy).then_inc(s_kh, 1)
                    if c < 2 and u + 2 == first[c + 1]:
                        weights(c + 1)

            @block.vector
            def _(dve):
                chain = [0]

                def link(ins):
                    chain[0] += 1
                    ins.then_inc(s_dv, 1)
                    dve.wait_ge(s_dv, chain[0])

                def weights(c):
                    w = COLS[c][1]
                    for k in range(KC):
                        dve.wait_ge(s_wh, KC * c + k + 1)
                        lo_part(dve, wl[:, k, 0:w], wf[:, k, 0:w], wh[:, k, 0:w]).then_inc(s_wl, 1)
                weights(0)
                dve.wait_ge(s_rope, 16)
                dve.wait_ge(s_g, 16)
                link(dve.tensor_scalar_mul(g[:, 0], g[:, 0], -HD ** -0.5))
                for a in range(2):
                    gb = g[:, a:a + 1, :].to_broadcast([P, NT, HD])
                    dve.tensor_tensor(ct[:, a], ropev[:, 0], gb, ALU.mult).then_inc(s_tabs, 1)
                    for ax in range(2):
                        for s in range(2):
                            lanes = slice(32 * ax + 16 * s, 32 * ax + 16 * s + 16)
                            partner = slice(32 * ax + 16 * (1 - s), 32 * ax + 16 * (1 - s) + 16)
                            dve.tensor_tensor(st[:, a, :, lanes], ropev[:, 1, :, lanes], g[:, a:a + 1, partner].to_broadcast([P, NT, 16]),
                                              ALU.mult).then_inc(s_tabs, 1)
                dve.wait_ge(s_tabs, 10)
                for u, (c, t) in enumerate(UNITS):
                    nq = KVH * HD if c == 0 else 512
                    H = nq // HD
                    q = raw[u % 2][:, 0:nq].rearrange("p (h d) -> p h d", d=HD)
                    m = tmp[u % 2][:, 0:nq].rearrange("p (h d) -> p h d", d=HD)
                    a = 1 if c == 0 else 0
                    dve.wait_ge(s_sq, u + 1)
                    dve.reduce_sum(ss[:, u % 2, 0:H], m, axis=AX.X).then_inc(s_ss, 1)
                    if c == 0:
                        tb = t + 1 if t < QB else t + 2
                        dve.wait_ge(s_vh, u + 1)
                        lo_part(dve, vs[:, tb, :, HD:2 * HD], raw[u % 2][:, 128:256].rearrange("p (a d) -> p a d", a=KVH),
                                vs[:, tb, :, 0:HD]).then_inc(s_vl, 1)
                    dve.wait_ge(s_std, u + 1)
                    link(dve.reciprocal(ss[:, u % 2, 0:H], ss[:, u % 2, 0:H]))
                    dve.wait_ge(s_raw, u + 1)
                    link(dve.tensor_tensor(q, q, ss[:, u % 2, 0:H].rearrange("p (h o) -> p h o", o=1).to_broadcast([P, H, HD]), ALU.mult))
                    for s in range(2):
                        r = st[:, a, t:t + 1, :].to_broadcast([P, H, HD])
                        ins = dve.tensor_tensor(halves(m)[:, :, :, s, :], halves(q)[:, :, :, 1 - s, :], halves(r)[:, :, :, s, :], ALU.mult)
                    link(ins)
                    dst = kr[:, t, :, 0, :] if c == 0 else qo[u % 2][:].rearrange("p (h d) -> p h d", d=HD)
                    if c and u - NT >= 2:
                        dve.wait_ge(s_q[u % 2], 16 * ((u - NT) // 2))
                    link(dve.tensor_tensor(dst, q, ct[:, a, t:t + 1, :].to_broadcast([P, H, HD]), ALU.mult))
                    if c == 0:
                        dve.tensor_tensor(kr[:, t, :, 1, :], dst, m, ALU.add)
                    dve.tensor_tensor(dst, dst, m, ALU.add).then_inc(s_done, 1)
                    for i, kt, gg in keys_after(u):
                        tb = kt + 1 if kt < QB else kt + 2
                        dve.wait_ge(s_kh, i + 1)
                        lo_part(dve, kl[:, gg, tb * P:(tb + 1) * P], tr_ps[i % 2][:, 0:P], kh[:, gg, tb * P:(tb + 1) * P]).then_inc(s_kl, 1)
                    if c < 2 and u + 2 == first[c + 1]:
                        weights(c + 1)

            @block.tensor
            def _(pe):
                for u, (c, t) in enumerate(UNITS):
                    if u >= 3:
                        pe.wait_ge(s_sq, u - 2)
                    w = COLS[c][1]
                    leaving = c < 2 and u + 1 == first[c + 1]
                    for k in range(KC):
                        cols = slice(t * P, (t + 1) * P)
                        if u == first[c]:
                            pe.wait_ge(s_wl, KC * c + k + 1)
                        last = mm3(pe, p_ps[u % 3][:, 0:w], (nh[:, k, cols], nl[:, k, cols]), (wh[:, k, 0:w], wl[:, k, 0:w]),
                                   k == 0, k == KC - 1)
                        if k == KC - 1:
                            last.then_inc(s_p, 1)
                        elif leaving:
                            last.then_inc(s_used, 1)
                    for i, kt, gg in keys_after(u):
                        pe.wait_ge(s_done, kt + 1)
                        if i >= 2:
                            pe.wait_ge(s_kl, i - 1)
                        pe.transpose(tr_ps[i % 2][:, 0:P], kr[:, kt, gg].rearrange("p a d -> p (a d)"), ident[:]).then_inc(s_tr, 1)


def attention(nc, sem, sb, banks, masks, nsink, ident, qd, kh, kl, vs, nh, nl):
    PAIRS = QB // 2
    NQ = 8
    KB = KEYS // P
    W = 3 * P
    O_AT = (3, 4)
    SETS = 4
    with ExitStack() as ph:
        mstore = sb("mstore", [P, QB, 2, P], where=ph)
        mask = sb("mask", [P, KEYS], where=ph)
        zero4 = sb("zero4", [P, 4], where=ph)
        qb = sb("qb", [P, 4, 4, 2, HD], where=ph)
        qs = [sb(f"qs{i}", [P, 512], F32R, where=ph) for i in range(2)]
        vw = [sb(f"vw{i}", [P, 3, KVH, 2 * HD], F32R, where=ph) for i in range(2)]
        sc = sb("sc", [P, SETS, 4, KEYS + 1], where=ph)
        mn, den = sb("mn", [P, SETS, 4], where=ph), sb("den", [P, SETS, 4], where=ph)
        pth = [sb(f"pth{i}", [P, 512], F32R, where=ph) for i in range(2)]
        ptl = [sb(f"ptl{i}", [P, 512], F32R, where=ph) for i in range(2)]
        ot, of = sb("ot", [P, 2, 2, P], where=ph), sb("of", [P, 2, P], where=ph)
        s_ps = [ph.enter_context(nc.psum_tensor(f"s_ps{i}", [P, 1024], F32)) for i in range(2)]
        t_ps, o_ps = banks("t_ps", 2, ph), banks("pv_ps", 2, ph)
        q_ps = t_ps[1]

        def bank(kb):
            return t_ps[kb % 2 if kb < 3 else kb - 3]

        s_ms = [sem(f"t_mstore{i}") for i in range(2)]
        s_ns, s_z, s_m0, s_mask, s_vw, s_held = (sem("t_" + n) for n in (
            "nsink", "zero", "mask0", "mask", "vw", "held"))
        s_qb = [sem(f"t_qb{i}") for i in range(4)]
        s_qtr, s_qh, s_qs, s_sc, s_s, s_col, s_e, s_rd, s_p = (sem("t_" + n) for n in (
            "qtr", "qh", "qs", "scores", "masked", "sinkcol", "exp", "rden", "prob"))
        s_pt, s_ph, s_pl, s_o, s_ot, s_of, s_oh, s_ol = (sem("t_" + n) for n in ("ptr", "pth", "ptl", "pv", "ot", "of", "oh", "ol"))

        def at(jj, n, c, k):
            return jj * (NQ * c) + (PRE + c * n + k)

        def schedule(eng, whole_a, part_q, step):
            for n in range(2):
                part_q(0, n)
                whole_a(0, n)
            part_q(0, 2)
            step(0, 0, True, True, start=True)
            with eng.Fori(0, PAIRS - 1) as jj:
                for n in range(1, NQ + 1):
                    step(jj, n, True, True)
            for n in range(1, NQ):
                step(PAIRS - 1, n, n + 2 < NQ, n + 3 < NQ)

        with nc.Block() as block:
            @block.sync
            def _(sp):
                with sp.Fori(0, QB) as j:
                    for i in range(4):
                        sp.wait_ge(s_qtr, j * 4 + (PRE + i - 3))
                        for twice in range(2):
                            sp.dma_start(qb[:, i, :, twice, :], qd[bass.ds(j, 1), i].rearrange("a p (h d) -> p (a h) d", d=HD)).then_inc(s_qb[i], 16)

            @block.gpsimd
            def _(pool):
                pool.memset(zero4[:], 0.0).then_inc(s_z, 1)
                for s in (s_qtr, s_qh, s_qs, s_sc, s_s, s_col, s_e, s_rd, s_p, s_pt, s_ph, s_pl, s_o, s_ot, s_of, s_oh, s_ol):
                    pool.sem_inc(s, PRE)
                pool.wait_ge(s_z, 1)
                pool.wait_ge(s_ns, 1)

                def column(jj, n):
                    i, h0 = n % SETS, 4 * (n % 4)
                    pool.wait_ge(s_pt, at(jj, n, KB, -(SETS - 1) * KB))
                    pool.tensor_tensor(sc[:, i, :, KEYS], nsink[:, h0:h0 + 4], zero4[:], ALU.add).then_inc(s_col, 1)

                def part_o(jj, n):
                    pool.wait_ge(s_ot, at(jj, n, 1, 1))
                    pool.wait_ge(s_ol, at(jj, n, 1, 0))
                    pool.tensor_tensor(of[:], ot[:, 0], ot[:, 1], ALU.add).then_inc(s_of, 1)

                def normalise(jj, n):
                    i = n % SETS
                    pool.wait_ge(s_rd, at(jj, n, 1, 1))
                    for h in range(4):
                        pool.tensor_tensor(sc[:, i, h, 0:KEYS], sc[:, i, h, 0:KEYS], den[:, i, h:h + 1].to_broadcast([P, KEYS]),
                                           ALU.mult).then_inc(s_p, 1)

                def part_a(jj, n):
                    column(jj, n + 1)
                    normalise(jj, n)

                def step(jj, n, with_a, with_q, start=False):
                    if with_q:
                        column(jj, n + 3)
                    part_o(jj, n)
                    if with_a:
                        normalise(jj, n + 2)
                column(0, 0)
                schedule(pool, part_a, lambda jj, n: None, step)

            @block.scalar
            def _(act):
                act.dma_start(mstore[:, 0:1], masks[:, 0:1]).then_inc(s_ms[0], 16)

                def part_q(jj, n):
                    act.wait_ge(s_qtr, at(jj, n, 1, 1))
                    act.wait_ge(s_sc, at(jj, n, 4, -4))
                    act.activation(qs[n % 2][:], q_ps[:], ACT.Copy).then_inc(s_qh, 1)

                def head(jj, n, h):
                    i = n % SETS
                    if h == 0:
                        act.wait_ge(s_col, at(jj, n, 1, 1))
                    act.wait_ge(s_s, at(jj, n, 4, h + 1))
                    act.activation(sc[:, i, h, :], sc[:, i, h, :], ACT.Exp, scale=-1.0, bias=mn[:, i, h:h + 1],
                                   accum_out=den[:, i, h:h + 1]).then_inc(s_e, 1)

                def part_o(jj, n):
                    act.wait_ge(s_o, at(jj, n, KB, KB))
                    act.wait_ge(s_of, at(jj, n, 1, 0))
                    for half in range(2):
                        v = o_ps[n % 2][HD * half:HD * half + HD, :].rearrange("p (c s q) -> p c s q", c=2, s=2)
                        for s in range(2):
                            last = act.activation(ot[HD * s:HD * s + HD, half], v[:, :, s, :], ACT.Copy)
                    last.then_inc(s_ot, 1)

                def step(jj, n, with_a, with_q, start=False):
                    if start:
                        act.dma_start(mstore[:, 1:QB], masks[:, 1:QB]).then_inc(s_ms[1], 16)
                    for kb in range(KB):
                        slot = (n + kb) % 2
                        act.wait_ge(s_pt, at(jj, n, KB, kb + 1))
                        act.wait_ge(s_o, at(jj, n, KB, kb - 1))
                        act.activation(pth[slot][:], bank(kb)[:], ACT.Copy).then_inc(s_ph, 1)
                        if kb and with_a:
                            head(jj, n + 2, kb - 1)
                        if kb == 0 and not start:
                            part_o(jj, n - 1)
                        if kb == 2 and with_q:
                            part_q(jj, n + 3)
                schedule(act, lambda jj, n: [head(jj, n, h) for h in range(4)], part_q, step)
                part_o(PAIRS - 1, NQ - 1)

            @block.vector
            def _(dve):
                dve.tensor_scalar_mul(nsink[:], nsink[:], -1.0).then_inc(s_ns, 1)
                dve.memset(mask[:], 0.0).then_inc(s_m0, 1)
                dve.wait_ge(s_m0, 1)
                dve.wait_ge(s_ns, 1)
                dve.wait_ge(s_ms[0], 16)

                def part_q(jj, n):
                    low = qs[n % 2][HD:P, :]
                    dve.wait_ge(s_qh, at(jj, n, 1, 1))
                    dve.tensor_tensor(low, q_ps[HD:P, :], f32(low), ALU.subtract).then_inc(s_qs, 1)

                def head(jj, n, h):
                    i, h0, dj = n % SETS, 4 * (n % 4), n // 4
                    if n % 4 == 0 and h == 0:
                        dve.wait_ge(s_s, at(jj, n, 4, 0))
                        dve.wait_ge(s_o, at(jj, n, KB, -4 * KB))
                        dve.tensor_scalar_mul(vw[dj % 2][:], f32(vs[:, bass.ds(jj * 2 + dj, 3)]), 1.0).then_inc(s_vw, 1)
                        for side in range(2):
                            dve.tensor_scalar_mul(mask[:, 2 * side * P:(2 * side + 1) * P],
                                                  mstore[:, bass.ds(jj * 2 + dj, 1), side].rearrange("p a n -> p (a n)"), 1.0).then_inc(s_mask, 1)
                        dve.wait_ge(s_mask, jj * 4 + (2 * dj + 2))
                    dve.wait_ge(s_sc, at(jj, n, 4, h + 1))
                    dve.wait_ge(s_pt, at(jj, n, KB, -(SETS - 1) * KB))
                    dve.sem_inc(s_held, 1)
                    dve.tensor_tensor_reduce(out=sc[:, i, h, 0:KEYS], in0=s_ps[h % 2][:, P:P + KEYS], in1=mask[:], scale=1.0,
                                             scalar=nsink[:, h0 + h:h0 + h + 1], op0=ALU.add, op1=ALU.min,
                                             accum_out=mn[:, i, h:h + 1]).then_inc(s_s, 1)

                def recip(jj, n):
                    i = n % SETS
                    dve.wait_ge(s_e, at(jj, n, 4, 4))
                    dve.reciprocal(den[:, i], den[:, i]).then_inc(s_rd, 1)

                def part_o(jj, n, stage):
                    c0 = 2 * (n % 4)
                    cols = bass.ds(jj * (2 * P) + (n // 4) * P, P)
                    if stage == 0:
                        dve.wait_ge(s_of, at(jj, n, 1, 1))
                        dve.tensor_scalar_mul(nh[:, c0:c0 + 2, cols], of[:], 1.0).then_inc(s_oh, 1)
                    else:
                        dve.wait_ge(s_oh, at(jj, n, 1, 1))
                        lo_part(dve, nl[:, c0:c0 + 2, cols], of[:], nh[:, c0:c0 + 2, cols]).then_inc(s_ol, 1)

                def step(jj, n, with_a, with_q, start=False):
                    for kb in range(KB):
                        slot = (n + kb) % 2
                        dve.wait_ge(s_ph, at(jj, n, KB, kb + 1))
                        lo_part(dve, ptl[slot][:], bank(kb)[:], pth[slot][:]).then_inc(s_pl, 1)
                        if kb == 0 and (with_a or n + 1 < NQ):
                            recip(jj, n + 1)
                        if kb in O_AT and not start:
                            part_o(jj, n - 1, kb - O_AT[0])
                        if kb < 4 and with_a:
                            head(jj, n + 2, kb)
                        if kb == 2 and with_q:
                            part_q(jj, n + 3)
                    if start:
                        dve.wait_ge(s_ms[1], 16)

                def whole_a(jj, n):
                    for h in range(4):
                        head(jj, n, h)
                    if n == 0:
                        recip(jj, n)
                schedule(dve, whole_a, part_q, step)
                for stage in range(2):
                    part_o(PAIRS - 1, NQ - 1, stage)

            @block.tensor
            def _(pe):
                def part_q(jj, n):
                    i = n % 4
                    pe.wait_ge(s_qb[i], jj * 64 + (n // 4 + 1) * 32)
                    pe.wait_ge(s_qs, at(jj, n, 1, 0))
                    for h in range(4):
                        last = pe.transpose(q_ps[:, h * P:(h + 1) * P], qb[:, i, h].rearrange("p a d -> p (a d)"), ident[:])
                    last.then_inc(s_qtr, 1)

                def head(jj, n, h):
                    g, dj = (n % 4) // 2, n // 4
                    if h == 0:
                        pe.wait_ge(s_qs, at(jj, n, 1, 1))
                    pe.wait_ge(s_s, at(jj, n, 4, h - 1))
                    q = qs[n % 2][:, h * P:(h + 1) * P]
                    win = bass.ds(jj * (2 * P) + dj * P, W)
                    ctxk = slice((QB + 2) * P, (QB + 4) * P)
                    pe.matmul(s_ps[h % 2][:, P:P + W], q, kh[:, g, win], start=True, stop=False)
                    pe.matmul(s_ps[h % 2][:, P:P + W], q, kl[:, g, win], start=False, stop=True)
                    pe.matmul(s_ps[h % 2][:, P + W:P + KEYS], q, kh[:, g, ctxk], start=True, stop=False)
                    pe.matmul(s_ps[h % 2][:, P + W:P + KEYS], q, kl[:, g, ctxk], start=False, stop=True).then_inc(s_sc, 1)

                def values(jj, n, kb):
                    g, slot, o = (n % 4) // 2, (n + kb) % 2, o_ps[n % 2]
                    if kb == 0:
                        pe.wait_ge(s_ot, at(jj, n, 1, -1))
                        pe.wait_ge(s_vw, jj * 2 + (n // 4 + 1))
                    pe.wait_ge(s_pl, at(jj, n, KB, kb + 1))
                    v = vw[(n // 4) % 2][:, kb, g, :] if kb < 3 else vs[:, QB + 2 + kb - 3, g, :]
                    pe.matmul(o[:], v, pth[slot][:], start=(kb == 0), stop=False)
                    pe.matmul(o[:], v, ptl[slot][:], start=False, stop=(kb == KB - 1)).then_inc(s_o, 1)

                def step(jj, n, with_a, with_q, start=False):
                    pe.wait_ge(s_p, at(jj, n, 4, 4))
                    for kb in range(KB):
                        if kb == 1 and start:
                            pe.wait_ge(s_qs, at(jj, n + 2, 1, 1))
                        if kb < 3:
                            pe.wait_ge(s_pl, at(jj, n, KB, kb - 1))
                        elif kb == 3:
                            pe.wait_ge(s_pl, at(jj, n, KB, 3))
                        elif with_q:
                            pe.wait_ge(s_qs, at(jj, n + 3, 1, 1))
                        else:
                            pe.wait_ge(s_pl, at(jj, n, KB, 2))
                        for h in range(4):
                            last = pe.transpose(bank(kb)[:, h * P:(h + 1) * P], sc[:, n % SETS, h, kb * P:(kb + 1) * P], ident[:])
                        last.then_inc(s_pt, 1)
                        if kb < 4 and with_a:
                            head(jj, n + 2, kb)
                        if kb:
                            values(jj, n, kb - 1)
                        elif not start:
                            values(jj, n - 1, KB - 1)
                        if kb == 2 and with_q:
                            pe.wait_ge(s_pl, at(jj, n, KB, 2))
                            part_q(jj, n + 3)
                schedule(pe, lambda jj, n: [head(jj, n, h) for h in range(4)], part_q, step)
                values(PAIRS - 1, NQ - 1, KB - 1)


def attn_out(nc, sem, sb, banks, wo, park, mod, nh, nl, ht):
    TB = BLOCKS[:2]
    with ExitStack() as ph:
        wf = [sb(f"of{i}", [P, KC, P], where=ph) for i in range(2)]
        wh = [sb(f"owh{i}", [P, KC, P], F32R, where=ph) for i in range(2)]
        wl = [sb(f"owl{i}", [P, KC, P], F32R, where=ph) for i in range(2)]
        o_ps = banks("oo_ps", 4, ph)
        s_wh, s_wl, s_o, s_add = (sem("w_" + n) for n in ("wh", "wl", "prod", "add"))
        s_h = [sem(f"w_ht{i}") for i in range(2)]
        s_w = [sem(f"w_w{i}") for i in range(2)]
        with nc.Block() as block:
            @block.gpsimd
            def _(pool):
                for s in (s_wl, s_o, s_add):
                    pool.sem_inc(s, PRE)

            @block.sync
            def _(sp):
                with sp.Fori(0, KC // 2) as r:
                    for i in range(2):
                        sp.wait_ge(s_wl, r * 2 + (PRE + i - 1))
                        sp.dma_start(wf[i][:], wo[bass.ds(r * 2 + i, 1)].rearrange("a p k n -> p (a k) n")).then_inc(s_w[i], 16)

            @block.scalar
            def _(act):
                def high(r, i):
                    act.wait_ge(s_w[i % 2], r * 16 + 16 * (i // 2 + 1))
                    act.wait_ge(s_o, r * 4 + (PRE + 2 * i - 2))
                    act.activation(wh[i % 2][:], wf[i % 2][:], ACT.Copy).then_inc(s_wh, 1)
                high(0, 0)
                act.dma_start(ht[:, 0:2], park[:, 0:2]).then_inc(s_h[0], 16)
                high(0, 1)
                act.dma_start(ht[:, 2:KC], park[:, 2:KC]).then_inc(s_h[1], 16)
                with act.Fori(1, KC // 2) as r:
                    for i in range(2):
                        high(r, i)

            @block.vector
            def _(dve):
                def low(r, i):
                    dve.wait_ge(s_wh, r * 2 + (i + 1))
                    lo_part(dve, wl[i % 2][:], wf[i % 2][:], wh[i % 2][:]).then_inc(s_wl, 1)

                def pair(r, more):
                    for i in range(2):
                        for b, (t0, n) in enumerate(TB):
                            h = ht[:, bass.ds(r * 2 + i, 1), t0:t0 + n].rearrange("p a s -> p (a s)")
                            dve.wait_ge(s_o, r * 4 + (PRE + 2 * i + b + 1))
                            dve.scalar_tensor_tensor(out=h, in0=o_ps[2 * i + b][:, 0:n], scalar=mod[:, 1, G1, bass.ds(r * 2 + i, 1), 0],
                                                     in1=h, op0=ALU.mult, op1=ALU.add).then_inc(s_add, 1)
                            if b == 0 and (more or i == 0):
                                low(r, i + 1)
                low(0, 0)
                dve.wait_ge(s_h[0], 16)
                pair(0, True)
                dve.wait_ge(s_h[1], 16)
                with dve.Fori(1, KC // 2 - 1) as r:
                    pair(r, True)
                pair(KC // 2 - 1, False)

            @block.tensor
            def _(pe):
                with pe.Fori(0, KC // 2) as r:
                    for i in range(2):
                        pe.wait_ge(s_wl, r * 2 + (PRE + i + 1))
                        for b, (t0, n) in enumerate(TB):
                            pe.wait_ge(s_add, r * 4 + (PRE + 2 * i + b - 3))
                            for k in range(KC):
                                last = mm3(pe, o_ps[2 * i + b][:, 0:n], (wh[i][:, k, :], wl[i][:, k, :]),
                                           (nh[:, k, t0:t0 + n], nl[:, k, t0:t0 + n]), k == 0, k == KC - 1)
                            last.then_inc(s_o, 1)


def dft_tables():
    t, s = np.arange(256)[:, None], np.arange(256)[None, :]
    out = []
    for s1 in (0, 2, 1):
        a = 2 * np.pi * (((4 * s + s1) * t) % LAT) / LAT
        out.append(np.concatenate([np.cos(a), np.sin(a)], axis=1))
    c, s_ = out[2][:, :256], out[2][:, 256:]
    out.append(np.concatenate([-s_, c], axis=1))
    return np.stack([o.reshape(2, P, 512).transpose(1, 0, 2) for o in out]).astype(np.float32)


def rope_tables():
    inv = 10000.0 ** (-np.arange(16, dtype=np.float32) / np.float32(16))
    pos = np.arange(LAT)
    ar = (pos // 64).astype(np.float32)[:, None] * inv[None, :]
    ac = (pos % 64).astype(np.float32)[:, None] * inv[None, :]
    cos = np.concatenate([np.cos(ar), np.cos(ar), np.cos(ac), np.cos(ac)], axis=1)
    sin = np.concatenate([-np.sin(ar), np.sin(ar), -np.sin(ac), np.sin(ac)], axis=1)
    cos = np.concatenate([cos, np.ones((CTX, HD))]).reshape(NT, P, HD)
    sin = np.concatenate([sin, np.zeros((CTX, HD))]).reshape(NT, P, HD)
    return np.stack([cos, sin]).transpose(2, 0, 1, 3).astype(np.float32)


def band_masks():
    q, k = np.arange(P)[:, None], np.arange(P)[None, :]
    m = np.stack([np.where(k >= q, 0, BIG), np.where(k <= q, 0, BIG)])
    m = np.repeat(m[None], QB, axis=0)
    m[0, 0] = BIG
    m[QB - 1, 1] = BIG
    return m.transpose(2, 0, 1, 3).astype(np.float32)


def kernel(**inputs):
    import concourse.bacc as bacc
    from concourse.bass_utils import run_bass_kernel_spmd

    a = {k: np.ascontiguousarray(v) for k, v in inputs.items()}

    def columns(v):
        return v.reshape(-1, P).T

    cc = np.stack([columns(a["c"]), columns(a["c_ctx"])], axis=2).reshape(P, 2 * KC)
    vecs = np.concatenate([columns(a["norm1_g"]), columns(a["norm2_g"]), columns(a["ada_b"]), columns(a["fnet_b"]), cc], axis=1)
    negated = (np.arange(D) // GW) * GW + (-np.arange(D)) % GW
    fnet_w = a["fnet_w"][0][negated].reshape(KC, P, KC, P).transpose(2, 1, 0, 3)
    pieces = a["ada_w"].reshape(DEPTH, KC, P, 6 * D // PIECE, PIECE).transpose(0, 3, 2, 1, 4)
    both = pieces[1, 0:4].reshape(4, P, 2, 4 * PIECE).transpose(0, 2, 1, 3)
    lat = pieces[1, 4:12].reshape(4, 2, P, 4, 2, PIECE).transpose(0, 3, 2, 4, 1, 5).reshape(4, 4, P, 4 * PIECE)
    units = np.concatenate([both, lat], axis=1)
    arrays = {
        "x": a["x"][0], "ctx": a["ctx"][0], "vecs": vecs,
        "ada0": pieces[0], "ada1": units,
        "w1": a["mlp_w1"].reshape(DEPTH, KC, P, DFF // (2 * P), 2 * P).transpose(0, 3, 2, 1, 4),
        "w2": a["mlp_w2"].reshape(DEPTH, DFF // P, P, D),
        "fnet_w": fnet_w, "wqkv": a["attn_w_qkv"][0],
        "wo": a["attn_w_o"][0].reshape(KC, P, KC, P).transpose(2, 1, 0, 3),
        "qkg": np.broadcast_to(np.concatenate([a["attn_q_g"][0], a["attn_k_g"][0]]), (P, 2 * HD)),
        "sink": np.broadcast_to(a["attn_sink"][0], (P, HEADS)),
        "dft": dft_tables(), "rope": rope_tables(), "masks": band_masks(), "eye": np.eye(P, dtype=np.float32),
    }
    arrays = {k: np.ascontiguousarray(v) for k, v in arrays.items()}
    nc = bacc.Bacc("TRN2", target_bir_lowering=False, num_devices=1)
    args = [nc.dram_tensor(n, v.shape, mybir.dt.from_np(v.dtype), kind="ExternalInput").ap() for n, v in arrays.items()]
    out = nc.dram_tensor("out", (LAT, D), F32, kind="ExternalOutput").ap()
    park = nc.dram_tensor("park", (P, KC, LAT), F32, kind="Internal").ap()
    qd = nc.dram_tensor("queries", (QB, HEADS // 4, P, 4 * HD), F32, kind="Internal").ap()
    hybrid_kernel(nc, *args, out, park, qd)
    r = run_bass_kernel_spmd(nc, [arrays], core_ids=[0])
    return r.results[0]["out"].reshape(1, LAT, D)
```
